# Optimizing a Trainium2 kernel written in Bass

```python
import math
import jax, jax.numpy as jnp
from jax import lax
import numpy as np

D_MODEL = 1024
BATCH = 1
SEQ = 256
DEPTH = 2

N_MIXERS = 4
ROPE_THETA = 500000.0
Q_BLOCK = 128
LN_EPS = 1e-5
RMS_EPS = 1e-6
MAX_POS_OFFSET = 4096
DIFF_HEADS = 8
DIFF_HEAD_DIM = 64
FOX_HEADS = 16
FOX_HEAD_DIM = 64
MLA_HEADS = 16
MLA_NOPE = 64
MLA_ROPE = 32
MLA_V = 64
MLA_Q_RANK = 384
MLA_KV_RANK = 256
MOBA_HEADS = 16
MOBA_HEAD_DIM = 64
MOBA_BLOCK = 256
MOBA_TOPK = 3
MOBA_Q_CHUNK = 32
PARTIAL_ROT = 64 // 4
D_FF = 2816
CONV_WIDTH = 3
DEEPNORM_ALPHA = (2 * DEPTH) ** 0.25
DEEPNORM_BETA = (8 * DEPTH) ** -0.25


def _n_uses(m):
    return len(range(m, DEPTH, N_MIXERS))

def diff_lambda_init(layer):
    return 0.8 - 0.6 * math.exp(-0.3 * layer)

def layer_norm(x, g, b):
    xf = x.astype(jnp.float32)
    mu = xf.mean(-1, keepdims=True)
    var = jnp.square(xf - mu).mean(-1, keepdims=True)
    y = (xf - mu) * lax.rsqrt(var + LN_EPS) * g.astype(jnp.float32) + b.astype(jnp.float32)
    return y.astype(x.dtype)

def rms_norm(x, g):
    xf = x.astype(jnp.float32)
    y = xf * lax.rsqrt(jnp.mean(xf * xf, -1, keepdims=True) + RMS_EPS) * g.astype(jnp.float32)
    return y.astype(x.dtype)

def rotary_angles(positions, rot_dim):
    inv_freq = ROPE_THETA ** (-jnp.arange(0, rot_dim, 2, dtype=jnp.float32) / rot_dim)
    ang = positions.astype(jnp.float32)[..., None] * inv_freq
    return jnp.cos(ang), jnp.sin(ang)

def apply_rotary(x, cos, sin, rot_dim):
    expand = (1,) * (x.ndim - 3)
    cos = cos.reshape(cos.shape[:2] + expand + cos.shape[-1:])
    sin = sin.reshape(sin.shape[:2] + expand + sin.shape[-1:])
    half = rot_dim // 2
    xr = x[..., :rot_dim].astype(jnp.float32)
    x1, x2 = xr[..., :half], xr[..., half:]
    rot = jnp.concatenate([x1 * cos - x2 * sin, x2 * cos + x1 * sin], -1).astype(x.dtype)
    return jnp.concatenate([rot, x[..., rot_dim:]], -1)

def causal_mask(q_start, q_len, k_len):
    q_idx = q_start + jnp.arange(q_len)
    k_idx = jnp.arange(k_len)
    return k_idx[None, :] <= q_idx[:, None]

def masked_softmax(scores, mask):
    s = jnp.where(mask, scores.astype(jnp.float32), -jnp.inf)
    return jax.nn.softmax(s, axis=-1)

def sweep_query_blocks(block_fn, seq, block):
    starts = jnp.arange(seq // block) * block
    out = lax.map(block_fn, starts)
    n, b, blk, f = out.shape
    return out.transpose(1, 0, 2, 3).reshape(b, n * blk, f)

def diff_attention(x, cos, sin, w_qkv, lam_q1, lam_k1, lam_q2, lam_k2, subln_g, w_o, lambda_init):
    B, S, _ = x.shape
    H, d = DIFF_HEADS, DIFF_HEAD_DIM
    q, k, v = jnp.split(x @ w_qkv, 3, axis=-1)
    q = apply_rotary(q.reshape(B, S, H, 2, d), cos, sin, PARTIAL_ROT).transpose(0, 2, 3, 1, 4)
    k = apply_rotary(k.reshape(B, S, H, 2, d), cos, sin, PARTIAL_ROT).transpose(0, 2, 3, 1, 4)
    v = v.reshape(B, S, H, 2 * d).transpose(0, 2, 1, 3)
    f32 = jnp.float32
    lam = (jnp.exp(jnp.sum(lam_q1.astype(f32) * lam_k1.astype(f32)))
           - jnp.exp(jnp.sum(lam_q2.astype(f32) * lam_k2.astype(f32))) + lambda_init)
    scale = d ** -0.5

    def block(start):
        qb = lax.dynamic_slice_in_dim(q, start, Q_BLOCK, axis=3)
        s = jnp.einsum('bhcqd,bhckd->bhcqk', qb, k) * scale
        p = masked_softmax(s, causal_mask(start, Q_BLOCK, S))
        a = (p[:, :, 0] - lam * p[:, :, 1]).astype(v.dtype)
        o = jnp.einsum('bhqk,bhkd->bqhd', a, v)
        o = rms_norm(o, subln_g) * (1.0 - lambda_init)
        return o.reshape(B, Q_BLOCK, H * 2 * d)

    return sweep_query_blocks(block, S, Q_BLOCK) @ w_o

def forgetting_attention(x, w_in, b_f, w_o):
    B, S, _ = x.shape
    H, d = FOX_HEADS, FOX_HEAD_DIM
    q, k, v, f_logit = jnp.split(x @ w_in, [H * d, 2 * H * d, 3 * H * d], axis=-1)
    q = q.reshape(B, S, H, d).transpose(0, 2, 1, 3)
    k = k.reshape(B, S, H, d).transpose(0, 2, 1, 3)
    v = v.reshape(B, S, H, d).transpose(0, 2, 1, 3)
    log_f = jax.nn.log_sigmoid((f_logit + b_f).astype(jnp.float32))
    c = jnp.cumsum(log_f, axis=1).transpose(0, 2, 1)
    scale = d ** -0.5

    def block(start):
        qb = lax.dynamic_slice_in_dim(q, start, Q_BLOCK, axis=2)
        cb = lax.dynamic_slice_in_dim(c, start, Q_BLOCK, axis=2)
        s = (jnp.einsum('bhqd,bhkd->bhqk', qb, k).astype(jnp.float32) * scale
             + cb[..., :, None] - c[..., None, :])
        p = masked_softmax(s, causal_mask(start, Q_BLOCK, S)).astype(v.dtype)
        o = jnp.einsum('bhqk,bhkd->bqhd', p, v)
        return o.reshape(B, Q_BLOCK, H * d)

    return sweep_query_blocks(block, S, Q_BLOCK) @ w_o

def latent_attention(x, cos, sin, w_down, q_norm_g, kv_norm_g, w_uq, w_ukv, w_o):
    B, S, _ = x.shape
    H = MLA_HEADS
    c_q, c_kv, k_rope = jnp.split(x @ w_down, [MLA_Q_RANK, MLA_Q_RANK + MLA_KV_RANK], axis=-1)
    c_q = rms_norm(c_q, q_norm_g)
    c_kv = rms_norm(c_kv, kv_norm_g)
    q = (c_q @ w_uq).reshape(B, S, H, MLA_NOPE + MLA_ROPE)
    q_nope = q[..., :MLA_NOPE].transpose(0, 2, 1, 3)
    q_rope = apply_rotary(q[..., MLA_NOPE:], cos, sin, MLA_ROPE).transpose(0, 2, 1, 3)
    kv = (c_kv @ w_ukv).reshape(B, S, H, MLA_NOPE + MLA_V)
    k_nope = kv[..., :MLA_NOPE].transpose(0, 2, 1, 3)
    v = kv[..., MLA_NOPE:].transpose(0, 2, 1, 3)
    k_rope = apply_rotary(k_rope, cos, sin, MLA_ROPE)
    scale = (MLA_NOPE + MLA_ROPE) ** -0.5

    def block(start):
        qn = lax.dynamic_slice_in_dim(q_nope, start, Q_BLOCK, axis=2)
        qr = lax.dynamic_slice_in_dim(q_rope, start, Q_BLOCK, axis=2)
        s = (jnp.einsum('bhqd,bhkd->bhqk', qn, k_nope)
             + jnp.einsum('bhqr,bkr->bhqk', qr, k_rope)) * scale
        p = masked_softmax(s, causal_mask(start, Q_BLOCK, S)).astype(v.dtype)
        o = jnp.einsum('bhqk,bhkd->bqhd', p, v)
        return o.reshape(B, Q_BLOCK, H * MLA_V)

    return sweep_query_blocks(block, S, Q_BLOCK) @ w_o

def moba_attention(x, cos, sin, w_qkv, w_o):
    B, S, _ = x.shape
    H, d, BS, QC = MOBA_HEADS, MOBA_HEAD_DIM, MOBA_BLOCK, MOBA_Q_CHUNK
    q, k, v = jnp.split(x @ w_qkv, 3, axis=-1)
    q = apply_rotary(q.reshape(B, S, H, d), cos, sin, PARTIAL_ROT).transpose(0, 2, 1, 3)
    k = apply_rotary(k.reshape(B, S, H, d), cos, sin, PARTIAL_ROT).transpose(0, 2, 1, 3)
    v = v.reshape(B, S, H, d).transpose(0, 2, 1, 3)
    nb = -(-S // BS)
    pad = nb * BS - S
    k_blocks = jnp.pad(k, ((0, 0), (0, 0), (0, pad), (0, 0))).reshape(B, H, nb, BS, d)
    v_blocks = jnp.pad(v, ((0, 0), (0, 0), (0, pad), (0, 0))).reshape(B, H, nb, BS, d)
    k_mean = k_blocks.astype(jnp.float32).mean(axis=3).astype(k.dtype)
    topk = min(MOBA_TOPK, max(nb - 1, 1))
    bidx = jnp.arange(B)[:, None, None, None]
    hidx = jnp.arange(H)[None, :, None, None]
    scale = d ** -0.5

    def chunk(start):
        qc = lax.dynamic_slice_in_dim(q, start, QC, axis=2)
        cur = start // BS
        gate = jnp.einsum('bhqd,bhnd->bhqn', qc, k_mean).astype(jnp.float32)
        gate = jnp.where(jnp.arange(nb) < cur, gate, -jnp.inf)
        _, idx = lax.top_k(gate, topk)
        sel_ok = idx < cur
        k_sel = k_blocks[bidx, hidx, idx]
        v_sel = v_blocks[bidx, hidx, idx]
        s_sel = jnp.einsum('bhqd,bhqnkd->bhqnk', qc, k_sel).reshape(B, H, QC, topk * BS)
        k_own = lax.dynamic_index_in_dim(k_blocks, cur, axis=2, keepdims=False)
        v_own = lax.dynamic_index_in_dim(v_blocks, cur, axis=2, keepdims=False)
        s_own = jnp.einsum('bhqd,bhkd->bhqk', qc, k_own)
        own_mask = (cur * BS + jnp.arange(BS))[None, :] <= (start + jnp.arange(QC))[:, None]
        s = jnp.concatenate([s_sel, s_own], -1) * scale
        mask = jnp.concatenate([jnp.repeat(sel_ok, BS, axis=-1),
                                jnp.broadcast_to(own_mask, (B, H, QC, BS))], -1)
        p = masked_softmax(s, mask).astype(v.dtype)
        p_sel = p[..., :topk * BS].reshape(B, H, QC, topk, BS)
        o = (jnp.einsum('bhqnk,bhqnkd->bqhd', p_sel, v_sel)
             + jnp.einsum('bhqk,bhkd->bqhd', p[..., topk * BS:], v_own))
        return o.reshape(B, QC, H * d)

    return sweep_query_blocks(chunk, S, QC) @ w_o

def conv_ffn(x, w_in, conv_w, conv_b, w_out):
    gate, up = jnp.split(x @ w_in, 2, axis=-1)
    gate = lax.conv_general_dilated(
        gate, conv_w[:, None, :], window_strides=(1,), padding=[(CONV_WIDTH - 1, 0)],
        dimension_numbers=('NWC', 'WIO', 'NWC'), feature_group_count=D_FF) + conv_b
    return (jax.nn.silu(gate) * up) @ w_out

def first_inputs(seed: int = 0) -> dict:
    key = jax.random.key(seed)
    keys = iter(jax.random.split(key, 32))
    f32 = jnp.float32

    def normal(shape, std):
        return std * jax.random.normal(next(keys), shape, f32)

    def gain(shape):
        return 1.0 + normal(shape, 0.02)

    n_diff, n_fox, n_mla, n_moba = [_n_uses(m) for m in range(N_MIXERS)]
    D = D_MODEL
    beta = DEEPNORM_BETA
    x = normal((BATCH, SEQ, D), 1.0)
    offset = jax.random.randint(next(keys), (BATCH, 1), 0, MAX_POS_OFFSET, dtype=jnp.int32)
    positions = jnp.arange(SEQ, dtype=jnp.int32)[None, :] + offset
    diff_w = DIFF_HEADS * 2 * DIFF_HEAD_DIM
    fox_w = FOX_HEADS * FOX_HEAD_DIM
    moba_w = MOBA_HEADS * MOBA_HEAD_DIM
    return {
        'x': x,
        'positions': positions,
        'diff_w_qkv': normal((n_diff, D, 3 * diff_w), D ** -0.5),
        'diff_lambda_q1': normal((n_diff, DIFF_HEAD_DIM), 0.1),
        'diff_lambda_k1': normal((n_diff, DIFF_HEAD_DIM), 0.1),
        'diff_lambda_q2': normal((n_diff, DIFF_HEAD_DIM), 0.1),
        'diff_lambda_k2': normal((n_diff, DIFF_HEAD_DIM), 0.1),
        'diff_subln_g': gain((n_diff, 2 * DIFF_HEAD_DIM)),
        'diff_w_o': normal((n_diff, diff_w, D), beta * diff_w ** -0.5),
        'fox_w_in': normal((n_fox, D, 3 * fox_w + FOX_HEADS), D ** -0.5),
        'fox_b_f': jax.random.uniform(next(keys), (n_fox, FOX_HEADS), f32, 1.0, 5.0),
        'fox_w_o': normal((n_fox, fox_w, D), beta * fox_w ** -0.5),
        'mla_w_down': normal((n_mla, D, MLA_Q_RANK + MLA_KV_RANK + MLA_ROPE), D ** -0.5),
        'mla_q_norm_g': gain((n_mla, MLA_Q_RANK)),
        'mla_kv_norm_g': gain((n_mla, MLA_KV_RANK)),
        'mla_w_uq': normal((n_mla, MLA_Q_RANK, MLA_HEADS * (MLA_NOPE + MLA_ROPE)), MLA_Q_RANK ** -0.5),
        'mla_w_ukv': normal((n_mla, MLA_KV_RANK, MLA_HEADS * (MLA_NOPE + MLA_V)), MLA_KV_RANK ** -0.5),
        'mla_w_o': normal((n_mla, MLA_HEADS * MLA_V, D), beta * (MLA_HEADS * MLA_V) ** -0.5),
        'moba_w_qkv': normal((n_moba, D, 3 * moba_w), D ** -0.5),
        'moba_w_o': normal((n_moba, moba_w, D), beta * moba_w ** -0.5),
        'ffn_w_in': normal((DEPTH, D, 2 * D_FF), D ** -0.5),
        'ffn_conv_w': normal((DEPTH, CONV_WIDTH, D_FF), CONV_WIDTH ** -0.5),
        'ffn_conv_b': normal((DEPTH, D_FF), 0.02),
        'ffn_w_out': normal((DEPTH, D_FF, D), beta * D_FF ** -0.5),
        'ln1_g': gain((DEPTH, D)),
        'ln1_b': normal((DEPTH, D), 0.02),
        'ln2_g': gain((DEPTH, D)),
        'ln2_b': normal((DEPTH, D), 0.02),
    }

def first_block(x, positions, diff_w_qkv, diff_lambda_q1, diff_lambda_k1, diff_lambda_q2, diff_lambda_k2,
              diff_subln_g, diff_w_o, fox_w_in, fox_b_f, fox_w_o, mla_w_down, mla_q_norm_g, mla_kv_norm_g,
              mla_w_uq, mla_w_ukv, mla_w_o, moba_w_qkv, moba_w_o, ffn_w_in, ffn_conv_w, ffn_conv_b,
              ffn_w_out, ln1_g, ln1_b, ln2_g, ln2_b):
    cos_p, sin_p = rotary_angles(positions, PARTIAL_ROT)
    cos_m, sin_m = rotary_angles(positions, MLA_ROPE)
    h = x
    for i in range(DEPTH):
        m, u = i % N_MIXERS, i // N_MIXERS
        if m == 0:
            y = diff_attention(h, cos_p, sin_p, diff_w_qkv[u], diff_lambda_q1[u], diff_lambda_k1[u],
                               diff_lambda_q2[u], diff_lambda_k2[u], diff_subln_g[u], diff_w_o[u],
                               diff_lambda_init(i))
        elif m == 1:
            y = forgetting_attention(h, fox_w_in[u], fox_b_f[u], fox_w_o[u])
        elif m == 2:
            y = latent_attention(h, cos_m, sin_m, mla_w_down[u], mla_q_norm_g[u], mla_kv_norm_g[u],
                                 mla_w_uq[u], mla_w_ukv[u], mla_w_o[u])
        else:
            y = moba_attention(h, cos_p, sin_p, moba_w_qkv[u], moba_w_o[u])
        h = layer_norm(DEEPNORM_ALPHA * h + y, ln1_g[i], ln1_b[i])
        f = conv_ffn(h, ffn_w_in[i], ffn_conv_w[i], ffn_conv_b[i], ffn_w_out[i])
        h = layer_norm(DEEPNORM_ALPHA * h + f, ln2_g[i], ln2_b[i])
    return h


DEPTH_2 = 1

N_MEM = 256
GRID_W = 64
HY_W = 512
NA_HEADS = 8
NA_HEAD_DIM = 64
NA_W = NA_HEADS * NA_HEAD_DIM
NA_WIN_ROWS = 8
NA_WIN_COLS = 16
SC_W = 512
XA_HEADS = 4
XA_HEAD_DIM = D_MODEL // XA_HEADS
HY_ORDER = 2
HY_EMB = 33
HY_HIDDEN = 64
HY_FAST_DECAY = 0.3
HY_SLOW_DECAY = 1.5
HY_TARGET = 1e-2
N_BRANCH = 3
EPS = 1e-6
PROJ_W = 3 * HY_W + 3 * NA_W + 3 * SC_W + N_BRANCH * D_MODEL


def rms_norm_2(x, g):
    xf = x.astype(jnp.float32)
    y = xf * lax.rsqrt(jnp.mean(xf * xf, axis=-1, keepdims=True) + EPS)
    return (y * g.astype(jnp.float32)).astype(x.dtype)

def dwconv3(x, w):
    xp = jnp.pad(x, ((0, 0), (1, 1), (0, 0)))
    return xp[:, :-2] * w[0] + xp[:, 1:-1] * w[1] + xp[:, 2:] * w[2]

def hyena_filters(L, w1, b1, w2, b2, w3, freq):
    f32 = jnp.float32
    t = jnp.linspace(0.0, 1.0, L, dtype=f32)[:, None]
    bands = (HY_EMB - 1) // 2
    w = 2.0 * math.pi * jnp.arange(L, dtype=f32)[:, None] / L
    f = jnp.linspace(1e-4, bands - 1, bands, dtype=f32)[None, :]
    z = jnp.concatenate([t, jnp.cos(f * w), -jnp.sin(f * w)], axis=-1)
    h = jnp.sin(freq[0].astype(f32) * (z @ w1.astype(f32) + b1.astype(f32)))
    h = jnp.sin(freq[1].astype(f32) * (h @ w2.astype(f32) + b2.astype(f32)))
    h = (h @ w3.astype(f32)).reshape(L, 2, HY_ORDER, HY_W)
    deltas = jnp.abs(jnp.linspace(math.log(HY_TARGET) / HY_SLOW_DECAY,
                                  math.log(HY_TARGET) / HY_FAST_DECAY, HY_W, dtype=f32))
    h = h * jnp.exp(-t * deltas)[:, None, None, :]
    h_fwd, h_bwd = h[:, 0], h[:, 1]
    k2 = jnp.concatenate([h_fwd, jnp.zeros((1, HY_ORDER, HY_W), f32), h_bwd[1:][::-1]], axis=0)
    return jnp.fft.rfft(k2, axis=0)

def long_conv(z, kf, bias):
    L = z.shape[1]
    zf32 = z.astype(jnp.float32)
    zf = jnp.fft.rfft(zf32, n=2 * L, axis=1)
    y = jnp.fft.irfft(zf * kf[None], n=2 * L, axis=1)[:, :L]
    return (y + zf32 * bias.astype(jnp.float32)).astype(z.dtype)

def hyena_mixer(u, short_w, kf, bias):
    u = dwconv3(u, short_w)
    v, x1, x2 = jnp.split(u, 3, axis=-1)
    z = x1 * long_conv(v, kf[:, 0], bias[0])
    return x2 * long_conv(z, kf[:, 1], bias[1])

def neighbourhood_attention(q, k, v, rpb):
    B, L, _ = q.shape
    rows = L // GRID_W
    kr = min(NA_WIN_ROWS, rows)

    def grid(t):
        return t.reshape(B, rows, GRID_W, NA_HEADS, NA_HEAD_DIM).transpose(0, 3, 1, 2, 4)

    qg = grid(q) * (NA_HEAD_DIM ** -0.5)
    kg, vg = grid(k), grid(v)
    r = jnp.arange(rows)
    row_idx = jnp.clip(r - kr // 2, 0, rows - kr)[:, None] + jnp.arange(kr)[None, :]
    k_rows = kg[:, :, row_idx]
    v_rows = vg[:, :, row_idx]
    c = jnp.arange(GRID_W)
    col_start = jnp.clip(c - NA_WIN_COLS // 2, 0, GRID_W - NA_WIN_COLS)
    col_mask = (c[None, :] >= col_start[:, None]) & (c[None, :] < col_start[:, None] + NA_WIN_COLS)
    dr = row_idx - r[:, None] + (NA_WIN_ROWS - 1)
    dc = jnp.clip(c[None, :] - c[:, None] + NA_WIN_COLS - 1, 0, 2 * NA_WIN_COLS - 2)
    bias = rpb[:, dr][..., dc].transpose(0, 1, 3, 2, 4)
    s = jnp.einsum('bhrqd,bhrkcd->bhrqkc', qg, k_rows).astype(jnp.float32)
    s = s + bias[None].astype(jnp.float32)
    s = jnp.where(col_mask[:, None, :], s, -1e30)
    p = jax.nn.softmax(s, axis=(-2, -1)).astype(v.dtype)
    o = jnp.einsum('bhrqkc,bhrkcd->bhrqd', p, v_rows)
    return o.transpose(0, 2, 3, 1, 4).reshape(B, L, NA_W)

def short_conv_mixer(b_gate, c_gate, x_in, w):
    return b_gate * dwconv3(c_gate * x_in, w)

def memory_cross_attention(h, mem_n, wq, wkv, wo):
    B, L, _ = h.shape
    M = mem_n.shape[1]
    q = (h @ wq).reshape(B, L, XA_HEADS, XA_HEAD_DIM)
    km, vm = jnp.split(mem_n @ wkv, 2, axis=-1)
    km = km.reshape(B, M, XA_HEADS, XA_HEAD_DIM)
    vm = vm.reshape(B, M, XA_HEADS, XA_HEAD_DIM)
    s = jnp.einsum('bshd,bmhd->bhsm', q, km).astype(jnp.float32) * (XA_HEAD_DIM ** -0.5)
    p = jax.nn.softmax(s, axis=-1).astype(h.dtype)
    o = jnp.einsum('bhsm,bmhd->bshd', p, vm).reshape(B, L, D_MODEL)
    return o @ wo

def conv_glu_ffn(h, w_up, w_conv, w_down):
    u = dwconv3(h @ w_up, w_conv)
    g, val = jnp.split(u, 2, axis=-1)
    return (jax.nn.gelu(g, approximate=True) * val) @ w_down

def second_inputs(seed: int = 0) -> dict:
    key = jax.random.key(seed)
    ks = jax.random.split(key, 24)

    def nrm(k, shape, scale):
        return jax.random.normal(k, shape, jnp.float32) * scale

    return {
        "x": nrm(ks[0], (BATCH, SEQ, D_MODEL), 1.0),
        "mem": nrm(ks[1], (BATCH, N_MEM, D_MODEL), 1.0),
        "norm_gains": 1.0 + nrm(ks[2], (DEPTH_2, 6, D_MODEL), 0.05),
        "mem_norm": 1.0 + nrm(ks[3], (DEPTH_2, D_MODEL), 0.05),
        "w_in": nrm(ks[4], (DEPTH_2, D_MODEL, PROJ_W), D_MODEL ** -0.5),
        "gate_bias": nrm(ks[5], (DEPTH_2, N_BRANCH, D_MODEL), 0.02),
        "hy_short_w": nrm(ks[6], (DEPTH_2, 3, 3 * HY_W), 3 ** -0.5),
        "hy_w1": nrm(ks[7], (DEPTH_2, HY_EMB, HY_HIDDEN), HY_EMB ** -0.5),
        "hy_b1": nrm(ks[8], (DEPTH_2, HY_HIDDEN), 0.02),
        "hy_w2": nrm(ks[9], (DEPTH_2, HY_HIDDEN, HY_HIDDEN), HY_HIDDEN ** -0.5),
        "hy_b2": nrm(ks[10], (DEPTH_2, HY_HIDDEN), 0.02),
        "hy_w3": nrm(ks[11], (DEPTH_2, HY_HIDDEN, 2 * HY_ORDER * HY_W), 0.05 * HY_HIDDEN ** -0.5),
        "hy_freq": 1.0 + nrm(ks[12], (DEPTH_2, 2, HY_HIDDEN), 0.05),
        "hy_bias": nrm(ks[13], (DEPTH_2, HY_ORDER, HY_W), 0.1),
        "na_rpb": nrm(ks[14], (DEPTH_2, NA_HEADS, 2 * NA_WIN_ROWS - 1, 2 * NA_WIN_COLS - 1), 0.02),
        "sc_conv_w": nrm(ks[15], (DEPTH_2, 3, SC_W), 3 ** -0.5),
        "w_branch": nrm(ks[16], (DEPTH_2, N_BRANCH, HY_W, D_MODEL), HY_W ** -0.5),
        "w_out": nrm(ks[17], (DEPTH_2, D_MODEL, D_MODEL), D_MODEL ** -0.5),
        "xa_wq": nrm(ks[18], (DEPTH_2, D_MODEL, D_MODEL), D_MODEL ** -0.5),
        "xa_wkv": nrm(ks[19], (DEPTH_2, D_MODEL, 2 * D_MODEL), D_MODEL ** -0.5),
        "xa_wo": nrm(ks[20], (DEPTH_2, D_MODEL, D_MODEL), D_MODEL ** -0.5),
        "ffn_up": nrm(ks[21], (DEPTH_2, D_MODEL, 2 * D_FF), D_MODEL ** -0.5),
        "ffn_conv": nrm(ks[22], (DEPTH_2, 3, 2 * D_FF), 3 ** -0.5),
        "ffn_down": nrm(ks[23], (DEPTH_2, D_FF, D_MODEL), D_FF ** -0.5),
    }

def second_block(x, mem, norm_gains, mem_norm, w_in, gate_bias, hy_short_w, hy_w1, hy_b1, hy_w2, hy_b2,
              hy_w3, hy_freq, hy_bias, na_rpb, sc_conv_w, w_branch, w_out, xa_wq, xa_wkv, xa_wo,
              ffn_up, ffn_conv, ffn_down):
    B, L, _ = x.shape
    splits = [3 * HY_W, 3 * HY_W + 3 * NA_W, 3 * HY_W + 3 * NA_W + 3 * SC_W]
    for l in range(DEPTH_2):
        g = norm_gains[l]
        h = rms_norm_2(x, g[0])
        proj = h @ w_in[l]
        hy_u, na_qkv, sc_u, gate_pre = jnp.split(proj, splits, axis=-1)
        kf = hyena_filters(L, hy_w1[l], hy_b1[l], hy_w2[l], hy_b2[l], hy_w3[l], hy_freq[l])
        y_a = hyena_mixer(hy_u, hy_short_w[l], kf, hy_bias[l])
        q, k, v = jnp.split(na_qkv, 3, axis=-1)
        y_b = neighbourhood_attention(q, k, v, na_rpb[l])
        b_gate, c_gate, x_in = jnp.split(sc_u, 3, axis=-1)
        y_c = short_conv_mixer(b_gate, c_gate, x_in, sc_conv_w[l])
        gates = jax.nn.sigmoid(gate_pre.reshape(B, L, N_BRANCH, D_MODEL) + gate_bias[l])
        merged = (gates[:, :, 0] * (y_a @ w_branch[l, 0])
                  + gates[:, :, 1] * (y_b @ w_branch[l, 1])
                  + gates[:, :, 2] * (y_c @ w_branch[l, 2]))
        x = x + rms_norm_2(merged @ w_out[l], g[1])
        h = rms_norm_2(x, g[2])
        mem_n = rms_norm_2(mem, mem_norm[l])
        x = x + rms_norm_2(memory_cross_attention(h, mem_n, xa_wq[l], xa_wkv[l], xa_wo[l]), g[3])
        h = rms_norm_2(x, g[4])
        x = x + rms_norm_2(conv_glu_ffn(h, ffn_up[l], ffn_conv[l], ffn_down[l]), g[5])
    return x


def setup_inputs(seed=0):
    out = dict(first_inputs(seed))
    for name, value in second_inputs(seed + 1).items():
        if name != "x":
            out[name + "_2"] = value
    return out


def reference(
    x, positions, diff_w_qkv, diff_lambda_q1, diff_lambda_k1, diff_lambda_q2, diff_lambda_k2,
    diff_subln_g, diff_w_o, fox_w_in, fox_b_f, fox_w_o, mla_w_down, mla_q_norm_g, mla_kv_norm_g,
    mla_w_uq, mla_w_ukv, mla_w_o, moba_w_qkv, moba_w_o, ffn_w_in, ffn_conv_w, ffn_conv_b,
    ffn_w_out, ln1_g, ln1_b, ln2_g, ln2_b, mem_2, norm_gains_2, mem_norm_2, w_in_2, gate_bias_2,
    hy_short_w_2, hy_w1_2, hy_b1_2, hy_w2_2, hy_b2_2, hy_w3_2, hy_freq_2, hy_bias_2, na_rpb_2,
    sc_conv_w_2, w_branch_2, w_out_2, xa_wq_2, xa_wkv_2, xa_wo_2, ffn_up_2, ffn_conv_2,
    ffn_down_2,
):
    x = first_block(
        x, positions, diff_w_qkv, diff_lambda_q1, diff_lambda_k1, diff_lambda_q2,
        diff_lambda_k2, diff_subln_g, diff_w_o, fox_w_in, fox_b_f, fox_w_o, mla_w_down,
        mla_q_norm_g, mla_kv_norm_g, mla_w_uq, mla_w_ukv, mla_w_o, moba_w_qkv, moba_w_o,
        ffn_w_in, ffn_conv_w, ffn_conv_b, ffn_w_out, ln1_g, ln1_b, ln2_g, ln2_b,
    )
    return second_block(
        x, mem_2, norm_gains_2, mem_norm_2, w_in_2, gate_bias_2, hy_short_w_2, hy_w1_2, hy_b1_2,
        hy_w2_2, hy_b2_2, hy_w3_2, hy_freq_2, hy_bias_2, na_rpb_2, sc_conv_w_2, w_branch_2,
        w_out_2, xa_wq_2, xa_wkv_2, xa_wo_2, ffn_up_2, ffn_conv_2, ffn_down_2,
    )


_drawn_inputs = setup_inputs


def setup_inputs(seed=0):
    import zlib

    import numpy as np

    out = dict(_drawn_inputs(seed))
    spreads = {}
    factors = {'diff_lambda_q1': 4.266,
     'diff_lambda_k1': 3.093,
     'diff_lambda_q2': 54.924,
     'diff_subln_g': 5.667,
     'ffn_conv_b': 5.989,
     'gate_bias_2': 8.0,
     'hy_b1_2': 8.0,
     'hy_b2_2': 8.0,
     'hy_freq_2': 8.0,
     'hy_bias_2': 3.016,
     'na_rpb_2': 22.806}
    for name, (base, spread) in spreads.items():
        noise = np.random.default_rng([zlib.crc32(name.encode()), seed]).standard_normal(out[name].shape)
        drawn = base * np.exp(spread * noise) if base else spread * noise
        out[name] = __import__('jax').numpy.asarray(drawn.astype(out[name].dtype))
    for name, factor in factors.items():
        out[name] = (out[name] * factor).astype(out[name].dtype)
    return out
```

```python
import math
from contextlib import ExitStack

import numpy as np

import concourse.bass as bass
from concourse import mybir

F32 = mybir.dt.float32
F32R = mybir.dt.float32r
ALU = mybir.AluOpType
ACT = mybir.ActivationFunctionType
AX = mybir.AxisListType.X

P = 128
S = 256
NT = S // P
D = 1024
KC = D // P
DFF = 2816
FI = DFF // 256
UNIT = 2048
DEPTH = 2
ALPHA = (2 * DEPTH) ** 0.25
LAMBDA_INIT = 0.8 - 0.6 * math.exp(-0.3 * 0)
NEG = -1e30

PHASES = [("l0_qk", 8, 4), ("l0_v", 4, 4), ("l0_wo", 4, 4), ("ffn0", 3 * FI, 3),
          ("l1_qk", 8, 4), ("l1_v", 4, 4), ("l1_wo", 4, 4), ("ffn1", 3 * FI, 3),
          ("hysc", 12, 4), ("naqkv", 6, 4), ("gates", 12, 4), ("branch", 6, 4), ("wout", 4, 4),
          ("xk", 4, 4), ("xv", 4, 4), ("xq", 4, 4), ("xo", 4, 4), ("ffn2", 3 * FI, 3)]


def plan():
    first, slot, use = {}, [], []
    uses, at = [0] * 4, 0
    for name, n, rot in PHASES:
        first[name] = len(slot)
        for j in range(n):
            s = (at + j % rot) % 4
            slot.append(s)
            uses[s] += 1
            use.append(uses[s])
        at = (at + (n if rot == 4 else n % rot)) % 4
    return first, slot, use


FIRST, SLOT, USE = plan()
NUNITS = len(SLOT)

BANK_STAGES = [("t_x", 4), ("l0_qk", 8), ("l0_v", 4), ("l0_wo", 4), ("t_ln0", 4), ("ffn0", 2 * FI), ("t_ln1", 4),
               ("l1_qk", 8), ("l1_v", 4), ("l1_wo", 4), ("t_ln2", 4), ("ffn1", 2 * FI),
               ("t_r0", 4), ("hysc", 12), ("naqkv", 6), ("gates", 12), ("branch", 12), ("wout", 4),
               ("t_mem", 4), ("xk", 4), ("xv", 4), ("t_r1", 4), ("xq", 4), ("xo", 4), ("t_r2", 4), ("ffn2", 2 * FI)]
BANK0, _n = {}, 0
for _name, _k in BANK_STAGES:
    BANK0[_name] = _n
    _n += _k

def counts_before(stages):
    before, total = {}, {}
    for tag, per_step, steps in stages:
        before[tag] = dict(total)
        for name, k in per_step.items():
            total[name] = total.get(name, 0) + k * steps
    for b in before.values():
        for name in total:
            b.setdefault(name, 0)
    return before


def attention_signals(kind):
    maps = 1 if kind == "xa" else 2
    npt = 1 if kind == "diff" else maps
    out = dict(st=1, sc=maps, sc_read=2 * maps, nb=1, ex=2 * maps, rs=1, pn=1, pt=npt, pt_read=npt, o=1, o_hi=1, o_read=1)
    if kind == "diff":
        out.update(rl=1, p2=2, sq=1, ms=1, ln=1, ov=1)
        out["or"] = 1
    return out


ATT0 = counts_before([("att0", attention_signals("diff"), 8), ("att1", attention_signals("fox"), 8),
                      ("attn", attention_signals("na"), 4), ("attx", attention_signals("xa"), 4)])
FFN0 = counts_before([("f0", dict(fa=2, fc=4, ft=1, fh=1, h=1), FI), ("f1", dict(fa=2, fc=4, ft=1, fh=1, h=1), FI),
                      ("f2", dict(fa=4, fc=8, fs=1, ft=1, fd=1, fv=1, fh=1, h=1), FI)])

COLS, _n = {}, 0
for _name, _k in [("ident", P), ("rotT", P), ("mean", P), ("cmask", 384), ("namask", 256), ("ones16", P), ("eye16", 16),
                  ("ln1g", 16), ("ln1b", 16), ("ln2g", 16), ("ln2b", 16), ("ng", 48), ("memg", 8),
                  ("conv0", FI * 8), ("conv1", FI * 8), ("conv2", FI * 12), ("hyw", 36), ("hyb", 8), ("scw", 12),
                  ("gateb", 24), ("hb1", 1), ("hb2", 1), ("hf1", 1), ("hf2", 1), ("invf", 1), ("subg", 1),
                  ("eps_rms", 1), ("halfpi", 1)]:
    COLS[_name] = (_n, _n + _k)
    _n += _k
NCOLS = _n
ROWS = ["ln1g0", "ln1b0", "ln2g0", "ln2b0", "ln1g1", "ln1b1", "ln2g1", "ln2b1", "ng1", "ng3", "ng5"]


class Unit:

    def __init__(self, g, i=None, body=0, trips=1):
        self.g, self.i, self.body, self.trips = g, i, body, trips

    def plus(self, k):
        return Unit(self.g + k, self.i, self.body, self.trips)

    def count(self, k=0):
        return self.g + k if self.i is None else self.i * self.body + (self.g + k)

    @property
    def slot(self):
        assert all(SLOT[self.g + self.body * m] == SLOT[self.g] for m in range(self.trips))
        return SLOT[self.g]

    @property
    def loaded(self):
        if self.i is None:
            return 16 * USE[self.g]
        step = USE[self.g + self.body] - USE[self.g]
        assert all(USE[self.g + self.body * m] == USE[self.g] + step * m for m in range(self.trips))
        return self.i * (16 * step) + 16 * USE[self.g]

    @property
    def par(self):
        return self.g % 2


def two_blocks_kernel(nc, A):
    ctx = ExitStack()
    with ctx:
        sems = {}

        def sem(name):
            if name not in sems:
                sems[name] = ctx.enter_context(nc.semaphore(name))
            return sems[name]

        at = [16512]

        def region(nbytes):
            r = at[0]
            at[0] += nbytes
            assert at[0] <= 229344, at[0]
            return r

        def place(name, shape, off, dt=F32):
            return nc.alloc_sbuf_tensor_at(name, shape, dt, offset=off)

        KB = 1024
        w_raw = [place(f"w_raw{j}", [P, UNIT], region(8 * KB)) for j in range(4)]
        w_hi = [place(f"w_hi{j}", [P, UNIT], region(8 * KB), F32R) for j in range(2)]
        w_lo = [place(f"w_lo{j}", [P, UNIT], region(8 * KB), F32R) for j in range(2)]
        x_tok = place("x_tok", [P, NT, D], region(8 * KB))
        scr = region(28 * KB)
        aT_hi = place("aT_hi", [P, KC, S], region(8 * KB), F32R)
        aT_lo = place("aT_lo", [P, KC, S], region(8 * KB), F32R)
        qkv_at = region(24 * KB)
        hysc_at = region(24 * KB)
        yT_at = region(24 * KB)
        maps_at = region(8 * KB)
        cst = place("cst", [P, NCOLS], region((NCOLS * 4 + 31) // 32 * 32))
        small_at = region(2 * KB)

        def col(name, a=0, b=None):
            lo, hi = COLS[name]
            return cst[:, lo + a:hi if b is None else lo + b]

        ident = col("ident")
        qkv = place("qkv", [P, 8, 768], qkv_at)
        xqkv = place("xqkv", [P, 4, 1536], qkv_at)
        hysc = place("hysc", [P, 24, S], hysc_at)
        gates = place("gates", [P, 24, S], hysc_at)
        mem_tok = place("mem_tok", [P, NT, D], hysc_at)
        fox_c = place("fox_c", [P, 16, S], hysc_at)
        fox_d = place("fox_d", [16, 16, S], yT_at)
        ya_hi = place("ya_hi", [P, 4, S], yT_at, F32R)
        ya_lo = place("ya_lo", [P, 4, S], yT_at + 4 * KB, F32R)
        yb_hi = place("yb_hi", [P, 4, S], yT_at + 8 * KB, F32R)
        yb_lo = place("yb_lo", [P, 4, S], yT_at + 12 * KB, F32R)
        yc_hi = place("yc_hi", [P, 4, S], yT_at + 16 * KB, F32R)
        yc_lo = place("yc_lo", [P, 4, S], yT_at + 20 * KB, F32R)
        memT_hi = place("memT_hi", [P, KC, S], yT_at, F32R)
        memT_lo = place("memT_lo", [P, KC, S], yT_at + 8 * KB, F32R)
        spec = place("spec", [P, 2, 2, 2, 512], yT_at + 8 * KB)
        gmap = place("gmap", [P, D], maps_at)
        bmap = place("bmap", [P, D], maps_at + 4 * KB)
        dft = place("dft", [P, 4, 2, S], maps_at)
        rope_c = place("rope_c", [P, S], small_at)
        rope_s = place("rope_s", [P, S], small_at + KB)

        nrm = place("nrm", [P, NT, D], scr)
        vT = place("vT", [P, KC, S], scr + 8 * KB)
        junk = [place(f"junk{t}", [P, D], scr + (16 + 4 * t) * KB) for t in range(NT)]
        tiny = region(KB)
        stat = place("stat", [P, NT, 2, 6], tiny)
        mv = place("mv", [P, NT, 2], tiny + 128)
        rstd = place("rstd", [P, NT], tiny + 192)
        ssum = place("ssum", [P, NT, 4], tiny + 256)
        ssq = place("ssq", [P, NT], tiny + 320)
        mhalf = place("mhalf", [P, NT], tiny + 384)
        ff = scr + 8 * KB
        f_a = [place(f"f_a{j}", [P, 2, S], ff + 2 * KB * j) for j in range(2)]
        f_u = [place(f"f_u{j}", [P, 2, S], ff + (4 + 2 * j) * KB) for j in range(2)]
        f_t = place("f_t", [P, 2, S], ff + 8 * KB)
        f_v = place("f_v", [P, 2, S], ff + 10 * KB)
        hT_hi = [place(f"hT_hi{j}", [P, 2, S], ff + (12 + 2 * j) * KB, F32R) for j in range(2)]
        hT_lo = [place(f"hT_lo{j}", [P, 2, S], ff + (16 + 2 * j) * KB, F32R) for j in range(2)]
        st = [place(f"st{j}", [P, 1536], scr + 6 * KB * j) for j in range(2)]
        mc = [place(f"mc{j}", [P, 2, 512], scr + (6 + 4 * j) * KB) for j in range(2)]
        pb = [place(f"pb{j}", [P, 2, 512], scr + (14 + 4 * j) * KB) for j in range(2)]
        pT = place("pT", [P, 2, 512], scr + 22 * KB)
        o_v = place("o_v", [P, S], scr + 26 * KB)
        o_r = place("o_r", [P, S], scr + 7 * KB)
        o_q = place("o_q", [P, S], scr + 12 * KB + 0)
        mx = [place(f"mx{j}", [P, 4], tiny + 448 + 32 * j) for j in range(2)]
        nb = [place(f"nb{j}", [P, 4], tiny + 576 + 32 * j) for j in range(2)]
        sm = [place(f"sm{j}", [P, 4], tiny + 704 + 32 * j) for j in range(2)]
        rs = [place(f"rs{j}", [P, 4], tiny + 832 + 32 * j) for j in range(2)]
        st_d = [place(f"st_d{j}", [P, 768], scr + 3 * KB * j) for j in range(2)]
        ang = place("ang", [P, S], scr + 0)
        ang_k = place("ang_k", [P, S], scr + KB)
        ang_a = place("ang_a", [P, S], scr + 2 * KB)
        pos_i = place("pos_i", [P, S], scr + 3 * KB, mybir.dt.int32)
        lam_in = place("lam_in", [P, 4, 64], scr + 4 * KB)
        lam_j = place("lam_j", [P, 2, 64], scr + 5 * KB)
        lam = place("lam", [P, 4], region(32))
        sub_g = place("sub_g", [P, 1], region(32))
        rot_t = place("rot_t", [P, 2, S], scr + 20 * KB)
        fw = place("fw", [P, KC, 16], scr + 0)
        fw_hi = place("fw_hi", [P, KC, 16], scr + 512, F32R)
        fw_lo = place("fw_lo", [P, KC, 16], scr + 1024, F32R)
        f_b = place("f_b", [P, 16], scr + 1536)
        f_tok = place("f_tok", [P, NT, 16], scr + 1664)
        f_z = place("f_z", [16, S], scr + 2 * KB)
        f_abs = place("f_abs", [16, S], scr + 3 * KB)
        f_min = place("f_min", [16, S], scr + 4 * KB)
        f_ones = place("f_ones", [16, S], scr + 5 * KB)
        f_cum = place("f_cum", [16, S], scr + 6 * KB)
        zembT = place("zembT", [33, S], scr + 0)
        hw1 = place("hw1", [33, 64], scr + KB)
        hw2 = place("hw2", [64, 64], scr + KB + 256)
        hw3 = place("hw3", [64, 2048], scr + 2 * KB)
        h_x = place("h_x", [64, S], scr + 10 * KB)
        h_k = place("h_k", [64, S], scr + 11 * KB)
        h_a = place("h_a", [64, S], qkv_at + 4 * KB)
        decay = place("decay", [P, 2, NT, 512], scr + 12 * KB)
        h_s = place("h_s", [P, 2, NT, 512], scr + 20 * KB)
        h_t = place("h_t", [P, 512], qkv_at)
        h_u = place("h_u", [P, 512], qkv_at + 2 * KB)
        z_tok = place("z_tok", [P, NT, 512], scr + 0)
        y_f = place("y_f", [P, 2, 2, 512], scr + 4 * KB)
        y_t = place("y_t", [P, 512], scr + 12 * KB)
        cv = [place(f"cv{j}", [P, 4, S], scr + (14 + 4 * j) * KB) for j in range(2)]
        cp = [place(f"cp{j}", [P, 4, S], qkv_at + (12 + 4 * j) * KB) for j in range(2)]
        z_s = place("z_s", [P, 4, S], scr + 22 * KB)
        m_acc = place("m_acc", [P, KC, S], scr + 0)
        m_t = place("m_t", [P, 2, S], scr + 8 * KB)

        ps = ctx.enter_context(nc.psum_tensor("ps", [P, 8, 512], F32))

        block = ctx.enter_context(nc.Block())

        def convert_hi(act, u):
            act.wait_ge(sem(f"w_loaded{u.slot}"), u.loaded)
            if u.g >= 2:
                act.wait_ge(sem("w_used"), u.count(-1))
            act.activation(w_hi[u.par][:, :], w_raw[u.slot][:, :], ACT.Copy).then_inc(sem("hi_ready"), 1)

        def convert_lo(dve, u):
            dve.wait_ge(sem("hi_ready"), u.count(1))
            dve.tensor_tensor(w_lo[u.par][:, :], w_raw[u.slot][:, :], w_hi[u.par][:, :], ALU.subtract)\
               .then_inc(sem("lo_ready"), 1)

        def next_hi(act, u, ahead=2):
            if u.g + ahead < NUNITS:
                convert_hi(act, u.plus(ahead))

        def next_lo(dve, u, ahead=2):
            if u.g + ahead < NUNITS:
                convert_lo(dve, u.plus(ahead))

        def bank(stage, j):
            return (BANK0[stage] + j) % 4

        def bank_value(stage, j, i=None, body=4, k=0):
            v = BANK0[stage] + j + k
            return v if i is None else i * body + v

        def v(u, k, m, i):
            return (u + m) * k if i is None else i * (2 * k) + (u + m) * k

        def heads(eng, step, n):
            step(0, None)
            step(1, 0)
            trips = (n - 2) // 2
            if trips > 1:
                with eng.Fori(0, trips) as i:
                    step(2, 1, i)
                    step(3, 2, i)
            else:
                step(2, 1)
                step(3, 2)
            step(None, n - 1)

        def last_unit(phase):
            return FIRST[phase] + dict((x[0], x[1]) for x in PHASES)[phase]

        @block.sync
        def _(sp):
            def load(u):
                if u.g >= 3:
                    sp.wait_ge(sem("lo_ready"), u.count(-2))
                src = A["wstream"][u.g] if u.i is None else A["wstream"][u.i * u.body + u.g]
                sp.dma_start(w_raw[u.slot][:, :], src).then_inc(sem(f"w_loaded{u.slot}"), 16)

            sp.dma_start(x_tok[:, :, :], A["x"].rearrange("(t p) d -> p t d", p=P)).then_inc(sem("x_loaded"), 16)
            sp.dma_start(cst[:, :], A["cst"]).then_inc(sem("cst_loaded"), 16)
            for name, n, rot in PHASES:
                g0 = FIRST[name]
                if name == "l0_qk":
                    for j in range(4):
                        load(Unit(g0 + j))
                    for j in range(4, 8):
                        load(Unit(g0 + j))
                elif rot == 3:
                    trips = (n - 3) // 6
                    with sp.Fori(0, trips) as i:
                        for j in range(6):
                            load(Unit(g0 + j, i, 6, trips))
                    for j in range(6 * trips, n):
                        load(Unit(g0 + j))
                elif n >= 8:
                    with sp.Fori(0, n // 4) as i:
                        for j in range(4):
                            load(Unit(g0 + j, i, 4, n // 4))
                else:
                    for j in range(n):
                        load(Unit(g0 + j))
            sp.wait_ge(sem("out_ready"), 2)
            sp.dma_start(A["out"].rearrange("(t p) d -> p t d", p=P), x_tok[:, :, :]).then_inc(sem("out_stored"), 16)
            sp.wait_ge(sem("out_stored"), 16)

        @block.tensor
        def _(pe):
            def three(out, l_hi, l_lo, r_hi, r_lo, start, stop):
                pe.matmul(out, l_hi, r_hi, start=start, stop=False)
                pe.matmul(out, l_hi, r_lo, start=False, stop=False)
                return pe.matmul(out, l_lo, r_hi, start=False, stop=stop)

            def transposes(stage, src):
                for b in range(4):
                    pe.wait_ge(sem("src_" + stage), 1 if stage == "t_x" else 2)
                    if stage != "t_x":
                        pe.wait_ge(sem("bank_free"), bank_value(stage, b, k=-3))
                    for c in range(2):
                        for t in range(NT):
                            k = 2 * b + c
                            mm = pe.transpose(ps[:, bank(stage, b), c * S + t * P:c * S + t * P + P],
                                              src[:, t, k * P:(k + 1) * P], ident)
                    mm.then_inc(sem("pe_" + stage), 1)

            def unit_b(u, stage, j, i=None, a=(aT_hi, aT_lo)):
                pe.wait_ge(sem("lo_ready"), u.count(1))
                pe.wait_ge(sem("bank_free"), bank_value(stage, j, i, k=-3))
                hi = w_hi[u.par][:, :].rearrange("p (k n) -> p k n", k=KC)
                lo = w_lo[u.par][:, :].rearrange("p (k n) -> p k n", k=KC)
                for c in range(2):
                    for k in range(KC):
                        mm = three(ps[:, bank(stage, j), c * S:(c + 1) * S], hi[:, k, c * P:(c + 1) * P],
                                   lo[:, k, c * P:(c + 1) * P], a[0][:, k, :], a[1][:, k, :], k == 0, k == KC - 1)
                mm.then_inc(sem("w_used"), 1)

            def unit_a(u, stage, j, i=None, a=(aT_hi, aT_lo)):
                pe.wait_ge(sem("lo_ready"), u.count(1))
                pe.wait_ge(sem("bank_free"), bank_value(stage, j, i, k=-3))
                hi = w_hi[u.par][:, :].rearrange("p (k n) -> p k n", k=KC)
                lo = w_lo[u.par][:, :].rearrange("p (k n) -> p k n", k=KC)
                for t in range(NT):
                    for k in range(KC):
                        mm = three(ps[:, bank(stage, j), t * S:(t + 1) * S], a[0][:, k, t * P:(t + 1) * P],
                                   a[1][:, k, t * P:(t + 1) * P], hi[:, k, :], lo[:, k, :], k == 0, k == KC - 1)
                mm.then_inc(sem("w_used"), 1)

            def units(stage, unit, a=(aT_hi, aT_lo)):
                n, g0 = dict((x[0], x[1]) for x in PHASES)[stage], FIRST[stage]
                if n >= 8:
                    with pe.Fori(0, n // 4) as i:
                        for j in range(4):
                            unit(Unit(g0 + j, i, 4, n // 4), stage, j, i, a)
                else:
                    for j in range(n):
                        unit(Unit(g0 + j), stage, j, None, a)

            def ffn(stage, tag):
                g0 = FIRST[stage]

                def up(u, k, i=None):
                    for j in range(2):
                        unit_b(u.plus(j), stage, 2 * k + j, i)

                def down(u, k, first=False, last=False, i=None):
                    pe.wait_ge(sem("lo_ready"), u.count(1))
                    pe.wait_ge(sem("ffn_h"), FFN0[tag]["h"] + (i * 2 if i is not None else 0) + k + 1)
                    hi = w_hi[u.par][:, :].rearrange("p (k n) -> p k n", k=2)
                    lo = w_lo[u.par][:, :].rearrange("p (k n) -> p k n", k=2)
                    q = k % 2
                    for t in range(NT):
                        for h in range(2):
                            for c in range(2):
                                mm = three(ps[:, 4 + 2 * t + h, :], hT_hi[q][:, c, t * P:(t + 1) * P],
                                           hT_lo[q][:, c, t * P:(t + 1) * P], hi[:, c, h * 512:(h + 1) * 512],
                                           lo[:, c, h * 512:(h + 1) * 512], first and c == 0, last and c == 1)
                    mm.then_inc(sem("w_used"), 1)

                up(Unit(g0), 0)
                up(Unit(g0 + 2), 1)
                down(Unit(g0 + 4), 0, first=True)
                trips = (FI - 3) // 2
                with pe.Fori(0, trips) as i:
                    for j in range(2):
                        up(Unit(g0 + 5 + 3 * j, i, 6, trips), 2 + j, i)
                        down(Unit(g0 + 7 + 3 * j, i, 6, trips), 1 + j, i=i)
                up(Unit(g0 + 5 + 6 * trips), FI - 1)
                down(Unit(g0 + 7 + 6 * trips), FI - 2)
                down(Unit(g0 + 8 + 6 * trips), FI - 1, last=True)

            def attention(tag, kind, n):
                causal = kind in ("diff", "fox")
                maps = 1 if kind == "xa" else 2
                q_cols = [(0, 128), (128, 256)] if causal else [(0, 256), (256, 256)]

                def scores(u, i=None):
                    p = u % 2
                    src = st_d[p] if kind != "xa" else st[p]
                    pe.wait_ge(sem("att_st"), ATT0[tag]["st"] + v(u, 1, 1, i))
                    if u > 0 or i is not None:
                        pe.wait_ge(sem("att_sc_read"), ATT0[tag]["sc_read"] + v(u, 2 * maps, 0, i))
                    for m in range(maps):
                        for t in range(NT):
                            c0, n_k = q_cols[t]
                            out = ps[:, 4 + m, c0:c0 + n_k]
                            if kind == "xa":
                                for c in range(2):
                                    mm = pe.matmul(out, src[:, c * S + t * P:c * S + t * P + P],
                                                   src[:, 512 + c * S:512 + (c + 1) * S], start=c == 0, stop=c == 1)
                            else:
                                r = slice(64 * m, 64 * m + 64)
                                mm = pe.matmul(out, src[r, t * P:(t + 1) * P], src[r, S:S + n_k], start=True, stop=True)
                        mm.then_inc(sem("att_sc"), 1)

                def values(u, i=None):
                    p = u % 2
                    src = st_d[p] if kind != "xa" else st[p]
                    npt = 1 if kind == "diff" else maps
                    pe.wait_ge(sem("att_pn"), ATT0[tag]["pn"] + v(u, 1, 1, i))
                    if u > 0 or i is not None:
                        pe.wait_ge(sem("att_pt_read"), ATT0[tag]["pt_read"] + v(u, npt, 0, i))
                    for m in range(npt):
                        for kt in range(NT):
                            for t in range(NT):
                                if causal and kt > t:
                                    continue
                                c0 = q_cols[t][0] + kt * P
                                to = (0 if kt == 0 else S) + (t * P if not (causal and kt == 1) else 0)
                                mm = pe.transpose(ps[:, 6 + m, to:to + P], pb[p][:, m, c0:c0 + P], ident)
                        mm.then_inc(sem("att_pt"), 1)
                    if u > 0 or i is not None:
                        pe.wait_ge(sem("att_o_read"), ATT0[tag]["o_read"] + v(u, 1, 0, i))
                    ob = ps[:, p, :]
                    for m in range(npt):
                        pe.wait_ge(sem("att_pt_read"), ATT0[tag]["pt_read"] + v(u, npt, 0, i) + (m + 1))
                        outs = [(slice(64 * m, 64 * m + 64), 0, S + 64 * m, 64, P)]
                        if kind == "diff":
                            outs = [(slice(0, P), 0, S + S, P, P)]
                        elif kind == "xa":
                            outs = [(slice(0, P), c * S, 1024 + c * P, P, S) for c in range(2)]
                        else:
                            outs = [(slice(64 * m, 64 * m + 64), 0, 2 * S + 64 * m, 64, P)]
                        for rows, o0, v0, width, step in outs:
                            for kt in range(NT):
                                lhs = src[:, v0 + kt * step:v0 + kt * step + width]
                                if kt == 0:
                                    mm = pe.matmul(ob[rows, o0:o0 + S], lhs, pT[:, m, 0:S], start=True, stop=False)
                                elif causal:
                                    mm = pe.matmul(ob[rows, o0 + P:o0 + S], lhs, pT[:, m, S:S + P], start=False, stop=True)
                                else:
                                    mm = pe.matmul(ob[rows, o0:o0 + S], lhs, pT[:, m, S:2 * S], start=False, stop=True)
                    mm.then_inc(sem("att_o"), 1)
                    if kind == "diff":
                        pe.wait_ge(sem("att_sq"), ATT0[tag]["sq"] + v(u, 1, 1, i))
                        pe.matmul(ob[:, S:2 * S], col("mean"), o_q[:, :], start=True, stop=True)\
                          .then_inc(sem("att_ms"), 1)

                def step(ahead, behind, i=None):
                    if ahead is not None:
                        scores(ahead, i)
                    if behind is not None:
                        values(behind, i)

                heads(pe, step, n)

            pe.wait_ge(sem("cst_loaded"), 16)
            pe.wait_ge(sem("x_loaded"), 16)
            for b in range(4):
                for c in range(2):
                    for t in range(NT):
                        k = 2 * b + c
                        mm = pe.transpose(ps[:, b, c * S + t * P:c * S + t * P + P], x_tok[:, t, k * P:(k + 1) * P], ident)
                mm.then_inc(sem("pe_t_x"), 1)
            pe.wait_ge(sem("bank_free"), BANK0["t_x"] + 4)
            units("l0_qk", unit_b)
            for j in range(4):
                unit_a(Unit(FIRST["l0_v"] + j), "l0_v", j)
                for h in (2 * j, 2 * j + 1):
                    pe.wait_ge(sem("bank_free"), BANK0["l0_v"])
                    if h >= 4:
                        pe.wait_ge(sem("rot_read"), h - 3)
                    pe.matmul(ps[:, 4 + h % 4, :], col("rotT"), qkv[:, h, 0:512], start=True, stop=True)\
                      .then_inc(sem("rot_done"), 1)
            pe.wait_ge(sem("rot_read"), 8)
            pe.wait_ge(sem("bank_free"), BANK0["l0_wo"])
            attention("att0", "diff", 8)
            pe.wait_ge(sem("att_o_read"), ATT0["att0"]["o_read"] + 8)
            units("l0_wo", unit_a)
            transposes("t_ln0", nrm)
            pe.wait_ge(sem("bank_free"), BANK0["t_ln0"] + 4)
            ffn("ffn0", "f0")
            transposes("t_ln1", nrm)
            pe.wait_ge(sem("bank_free"), BANK0["t_ln1"] + 4)
            units("l1_qk", unit_b)
            units("l1_v", unit_a)
            pe.wait_ge(sem("fw_split"), 2)
            for t in range(NT):
                for k in range(KC):
                    mm = three(ps[:, 4, t * 16:t * 16 + 16], aT_hi[:, k, t * P:(t + 1) * P], aT_lo[:, k, t * P:(t + 1) * P],
                               fw_hi[:, k, :], fw_lo[:, k, :], k == 0, k == KC - 1)
            mm.then_inc(sem("f_done"), 1)
            pe.wait_ge(sem("f_tok"), 1)
            for t in range(NT):
                mm = pe.transpose(ps[0:16, 5, t * P:(t + 1) * P], f_tok[:, t, :], ident)
            mm.then_inc(sem("f_done"), 1)
            pe.wait_ge(sem("fox_d"), 1)
            for j in range(8):
                if j >= 4:
                    pe.wait_ge(sem("fox_c"), j - 3)
                pe.matmul(ps[:, 4 + j % 4, :], col("ones16")[0:16, :],
                          fox_d[:, 2 * j:2 * j + 2, :].rearrange("p a b -> p (a b)"), start=True, stop=True)\
                  .then_inc(sem("fox_pe"), 1)
            pe.wait_ge(sem("fox_c"), 8)
            pe.wait_ge(sem("bank_free"), BANK0["l1_wo"])
            attention("att1", "fox", 8)
            pe.wait_ge(sem("att_o_read"), ATT0["att1"]["o_read"] + 8)
            units("l1_wo", unit_a)
            transposes("t_ln2", nrm)
            pe.wait_ge(sem("bank_free"), BANK0["t_ln2"] + 4)
            ffn("ffn1", "f1")
            pe.wait_ge(sem("hin_loaded"), 16 * 6)
            pe.wait_ge(sem("ln3_read"), 4)
            pe.matmul(ps[0:64, 4, 0:S], hw1[:, :], zembT[:, :], start=True, stop=True).then_inc(sem("h_pe"), 1)
            pe.wait_ge(sem("h_sin"), 1)
            pe.matmul(ps[0:64, 5, 0:S], hw2[:, :], h_x[:, :], start=True, stop=True).then_inc(sem("h_pe"), 1)
            pe.wait_ge(sem("h_sin"), 2)
            for o in range(2):
                for t in range(NT):
                    if o + t > 0:
                        pe.wait_ge(sem("h_mix"), 2 * (2 * o + t))
                    for d in range(2):
                        mm = pe.matmul(ps[:, 4 + d, :], h_x[:, t * P:(t + 1) * P],
                                       hw3[:, (2 * d + o) * 512:(2 * d + o + 1) * 512], start=True, stop=True)
                    mm.then_inc(sem("h_pe"), 1)
                pe.wait_ge(sem("h_mix"), 4 * (o + 1))
                for part in range(2):
                    for f in range(2):
                        n = 4 * o + 2 * part + f
                        if n >= 2:
                            pe.wait_ge(sem("spec_read"), n - 1)
                        for t in range(NT):
                            mm = pe.matmul(ps[:, 6 + f, :], dft[:, part, t, f * P:(f + 1) * P], h_s[:, part, t, :],
                                           start=t == 0, stop=t == NT - 1)
                        mm.then_inc(sem("spec_pe"), 1)
            transposes("t_r0", nrm)
            pe.wait_ge(sem("bank_free"), BANK0["t_r0"] + 4)
            units("hysc", unit_b)
            for o in range(2):
                pe.wait_ge(sem("z_ready"), o + 1)
                for b in range(2):
                    for c in range(2):
                        for t in range(NT):
                            k = 2 * b + c
                            src = (z_s if o else hysc)[:, k, t * P:(t + 1) * P]
                            mm = pe.transpose(ps[:, 4 + t, k * P:(k + 1) * P], src, ident)
                mm.then_inc(sem("zt_pe"), 1)
                pe.wait_ge(sem("z_tok"), 2 * (o + 1))
                for part in range(2):
                    for f in range(2):
                        for t in range(NT):
                            mm = pe.matmul(ps[:, 4 + 2 * part + f, :], dft[:, part, t, f * P:(f + 1) * P], z_tok[:, t, :],
                                           start=t == 0, stop=t == NT - 1)
                mm.then_inc(sem("zf_pe"), 1)
                pe.wait_ge(sem("y_f"), o + 1)
                for k in range(4):
                    for part in range(2):
                        for f in range(2):
                            mm = pe.matmul(ps[:, 4 + k // 2, (k % 2) * S:(k % 2 + 1) * S],
                                           y_f[:, part, f, k * P:(k + 1) * P], dft[:, 2 + part, f, :],
                                           start=part + f == 0, stop=part + f == 2)
                mm.then_inc(sem("yt_pe"), 1)
            for j in range(4):
                unit_b(Unit(FIRST["naqkv"] + j), "naqkv", j)
            for j in range(4, 6):
                unit_a(Unit(FIRST["naqkv"] + j), "naqkv", j)
            pe.wait_ge(sem("bank_free"), BANK0["gates"])
            attention("attn", "na", 4)
            pe.wait_ge(sem("att_o_read"), ATT0["attn"]["o_read"] + 4)
            units("gates", unit_b)
            pe.wait_ge(sem("yc_split"), 2)
            for j in range(6):
                u, half, br = Unit(FIRST["branch"] + j), j // 3, j % 3
                a_hi, a_lo = [(ya_hi, ya_lo), (yb_hi, yb_lo), (yc_hi, yc_lo)][br]
                pe.wait_ge(sem("lo_ready"), u.count(1))
                hi = w_hi[u.par][:, :].rearrange("p (k n) -> p k n", k=4)
                lo = w_lo[u.par][:, :].rearrange("p (k n) -> p k n", k=4)
                for b in range(2):
                    pe.wait_ge(sem("bank_free"), bank_value("branch", 2 * j + b, k=-3))
                    for c in range(2):
                        m = 2 * b + c
                        for k in range(4):
                            mm = three(ps[:, bank("branch", 2 * j + b), c * S:(c + 1) * S], hi[:, k, m * P:(m + 1) * P],
                                       lo[:, k, m * P:(m + 1) * P], a_hi[:, k, :], a_lo[:, k, :], k == 0, k == 3)
                mm.then_inc(sem("w_used"), 1)
            pe.wait_ge(sem("merged"), 4)
            units("wout", unit_a)
            transposes("t_mem", mem_tok)
            pe.wait_ge(sem("bank_free"), BANK0["t_mem"] + 4)
            units("xk", unit_b, (memT_hi, memT_lo))
            units("xv", unit_a, (memT_hi, memT_lo))
            transposes("t_r1", nrm)
            pe.wait_ge(sem("bank_free"), BANK0["t_r1"] + 4)
            units("xq", unit_b)
            pe.wait_ge(sem("bank_free"), BANK0["xo"])
            attention("attx", "xa", 4)
            pe.wait_ge(sem("att_o_read"), ATT0["attx"]["o_read"] + 4)
            units("xo", unit_a)
            transposes("t_r2", nrm)
            pe.wait_ge(sem("bank_free"), BANK0["t_r2"] + 4)
            ffn("ffn2", "f2")

        @block.scalar
        def _(act):
            def follow(phase, extra=None):
                n, g0 = dict((x[0], x[1]) for x in PHASES)[phase], FIRST[phase]
                if n >= 8:
                    with act.Fori(0, n // 4) as i:
                        for j in range(4):
                            next_hi(act, Unit(g0 + j, i, 4, n // 4))
                            if extra:
                                extra(j, i)
                else:
                    for j in range(n):
                        next_hi(act, Unit(g0 + j))
                        if extra:
                            extra(j, None)

            def gains(stage, g, b=None):
                for k in range(KC):
                    act.wait_ge(sem("pe_" + stage), k // 2 + 1)
                    c = (k % 2) * S
                    act.activation(vT[:, k, :], ps[:, bank(stage, k // 2), c:c + S], ACT.Identity, scale=g[:, k:k + 1],
                                   bias=0.0 if b is None else b[:, k:k + 1]).then_inc(sem("v_" + stage), 1)

            def ffn(phase, tag, second=False):
                g0 = FIRST[phase]
                w = col("conv" + tag[1])
                per = 4 if second else 2

                def hidden(u, k, i=None):
                    q = k % 2
                    K = lambda a, c=0: v(k, a, 0, i) + c
                    gb, ub = bank(phase, 2 * k), bank(phase, 2 * k + 1)
                    cols = 12 if second else 8
                    act.wait_ge(sem("w_used"), u.count(1))
                    if second:
                        act.wait_ge(sem("w_used"), u.count(2))
                    if k >= 2:
                        act.wait_ge(sem("ffn_h"), FFN0[tag]["h"] + K(1, -1))
                    for c in range(2):
                        o = 6 * c if second else 4 * c
                        tap = w[:, bass.ds(K(cols, o + (1 if second else 2)), 1)]
                        off = 0.0 if second else w[:, bass.ds(K(cols, o + 3), 1)]
                        act.activation(f_a[q][:, c, :], ps[:, gb, c * S:(c + 1) * S], ACT.Identity, scale=tap, bias=off)\
                           .then_inc(sem("ffn_fa"), 1)
                        if second:
                            tap = w[:, bass.ds(K(cols, o + 4), 1)]
                            act.activation(f_u[q][:, c, :], ps[:, ub, c * S:(c + 1) * S], ACT.Identity, scale=tap)\
                               .then_inc(sem("ffn_fa"), 1)
                    act.wait_ge(sem("ffn_fc"), FFN0[tag]["fc"] + K(2 * per, 2 * per))
                    if k >= 1:
                        act.wait_ge(sem("ffn_h"), FFN0[tag]["h"] + K(1))
                    if second:
                        act.activation(f_t[:, :, :], f_a[q][:, :, :], ACT.Square).then_inc(sem("ffn_fs"), 1)
                        act.wait_ge(sem("bank_free"), bank_value(phase, 2 * k + 2, i))
                        act.activation(f_t[:, :, :], f_t[:, :, :], ACT.Tanh).then_inc(sem("ffn_ft"), 1)
                        act.wait_ge(sem("ffn_fv"), FFN0[tag]["fv"] + K(1, 1))
                    else:
                        act.activation(f_t[:, :, :], f_a[q][:, :, :], ACT.Tanh, scale=0.5).then_inc(sem("ffn_ft"), 1)
                        act.wait_ge(sem("bank_free"), bank_value(phase, 2 * k + 2, i))
                    act.activation(hT_hi[q][:, :, :], f_v[:, :, :], ACT.Copy).then_inc(sem("ffn_fh"), 1)

                def up(u, k, i=None):
                    next_hi(act, u)
                    next_hi(act, u.plus(1))
                    hidden(u, k, i)

                up(Unit(g0), 0)
                up(Unit(g0 + 2), 1)
                next_hi(act, Unit(g0 + 4))
                trips = (FI - 3) // 2
                with act.Fori(0, trips) as i:
                    for j in range(2):
                        up(Unit(g0 + 5 + 3 * j, i, 6, trips), 2 + j, i)
                        next_hi(act, Unit(g0 + 7 + 3 * j, i, 6, trips))
                up(Unit(g0 + 5 + 6 * trips), FI - 1)
                next_hi(act, Unit(g0 + 7 + 6 * trips))
                next_hi(act, Unit(g0 + 8 + 6 * trips))

            def attention(tag, kind, n):
                maps = 1 if kind == "xa" else 2
                npt = 1 if kind == "diff" else maps
                causal = kind in ("diff", "fox")
                q_cols = [(0, 128), (128, 256)] if causal else [(0, 256), (256, 256)]
                scale = 1 / 16 if kind == "xa" else 1 / 8

                def step(ahead, behind, i=None):
                    if behind is not None:
                        u = behind
                        for m in range(npt):
                            act.wait_ge(sem("att_pt"), ATT0[tag]["pt"] + v(u, npt, 0, i) + (m + 1))
                            if u > 0 or i is not None:
                                act.wait_ge(sem("att_o"), ATT0[tag]["o"] + v(u, 1, 0, i))
                            w = 384 if causal else 512
                            act.activation(pT[:, m, 0:w], ps[:, 6 + m, 0:w], ACT.Copy).then_inc(sem("att_pt_read"), 1)
                    if ahead is not None:
                        u, p = ahead, ahead % 2
                        act.wait_ge(sem("att_nb"), ATT0[tag]["nb"] + v(u, 1, 1, i))
                        for m in range(maps):
                            for t in range(NT):
                                c0, n_k = q_cols[t]
                                row = pb[p][:, m, c0:c0 + n_k]
                                act.activation(row, row, ACT.Exp, scale=scale, bias=nb[p][:, 2 * m + t:2 * m + t + 1],
                                               accum_out=sm[p][:, 2 * m + t:2 * m + t + 1]).then_inc(sem("att_ex"), 1)
                    if behind is not None:
                        u, p = behind, behind % 2
                        act.wait_ge(sem("att_o"), ATT0[tag]["o"] + v(u, 1, 1, i))
                        if kind == "diff":
                            act.activation(o_q[:, :], ps[:, p, 0:S], ACT.Square).then_inc(sem("att_sq"), 1)
                            act.wait_ge(sem("att_ms"), ATT0[tag]["ms"] + v(u, 1, 1, i))
                            act.activation(o_r[:, :], ps[:, p, S:2 * S], ACT.Ln, bias=col("eps_rms")).then_inc(sem("att_ln"), 1)
                            act.wait_ge(sem("att_ln"), ATT0[tag]["ln"] + v(u, 1, 1, i))
                            act.activation(o_r[:, :], o_r[:, :], ACT.Exp, scale=-0.5).then_inc(sem("att_or"), 1)
                            act.wait_ge(sem("att_ov"), ATT0[tag]["ov"] + v(u, 1, 1, i))
                            dst, src = aT_hi[:, bass.ds(v(u, 1, 0, i), 1), :], o_v[:, :]
                        elif kind == "xa":
                            dst, src = aT_hi[:, bass.ds(v(u, 2, 0, i), 2), :], ps[:, p, :]
                        else:
                            to = aT_hi if kind == "fox" else yb_hi
                            dst, src = to[:, bass.ds(v(u, 1, 0, i), 1), :], ps[:, p, 0:S]
                        act.activation(dst, src, ACT.Copy).then_inc(sem("att_o_hi"), 1)

                heads(act, step, n)

            def squares(tag, phase, kind):
                act.wait_ge(sem("w_used"), last_unit(phase))
                for t in range(NT):
                    for j in range(4 if kind == "rot" else 2):
                        src = ps[:, bank(phase, j), t * S:(t + 1) * S] if kind == "rot" else ps[:, 4 + 2 * t + j, :]
                        w = S if kind == "rot" else 512
                        act.activation(junk[t][:, j * w:(j + 1) * w], src, ACT.Square, accum_out=ssum[:, t, j:j + 1])\
                           .then_inc(sem("ss_" + tag), 1)

            def row_squares(tag, src, need, value):
                for t in range(NT):
                    act.wait_ge(sem(need), value + 1)
                    act.activation(junk[t][:, :], src[:, t, :], ACT.Square, accum_out=ssq[:, t:t + 1])\
                       .then_inc(sem("sq_" + tag), 1)

            act.dma_start(A["narep"], A["rpb"].to_broadcast([64, A["rpb"].shape[1]])).then_inc(sem("narep"), 16)
            act.wait_ge(sem("ang_red"), 1)
            act.activation(rope_s[:, :], ang[:, :], ACT.Sin).then_inc(sem("rope"), 1)
            act.activation(ang_a[:, :], ang[:, :], ACT.Abs).then_inc(sem("rope"), 1)
            act.wait_ge(sem("rope"), 2)
            act.activation(rope_c[:, :], ang_a[:, :], ACT.Sin, scale=-1.0, bias=col("halfpi")).then_inc(sem("rope"), 1)
            act.wait_ge(sem("lam_dot"), 2)
            act.activation(lam[:, 0:2], lam[:, 0:2], ACT.Exp).then_inc(sem("lam_exp"), 1)
            for b in range(4):
                act.wait_ge(sem("pe_t_x"), b + 1)
                act.activation(aT_hi[:, 2 * b:2 * b + 2, :].rearrange("p a b -> p (a b)"), ps[:, b, :], ACT.Copy)\
                   .then_inc(sem("hi_t_x"), 1)
                if b < 2:
                    convert_hi(act, Unit(b))
            follow("l0_qk")
            follow("l0_v")
            attention("att0", "diff", 8)
            follow("l0_wo")
            act.wait_ge(sem("narep"), 16)
            for h in range(8):
                for r in range(4):
                    src = bass.AP(tensor=A["narep"].tensor, offset=(h * 7 + 3 - r) * 127 + 63,
                                  ap=[[A["rpb"].shape[1] - 1, 64], [127, 4], [1, 64]])
                    act.dma_start(A["nabias"][h, r * 64:(r + 1) * 64, :].rearrange("q (a b) -> q a b", a=4), src)\
                       .then_inc(sem("nabias"), 16)
            gains("t_ln0", col("ln1g")[:, 0:8], col("ln1b")[:, 0:8])
            ffn("ffn0", "f0")
            gains("t_ln1", col("ln2g")[:, 0:8], col("ln2b")[:, 0:8])
            follow("l1_qk")
            follow("l1_v")
            act.wait_ge(sem("fw_loaded"), 32)
            act.activation(fw_hi[:, :, :], fw[:, :, :], ACT.Copy).then_inc(sem("fw_hi"), 1)
            act.wait_ge(sem("f_z"), 1)
            act.activation(f_abs[:, :], f_z[:, :], ACT.Abs).then_inc(sem("f_act"), 1)
            act.wait_ge(sem("f_act"), 1)
            act.activation(f_abs[:, :], f_abs[:, :], ACT.Exp, scale=-1.0).then_inc(sem("f_act"), 1)
            act.wait_ge(sem("f_act"), 2)
            act.activation(f_abs[:, :], f_abs[:, :], ACT.Ln, bias=1.0).then_inc(sem("f_act"), 1)
            for j in range(8):
                act.wait_ge(sem("fox_pe"), j + 1)
                act.activation(fox_c[:, 2 * j:2 * j + 2, :].rearrange("p a b -> p (a b)"), ps[:, 4 + j % 4, :], ACT.Copy)\
                   .then_inc(sem("fox_c"), 1)
            attention("att1", "fox", 8)
            follow("l1_wo")
            gains("t_ln2", col("ln1g")[:, 8:16], col("ln1b")[:, 8:16])
            ffn("ffn1", "f1")
            for layer in range(2):
                act.wait_ge(sem("h_red"), layer + 1)
                act.activation(h_x[:, :], h_k[:, :], ACT.Sin).then_inc(sem("h_sin"), 1)
            for n in range(8):
                o, part, f = n // 4, n // 2 % 2, n % 2
                act.wait_ge(sem("spec_pe"), n + 1)
                act.activation(spec[:, o, part, f, :], ps[:, 6 + f, :], ACT.Copy).then_inc(sem("spec_read"), 1)
            act.wait_ge(sem("h_mix"), 8)
            row_squares("r0", x_tok, "x_new4", 1)
            gains("t_r0", col("ng")[:, 0:8])
            follow("hysc")
            for o in range(2):
                act.wait_ge(sem("zt_pe"), o + 1)
                for t in range(NT):
                    act.activation(z_tok[:, t, :], ps[:, 4 + t, :], ACT.Copy).then_inc(sem("z_tok"), 1)
            follow("naqkv")
            attention("attn", "na", 4)

            def sigmoid_half(j, i):
                c = i * 8 + 2 * j
                act.wait_ge(sem("bank_free"), bank_value("gates", j, i, k=1))
                g = gates[:, bass.ds(c, 2), :]
                act.activation(g, g, ACT.Tanh, scale=0.5).then_inc(sem("gate_t"), 1)

            follow("gates", sigmoid_half)
            for j in range(6):
                next_hi(act, Unit(FIRST["branch"] + j))
            for b in range(4):
                act.wait_ge(sem("m_acc"), 1 + b // 2)
                act.activation(aT_hi[:, 2 * b:2 * b + 2, :], m_acc[:, 2 * b:2 * b + 2, :], ACT.Copy, scale=0.5)\
                   .then_inc(sem("merged_hi"), 1)
            follow("wout")
            act.wait_ge(sem("mem_loaded"), 16)
            for t in range(NT):
                act.activation(junk[t][:, :], mem_tok[:, t, :], ACT.Square, accum_out=mx[0][:, t:t + 1]).then_inc(sem("sq_mem"), 1)
            act.wait_ge(sem("sq_mem"), 2)
            squares("p0", "wout", "rot")
            gains("t_mem", col("memg"))
            follow("xk")
            follow("xv")
            row_squares("r1", x_tok, "x_res0", 1)
            gains("t_r1", col("ng")[:, 16:24])
            follow("xq")
            attention("attx", "xa", 4)
            follow("xo")
            squares("p1", "xo", "rot")
            row_squares("r2", x_tok, "x_res1", 1)
            gains("t_r2", col("ng")[:, 32:40])
            ffn("ffn2", "f2", second=True)
            squares("p2", "ffn2", "fixed")

        @block.vector
        def _(dve):
            def stt(out, in0, scalar, in1, op0, op1):
                return dve.scalar_tensor_tensor(out=out, in0=in0, scalar=scalar, in1=in1, op0=op0, op1=op1)

            chain = [0]

            def link(ins):
                chain[0] += 1
                ins.then_inc(sem("dve_chain"), 1)
                dve.wait_ge(sem("dve_chain"), chain[0])

            def follow(phase, evacuate):
                n, g0 = dict((x[0], x[1]) for x in PHASES)[phase], FIRST[phase]

                def one(u, j, i=None):
                    next_lo(dve, u)
                    dve.wait_ge(sem("w_used"), u.count(1))
                    evacuate(j, i)

                if n >= 8:
                    with dve.Fori(0, n // 4) as i:
                        for j in range(4):
                            one(Unit(g0 + j, i, 4, n // 4), j, i)
                else:
                    for j in range(n):
                        one(Unit(g0 + j), j)

            def no_evacuation(j, i):
                pass

            def qk_out(phase, dst=None):
                def out(j, i):
                    dve.tensor_copy(qkv[:, 2 * j:2 * j + 2, bass.ds(i * S, S)],
                                    ps[:, bank(phase, j), :].rearrange("p (c s) -> p c s", c=2)).then_inc(sem("bank_free"), 1)
                return out

            def v_out(phase, j, pair):
                src = ps[:, bank(phase, j), :].rearrange("p (t h d) -> p t h d", t=NT, h=2)
                for t in range(NT):
                    mm = dve.tensor_copy(qkv[:, 2 * pair:2 * pair + 2, 512 + t * P:512 + (t + 1) * P], src[:, t])
                mm.then_inc(sem("bank_free"), 1)

            def lows(stage, hi, lo):
                for b in range(4):
                    dve.wait_ge(sem("hi_" + stage), b + 1)
                    src = ps[:, b, :].rearrange("p (c s) -> p c s", c=2) if stage == "t_x" else vT[:, 2 * b:2 * b + 2, :]
                    dve.tensor_tensor(lo[:, 2 * b:2 * b + 2, :], src, hi[:, 2 * b:2 * b + 2, :], ALU.subtract)\
                       .then_inc(sem("bank_free"), 1)

            def attention(tag, kind, n):
                maps = 1 if kind == "xa" else 2
                npt = 1 if kind == "diff" else maps
                causal = kind in ("diff", "fox")
                q_cols = [(0, 128), (128, 256)] if causal else [(0, 256), (256, 256)]
                scale = 1 / 16 if kind == "xa" else 1 / 8

                def step(ahead, behind, i=None):
                    if behind is not None:
                        u, p = behind, behind % 2
                        dve.wait_ge(sem("att_ex"), ATT0[tag]["ex"] + v(u, 2 * maps, 0, i) + 2 * maps)
                        dve.reciprocal(rs[p][:, 0:2 * maps], sm[p][:, 0:2 * maps]).then_inc(sem("att_rs"), 1)
                        dve.wait_ge(sem("att_rs"), ATT0[tag]["rs"] + v(u, 1, 1, i))
                        if kind == "diff":
                            dve.tensor_scalar(rs[p][:, 2:4], rs[p][:, 2:4], lam[:, 2:3], None, ALU.mult)\
                               .then_inc(sem("att_rl"), 1)
                            dve.wait_ge(sem("att_rl"), ATT0[tag]["rl"] + v(u, 1, 1, i))
                            for t in range(NT):
                                c0, n_k = q_cols[t]
                                row = pb[p][:, 1, c0:c0 + n_k]
                                dve.tensor_scalar(row, row, rs[p][:, 2 + t:3 + t], None, ALU.mult).then_inc(sem("att_p2"), 1)
                            dve.wait_ge(sem("att_p2"), ATT0[tag]["p2"] + v(u, 2, 0, i) + 2)
                            for t in range(NT):
                                c0, n_k = q_cols[t]
                                row = pb[p][:, 0, c0:c0 + n_k]
                                mm = stt(row, row, rs[p][:, t:t + 1], pb[p][:, 1, c0:c0 + n_k], ALU.mult, ALU.add)
                        else:
                            for m in range(maps):
                                for t in range(NT):
                                    c0, n_k = q_cols[t]
                                    row = pb[p][:, m, c0:c0 + n_k]
                                    mm = dve.tensor_scalar(row, row, rs[p][:, 2 * m + t:2 * m + t + 1], None, ALU.mult)
                        mm.then_inc(sem("att_pn"), 1)
                    if ahead is not None:
                        u, p = ahead, ahead % 2
                        for m in range(maps):
                            if m == 0 and (u > 1 or i is not None):
                                dve.wait_ge(sem("att_pt"), ATT0[tag]["pt"] + v(u, npt, -1, i))
                            scores_made = ATT0[tag]["sc"] + v(u, maps, 0, i) + (m + 1)
                            if i is not None:
                                scores_made = dve.to_reg(scores_made)
                                dve.wait_ge(sem("cst_loaded"), 16)
                            dve.wait_ge(sem("att_sc"), scores_made)
                            for t in range(NT):
                                c0, n_k = q_cols[t]
                                src, to, top = ps[:, 4 + m, c0:c0 + n_k], pb[p][:, m, c0:c0 + n_k], mx[p][:, 2 * m + t:2 * m + t + 1]
                                if kind == "xa":
                                    mm = dve.tensor_scalar(to, src, 1.0, None, ALU.mult, ALU.max, accum_out=top)
                                else:
                                    add = col("cmask")[:, c0:c0 + n_k] if kind == "diff" else mc[p][:, m, c0:c0 + n_k]
                                    mm = dve.tensor_tensor_reduce(out=to, in0=src, in1=add, scale=1.0, scalar=-3e38,
                                                                  op0=ALU.add, op1=ALU.max, accum_out=top)
                                mm.then_inc(sem("att_sc_read"), 1)
                        dve.wait_ge(sem("att_sc_read"), ATT0[tag]["sc_read"] + v(u, 2 * maps, 0, i) + 2 * maps)
                        dve.tensor_scalar(nb[p][:, 0:2 * maps], mx[p][:, 0:2 * maps], -scale, None, ALU.mult)\
                           .then_inc(sem("att_nb"), 1)
                    if behind is not None:
                        u, p = behind, behind % 2
                        if kind == "diff":
                            dve.wait_ge(sem("att_or"), ATT0[tag]["or"] + v(u, 1, 1, i))
                            stt(o_v[:, :], ps[:, p, 0:S], sub_g[:, 0:1], o_r[:, :], ALU.mult, ALU.mult)\
                                .then_inc(sem("att_ov"), 1)
                            src, lo, hi, k = o_v[:, :], aT_lo, aT_hi, 1
                        elif kind == "xa":
                            src, lo, hi, k = ps[:, p, :], aT_lo, aT_hi, 2
                        else:
                            src, lo, hi, k = ps[:, p, 0:S], aT_lo if kind == "fox" else yb_lo, aT_hi if kind == "fox" else yb_hi, 1
                        dve.wait_ge(sem("att_o_hi"), ATT0[tag]["o_hi"] + v(u, 1, 1, i))
                        at_ = bass.ds(v(u, k, 0, i), k)
                        dve.tensor_tensor(lo[:, at_, :], src, hi[:, at_, :], ALU.subtract).then_inc(sem("att_o_read"), 1)

                heads(dve, step, n)

            def statistics(tag):
                for t in range(NT):
                    for h in range(2):
                        mm = dve.bn_stats(stat[:, t, h, :], nrm[:, t, h * 512:(h + 1) * 512])
                link(mm)
                for t in range(NT):
                    mm = dve.bn_aggr(mv[:, t, :], stat[:, t, :, :])
                mm.then_inc(sem("mv_" + tag), 1)

            def layer_norm(tag, phase, kind, x_needed, stage):
                dve.wait_ge(sem("w_used"), last_unit(phase))
                if x_needed:
                    dve.wait_ge(sem(x_needed), 2)
                if kind == "rot":
                    for j in range(4):
                        cs = slice(j * S, (j + 1) * S)
                        mm = stt(nrm[:, :, cs], x_tok[:, :, cs], ALPHA, ps[:, bank(phase, j), :].rearrange("p (t s) -> p t s", t=NT),
                                 ALU.mult, ALU.add).then_inc(sem("bank_free"), 1)
                    dve.wait_ge(sem("bank_free"), BANK0[phase] + 4)
                else:
                    for t in range(NT):
                        for h in range(2):
                            cs = slice(h * 512, (h + 1) * 512)
                            stt(nrm[:, t, cs], x_tok[:, t, cs], ALPHA, ps[:, 4 + 2 * t + h, :], ALU.mult, ALU.add)\
                                .then_inc(sem(tag + "_read"), 1)
                    dve.wait_ge(sem(tag + "_read"), 4)
                statistics(tag)
                dve.wait_ge(sem("rstd_" + tag), 1)
                for t in range(NT):
                    dve.tensor_scalar(nrm[:, t, :], nrm[:, t, :], mv[:, t, 0:1], rstd[:, t:t + 1], ALU.subtract, ALU.mult)\
                       .then_inc(sem("src_" + stage), 1)

            def post_norm(tag, phase, kind, done, n_ss, row_map):
                dve.wait_ge(sem("ss_" + tag), NT * n_ss)
                link(dve.tensor_reduce(ssq[:, :], ssum[:, :, 0:n_ss], AX, ALU.add))
                dve.tensor_copy(ssq[:, :], ssq[:, :]).then_inc(sem("sq_" + tag), 1)
                dve.wait_ge(sem("rstd_" + tag), 1)
                dve.wait_ge(sem("maps_loaded"), 16 * row_map)
                for t in range(NT):
                    for j in range(n_ss):
                        w = D // n_ss
                        cs = slice(j * w, (j + 1) * w)
                        src = ps[:, bank(phase, j), t * S:(t + 1) * S] if kind == "rot" else ps[:, 4 + 2 * t + j, :]
                        mm = stt(nrm[:, t, cs], src, rstd[:, t:t + 1], gmap[:, cs], ALU.mult, ALU.mult)
                        if kind == "rot" and t == 1:
                            mm.then_inc(sem("bank_free"), 1)
                        elif j == n_ss - 1:
                            mm.then_inc(sem(tag + "_t"), 1)
                if kind == "rot":
                    dve.wait_ge(sem("bank_free"), BANK0[phase] + 4)
                else:
                    dve.wait_ge(sem(tag + "_t"), 2)
                for t in range(NT):
                    dve.tensor_tensor(x_tok[:, t, :], x_tok[:, t, :], nrm[:, t, :], ALU.add).then_inc(sem(done), 1)

            def pre_norm(tag, src, stage):
                dve.wait_ge(sem("rstd_" + tag), 1)
                for t in range(NT):
                    dve.tensor_scalar(nrm[:, t, :], src[:, t, :], rstd[:, t:t + 1], None, ALU.mult)\
                       .then_inc(sem("src_" + stage), 1)

            def ffn(phase, tag, second=False):
                g0 = FIRST[phase]
                w = col("conv" + tag[1])
                per = 4 if second else 2

                def hidden(u, k, i=None):
                    q = k % 2
                    K = lambda a, c=0: v(k, a, 0, i) + c
                    gb, ub = bank(phase, 2 * k), bank(phase, 2 * k + 1)
                    cols = 12 if second else 8
                    dve.wait_ge(sem("ffn_fa"), FFN0[tag]["fa"] + K(per, per))
                    if second:
                        for back in (True, False):
                            for c in range(2):
                                for buf, b, o in ((f_a, gb, 0), (f_u, ub, 3)):
                                    at_ = 6 * c + o + (0 if back else 2)
                                    dst = buf[q][:, c, 1:S] if back else buf[q][:, c, 0:S - 1]
                                    src = ps[:, b, c * S:c * S + S - 1] if back else ps[:, b, c * S + 1:c * S + S]
                                    stt(dst, src, w[:, bass.ds(K(cols, at_), 1)], dst, ALU.mult, ALU.add)\
                                        .then_inc(sem("ffn_fc"), 1)
                            if back:
                                dve.wait_ge(sem("ffn_fc"), FFN0[tag]["fc"] + K(8, 4))
                        c1 = math.sqrt(2 / math.pi)
                        dve.wait_ge(sem("ffn_fs"), FFN0[tag]["fs"] + K(1, 1))
                        dve.tensor_scalar(f_t[:, :, :], f_t[:, :, :], 0.044715 * c1, c1, ALU.mult, ALU.add)\
                           .then_inc(sem("bank_free"), 1)
                        dve.wait_ge(sem("bank_free"), bank_value(phase, 2 * k + 1, i))
                        dve.tensor_tensor(f_t[:, :, :], f_t[:, :, :], f_a[q][:, :, :], ALU.mult).then_inc(sem("bank_free"), 1)
                        dve.wait_ge(sem("ffn_ft"), FFN0[tag]["ft"] + K(1, 1))
                        stt(f_t[:, :, :], f_t[:, :, :], 1.0, f_a[q][:, :, :], ALU.add, ALU.mult).then_inc(sem("ffn_fd"), 1)
                        dve.wait_ge(sem("ffn_fd"), FFN0[tag]["fd"] + K(1, 1))
                        stt(f_v[:, :, :], f_t[:, :, :], 0.5, f_u[q][:, :, :], ALU.mult, ALU.mult).then_inc(sem("ffn_fv"), 1)
                    else:
                        for tap in (1, 0):
                            for c in range(2):
                                s = 2 - tap
                                dst = f_a[q][:, c, s:S]
                                stt(dst, ps[:, gb, c * S:c * S + S - s], w[:, bass.ds(K(cols, 4 * c + tap), 1)], dst,
                                    ALU.mult, ALU.add).then_inc(sem("ffn_fc"), 1)
                            if tap:
                                dve.wait_ge(sem("ffn_fc"), FFN0[tag]["fc"] + K(4, 2))
                        dve.wait_ge(sem("ffn_ft"), FFN0[tag]["ft"] + K(1, 1))
                        stt(f_t[:, :, :], f_t[:, :, :], 1.0, f_a[q][:, :, :], ALU.add, ALU.mult).then_inc(sem("bank_free"), 1)
                        dve.wait_ge(sem("bank_free"), bank_value(phase, 2 * k + 1, i))
                        dve.wait_ge(sem("w_used"), u.count(2))
                        stt(f_v[:, :, :], f_t[:, :, :], 0.5, ps[:, ub, :].rearrange("p (c s) -> p c s", c=2), ALU.mult, ALU.mult)\
                            .then_inc(sem("bank_free"), 1)
                    dve.wait_ge(sem("ffn_fh"), FFN0[tag]["fh"] + K(1, 1))
                    dve.tensor_tensor(hT_lo[q][:, :, :], f_v[:, :, :], hT_hi[q][:, :, :], ALU.subtract)\
                       .then_inc(sem("ffn_h"), 1)

                def up(u, k, i=None):
                    next_lo(dve, u)
                    next_lo(dve, u.plus(1))
                    hidden(u, k, i)

                up(Unit(g0), 0)
                up(Unit(g0 + 2), 1)
                next_lo(dve, Unit(g0 + 4))
                trips = (FI - 3) // 2
                with dve.Fori(0, trips) as i:
                    for j in range(2):
                        up(Unit(g0 + 5 + 3 * j, i, 6, trips), 2 + j, i)
                        next_lo(dve, Unit(g0 + 7 + 3 * j, i, 6, trips))
                up(Unit(g0 + 5 + 6 * trips), FI - 1)
                next_lo(dve, Unit(g0 + 7 + 6 * trips))
                next_lo(dve, Unit(g0 + 8 + 6 * trips))

            MAGIC = 1.5 * 2.0 ** 23
            TWO_PI = [6.28125, 0.0019350051879882812, 3.0199159819e-07]
            assert abs(sum(TWO_PI) - 2 * math.pi) < 1e-15

            def reduce_angle(x, k, out):
                link(dve.tensor_scalar(k, x, 1 / (2 * math.pi), MAGIC, ALU.mult, ALU.add))
                link(dve.tensor_scalar(k, k, MAGIC, None, ALU.subtract))
                for part in TWO_PI:
                    link(stt(x, k, -part, x, ALU.mult, ALU.add))
                return dve.tensor_scalar(out, x, 3.1415925, -3.1415925, ALU.min, ALU.max)

            dve.wait_ge(sem("cst_loaded"), 16)
            dve.wait_ge(sem("pos_loaded"), 16)
            link(dve.tensor_scalar(ang[:, :], pos_i[:, :], col("invf"), None, ALU.mult))
            reduce_angle(ang[:, :], ang_k[:, :], ang[:, :]).then_inc(sem("ang_red"), 1)
            dve.wait_ge(sem("lam_loaded"), 16)
            for n in range(2):
                dve.tensor_tensor_reduce(out=lam_j[:, n, :], in0=lam_in[:, 2 * n, :], in1=lam_in[:, 2 * n + 1, :], scale=1.0,
                                         scalar=0.0, op0=ALU.mult, op1=ALU.add, accum_out=lam[:, n:n + 1])\
                   .then_inc(sem("lam_dot"), 1)
            dve.wait_ge(sem("lam_exp"), 1)
            dve.tensor_scalar(lam[:, 2:3], lam[:, 1:2], lam[:, 0:1], -LAMBDA_INIT, ALU.subtract, ALU.add)\
               .then_inc(sem("lam_ready"), 1)
            dve.tensor_scalar(sub_g[:, :], col("subg"), 1.0 - LAMBDA_INIT, None, ALU.mult).then_inc(sem("lam_ready"), 1)
            lows("t_x", aT_hi, aT_lo)
            convert_lo(dve, Unit(0))
            convert_lo(dve, Unit(1))
            follow("l0_qk", qk_out("l0_qk"))
            dve.wait_ge(sem("rope"), 3)

            def v_and_rotation(j, i):
                v_out("l0_v", j, j)
                for h in (2 * j, 2 * j + 1):
                    dve.wait_ge(sem("rot_done"), h + 1)
                    if h:
                        dve.wait_ge(sem("rot_add"), h)
                    dve.tensor_tensor(rot_t[:, :, :], ps[:, 4 + h % 4, :].rearrange("p (a s) -> p a s", a=2),
                                      rope_s[:, None, :].to_broadcast([P, 2, S]), ALU.mult).then_inc(sem("rot_read"), 1)
                    dve.wait_ge(sem("rot_read"), h + 1)
                    dve.wait_ge(sem("rot_cos"), h + 1)
                    both = qkv[:, h, 0:512].rearrange("p (a s) -> p a s", a=2)
                    dve.tensor_tensor(both, both, rot_t[:, :, :], ALU.add).then_inc(sem("rot_add"), 1)

            follow("l0_v", v_and_rotation)
            dve.wait_ge(sem("lam_ready"), 2)
            attention("att0", "diff", 8)
            follow("l0_wo", no_evacuation)
            layer_norm("ln0", "l0_wo", "rot", None, "t_ln0")
            lows("t_ln0", aT_hi, aT_lo)
            ffn("ffn0", "f0")
            layer_norm("ln1", "ffn0", "fixed", "x_new1", "t_ln1")
            lows("t_ln1", aT_hi, aT_lo)
            follow("l1_qk", qk_out("l1_qk"))
            follow("l1_v", lambda j, i: v_out("l1_v", j, j))
            dve.wait_ge(sem("fw_hi"), 1)
            dve.tensor_tensor(fw_lo[:, :, :], fw[:, :, :], fw_hi[:, :, :], ALU.subtract).then_inc(sem("fw_split"), 2)
            dve.wait_ge(sem("f_done"), 1)
            dve.tensor_tensor(f_tok[:, :, :], ps[:, 4, 0:32].rearrange("p (t h) -> p t h", t=NT),
                              f_b[:, None, :].to_broadcast([P, NT, 16]), ALU.add).then_inc(sem("f_tok"), 1)
            dve.wait_ge(sem("f_done"), 2)
            dve.tensor_copy(f_z[:, :], ps[0:16, 5, 0:S]).then_inc(sem("f_z"), 1)
            dve.tensor_scalar(f_min[:, :], ps[0:16, 5, 0:S], 0.0, None, ALU.min).then_inc(sem("f_min"), 1)
            link(dve.memset(f_ones[:, :], 1.0))
            dve.wait_ge(sem("f_min"), 1)
            dve.wait_ge(sem("f_act"), 3)
            link(dve.tensor_tensor(f_min[:, :], f_min[:, :], f_abs[:, :], ALU.subtract))
            link(dve.tensor_tensor_scan(f_cum[:, :], f_ones[:, :], f_min[:, :], 0.0, ALU.mult, ALU.add))
            link(dve.tensor_scalar(f_cum[:, :], f_cum[:, :], -8.0, None, ALU.mult))
            dve.tensor_tensor(fox_d[:, :, :], f_cum[:, None, :].to_broadcast([16, 16, S]),
                              col("eye16")[0:16, :, None].to_broadcast([16, 16, S]), ALU.mult).then_inc(sem("fox_d"), 1)
            attention("att1", "fox", 8)
            follow("l1_wo", no_evacuation)
            layer_norm("ln2", "l1_wo", "rot", "x_new2", "t_ln2")
            lows("t_ln2", aT_hi, aT_lo)
            ffn("ffn1", "f1")
            layer_norm("ln3", "ffn1", "fixed", "x_new3", "t_none")
            dve.wait_ge(sem("hin_loaded"), 16 * 6)
            for layer in range(2):
                dve.wait_ge(sem("h_pe"), layer + 1)
                if layer:
                    dve.wait_ge(sem("h_sin"), 1)
                link(dve.tensor_scalar(h_a[:, :], ps[0:64, 4 + layer, 0:S], col("hb1" if layer == 0 else "hb2")[0:64, :],
                                       col("hf1" if layer == 0 else "hf2")[0:64, :], ALU.add, ALU.mult))
                reduce_angle(h_a[:, :], h_k[:, :], h_k[:, :]).then_inc(sem("h_red"), 1)
            for o in range(2):
                for t in range(NT):
                    n = 2 * o + t
                    dve.wait_ge(sem("h_pe"), 3 + n)
                    if n == 2:
                        dve.wait_ge(sem("spec_pe"), 4)
                    if n:
                        dve.wait_ge(sem("h_mix"), 2 * n)
                    link(dve.tensor_tensor(h_t[:, :], ps[:, 4, :], decay[:, 0, t, :], ALU.mult))
                    link(dve.tensor_tensor(h_u[:, :], ps[:, 5, :], decay[:, 1, t, :], ALU.mult))
                    dve.tensor_tensor(h_s[:, 0, t, :], h_t[:, :], h_u[:, :], ALU.add).then_inc(sem("h_mix"), 1)
                    dve.tensor_tensor(h_s[:, 1, t, :], h_t[:, :], h_u[:, :], ALU.subtract).then_inc(sem("h_mix"), 1)
            dve.wait_ge(sem("h_mix"), 8)
            pre_norm("r0", x_tok, "t_r0")
            lows("t_r0", aT_hi, aT_lo)

            def copy_out(dst, phase, step):
                def out(j, i):
                    at_ = j * step if i is None else i * (4 * step) + j * step
                    dve.tensor_copy(dst[:, bass.ds(at_, step), :], ps[:, bank(phase, j), :].rearrange("p (c s) -> p c s", c=2))\
                       .then_inc(sem("bank_free"), 1)
                return out

            follow("hysc", copy_out(hysc, "hysc", 2))
            dve.wait_ge(sem("bank_free"), BANK0["naqkv"])

            def w3(name, first, tap, n=4):
                t3 = col(name).rearrange("p (k j) -> p k j", j=3)
                return t3[:, first:first + n, tap][:, :, None]

            vv = hysc[:, 0:4, :]
            link(dve.tensor_tensor(cv[0][:, :, :], vv, w3("hyw", 0, 1).to_broadcast([P, 4, S]), ALU.mult))
            link(dve.tensor_tensor(cv[1][:, :, 1:S], vv[:, :, 0:S - 1], w3("hyw", 0, 0).to_broadcast([P, 4, S - 1]), ALU.mult))
            link(dve.tensor_tensor(cv[0][:, :, 1:S], cv[0][:, :, 1:S], cv[1][:, :, 1:S], ALU.add))
            link(dve.tensor_tensor(cv[1][:, :, 0:S - 1], vv[:, :, 1:S], w3("hyw", 0, 2).to_broadcast([P, 4, S - 1]), ALU.mult))
            link(dve.tensor_tensor(vv[:, :, 0:S - 1], cv[0][:, :, 0:S - 1], cv[1][:, :, 0:S - 1], ALU.add))
            dve.tensor_copy(vv[:, :, S - 1:S], cv[0][:, :, S - 1:S]).then_inc(sem("z_ready"), 1)
            dve.wait_ge(sem("z_ready"), 1)
            for o in range(2):
                src = z_s if o else hysc
                dve.wait_ge(sem("zf_pe"), o + 1)
                for f in range(2):
                    zr, zi = ps[:, 4 + f, :], ps[:, 6 + f, :]
                    kr, ki = spec[:, o, 0, f, :], spec[:, o, 1, f, :]
                    if f == 0 and o == 1:
                        dve.wait_ge(sem("yt_pe"), 1)
                    link(dve.tensor_tensor(y_f[:, 0, f, :], zr, kr, ALU.mult))
                    link(dve.tensor_tensor(y_t[:, :], zi, ki, ALU.mult))
                    link(dve.tensor_tensor(y_f[:, 0, f, :], y_f[:, 0, f, :], y_t[:, :], ALU.subtract))
                    link(dve.tensor_tensor(y_f[:, 1, f, :], zr, ki, ALU.mult))
                    link(dve.tensor_tensor(y_t[:, :], zi, kr, ALU.mult))
                    mm = dve.tensor_tensor(y_f[:, 1, f, :], y_f[:, 1, f, :], y_t[:, :], ALU.add)
                    if f == 0:
                        link(mm)
                mm.then_inc(sem("y_f"), 1)
                dve.wait_ge(sem("yt_pe"), o + 1)
                for k in range(4):
                    mm = stt(cv[0][:, k, :], src[:, k, :], col("hyb")[:, 4 * o + k:4 * o + k + 1],
                             ps[:, 4 + k // 2, (k % 2) * S:(k % 2 + 1) * S], ALU.mult, ALU.add)
                link(mm)
                dve.wait_ge(sem("gate_conv"), o + 1)
                if o == 0:
                    dve.tensor_tensor(z_s[:, :, :], cv[0][:, :, :], hysc[:, 4:8, :], ALU.mult).then_inc(sem("z_ready"), 1)
                    dve.wait_ge(sem("z_ready"), 2)
                else:
                    dve.tensor_tensor(cv[1][:, :, :], cv[0][:, :, :], hysc[:, 8:12, :], ALU.mult).then_inc(sem("ya"), 1)
                    dve.wait_ge(sem("ya"), 1)
                    link(dve.tensor_copy(ya_hi[:, :, :], cv[1][:, :, :]))
                    link(dve.tensor_tensor(ya_lo[:, :, :], cv[1][:, :, :], ya_hi[:, :, :], ALU.subtract))

            def na_out(j, i):
                if j < 4:
                    kind, jj = j // 2, j % 2
                    dve.tensor_copy(qkv[:, 2 * jj:2 * jj + 2, kind * S:(kind + 1) * S],
                                    ps[:, bank("naqkv", j), :].rearrange("p (c s) -> p c s", c=2)).then_inc(sem("bank_free"), 1)
                else:
                    v_out("naqkv", j, j - 4)

            follow("naqkv", na_out)
            attention("attn", "na", 4)
            dve.wait_ge(sem("yc_split"), 2)

            def gates_out(j, i):
                c = i * 8 + 2 * j
                dve.tensor_tensor(gates[:, bass.ds(c, 2), :], ps[:, bank("gates", j), :].rearrange("p (c s) -> p c s", c=2),
                                  col("gateb")[:, bass.ds(c, 2)][:, :, None].to_broadcast([P, 2, S]), ALU.add)\
                   .then_inc(sem("bank_free"), 1)

            follow("gates", gates_out)
            dve.wait_ge(sem("gate_t"), 12)
            for j in range(6):
                u, half, br = Unit(FIRST["branch"] + j), j // 3, j % 3
                next_lo(dve, u)
                dve.wait_ge(sem("w_used"), u.count(1))
                for b in range(2):
                    c = 4 * half + 2 * b
                    g = gates[:, 8 * br + c:8 * br + c + 2, :]
                    src = ps[:, bank("branch", 2 * j + b), :].rearrange("p (c s) -> p c s", c=2)
                    acc = m_acc[:, c:c + 2, :]
                    if br == 0:
                        stt(acc, g, 1.0, src, ALU.add, ALU.mult).then_inc(sem("bank_free"), 1)
                    else:
                        stt(m_t[:, :, :], g, 1.0, src, ALU.add, ALU.mult).then_inc(sem("bank_free"), 1)
                        dve.wait_ge(sem("bank_free"), BANK0["branch"] + 2 * j + b + 1)
                        mm = dve.tensor_tensor(acc, acc, m_t[:, :, :], ALU.add)
                        if br == 2 and b == 1:
                            mm.then_inc(sem("m_acc"), 1)
                            dve.wait_ge(sem("m_acc"), half + 1)
                        else:
                            link(mm)
            for b in range(4):
                dve.wait_ge(sem("merged_hi"), b + 1)
                stt(aT_lo[:, 2 * b:2 * b + 2, :], m_acc[:, 2 * b:2 * b + 2, :], 0.5, aT_hi[:, 2 * b:2 * b + 2, :],
                    ALU.mult, ALU.subtract).then_inc(sem("merged"), 1)
            follow("wout", no_evacuation)
            dve.wait_ge(sem("rstd_mem"), 1)
            for t in range(NT):
                dve.tensor_scalar(mem_tok[:, t, :], mem_tok[:, t, :], mx[1][:, t:t + 1], None, ALU.mult)\
                   .then_inc(sem("src_t_mem"), 1)
            post_norm("p0", "wout", "rot", "x_res0", 4, 9)
            lows("t_mem", memT_hi, memT_lo)

            def x_out(at_, phase):
                def out(j, i):
                    dve.tensor_copy(xqkv[:, j, at_:at_ + 512], ps[:, bank(phase, j), :]).then_inc(sem("bank_free"), 1)
                return out

            follow("xk", x_out(512, "xk"))
            follow("xv", x_out(1024, "xv"))
            pre_norm("r1", x_tok, "t_r1")
            lows("t_r1", aT_hi, aT_lo)
            follow("xq", x_out(0, "xq"))
            attention("attx", "xa", 4)
            follow("xo", no_evacuation)
            post_norm("p1", "xo", "rot", "x_res1", 4, 10)
            pre_norm("r2", x_tok, "t_r2")
            lows("t_r2", aT_hi, aT_lo)
            ffn("ffn2", "f2", second=True)
            post_norm("p2", "ffn2", "fixed", "out_ready", 2, 11)

        @block.gpsimd
        def _(pool):
            chain = [0]

            def link(ins):
                chain[0] += 1
                ins.then_inc(sem("pool_chain"), 1)
                pool.wait_ge(sem("pool_chain"), chain[0])

            def load_map(dst, row):
                r = ROWS.index(row)
                pool.dma_start(dst[:, :], A["rows"][r:r + 1, :].to_broadcast([P, D])).then_inc(sem("maps_loaded"), 16)

            def inverse_root(tag, src, eps, scale=1.0, dst=None):
                dst = rstd if dst is None else dst
                link(pool.tensor_scalar(dst[:, 0:NT], src, scale, eps, ALU.mult, ALU.add))
                pool.tensor_tensor(dst[:, 0:NT], dst[:, 0:NT], mhalf[:, :], ALU.pow).then_inc(sem("rstd_" + tag), 1)

            def highs(stage, hi):
                for b in range(4):
                    pool.wait_ge(sem("v_" + stage), 2 * b + 2)
                    pool.tensor_copy(hi[:, 2 * b:2 * b + 2, :], vT[:, 2 * b:2 * b + 2, :]).then_inc(sem("hi_" + stage), 1)

            def layer_norm(tag, stage, n, maps, nxt):
                pool.wait_ge(sem("mv_" + tag), 1)
                inverse_root(tag, mv[:, :, 1], 1e-5)
                if n < 4:
                    highs(stage, aT_hi)
                pool.wait_ge(sem("maps_loaded"), 16 * maps)
                for t in range(NT):
                    pool.wait_ge(sem("src_" + stage), t + 1)
                    link(pool.tensor_tensor(x_tok[:, t, :], nrm[:, t, :], gmap[:, :], ALU.mult))
                    pool.tensor_tensor(x_tok[:, t, :], x_tok[:, t, :], bmap[:, :], ALU.add).then_inc(sem(f"x_new{n}"), 1)
                pool.wait_ge(sem(f"x_new{n}"), 2)
                for dst, row in zip((gmap, bmap), nxt):
                    load_map(dst, row)

            def attention(tag, kind, n):
                maps = 1 if kind == "xa" else 2
                npt = 1 if kind == "diff" else maps

                def step(ahead, behind, i=None):
                    if ahead is None:
                        return
                    u, p = ahead, ahead % 2
                    at_ = v(u, 1, 0, i)
                    if u > 1 or i is not None:
                        pool.wait_ge(sem("att_o"), ATT0[tag]["o"] + v(u, 1, -1, i))
                        if kind in ("fox", "na"):
                            pool.wait_ge(sem("att_sc_read"), ATT0[tag]["sc_read"] + v(u, 2 * maps, -1, i))
                    if kind == "fox":
                        for m in range(2):
                            head = v(u, 2, 0, i) + m
                            c = fox_c[:, bass.ds(head, 1), :].rearrange("p a s -> p (a s)")
                            pool.tensor_tensor(mc[p][:, m, 0:P], col("cmask")[:, 0:P], c[:, 0:P], ALU.add)
                            pool.tensor_tensor(mc[p][:, m, P:384], col("cmask")[:, P:384], c, ALU.add)
                    if kind == "na":
                        pool.dma_start(mc[p][:, :, :].rearrange("p m (t k) -> p (m t) k", t=NT),
                                       A["nabias"].rearrange("h (t q) k -> q (h t) k", q=P)[:, bass.ds(v(u, 4, 0, i), 4), :])\
                            .then_inc(sem(f"bias_in{p}"), 16)
                        pool.wait_ge(sem(f"bias_in{p}"), 16 * (u // 2 + 1))
                        b4 = mc[p][:, :, :].rearrange("p m (t k) -> p (m t) k", t=NT)
                        pool.tensor_scalar(b4, b4, 8.0, 0.0, ALU.mult, ALU.add).then_inc(sem("bias_8"), 1)
                        pool.wait_ge(sem("bias_8"), u + 1)
                        pool.tensor_tensor(b4, b4, col("namask")[:, None, :].to_broadcast([P, 4, S]), ALU.add)
                    if kind == "xa":
                        pool.tensor_copy(st[p][:, :], xqkv[:, bass.ds(at_, 1), :].rearrange("p a s -> p (a s)"))\
                            .then_inc(sem("att_st"), 1)
                    else:
                        pool.tensor_copy(st_d[p][:, :], qkv[:, bass.ds(at_, 1), :].rearrange("p a s -> p (a s)"))\
                            .then_inc(sem("att_st"), 1)

                heads(pool, step, n)

            link(pool.memset(mhalf[:, :], -0.5))
            pool.dma_start(pos_i[:, :], A["positions"].to_broadcast([P, S])).then_inc(sem("pos_loaded"), 16)
            pool.dma_start(lam_in[:, :, :].rearrange("p a b -> p (a b)"), A["lam"].to_broadcast([P, 256]))\
                .then_inc(sem("lam_loaded"), 16)
            load_map(gmap, "ln1g0")
            load_map(bmap, "ln1b0")
            pool.wait_ge(sem("rope"), 3)
            for h in range(8):
                pool.wait_ge(sem("rot_done"), h + 1)
                both = qkv[:, h, 0:512].rearrange("p (a s) -> p a s", a=2)
                pool.tensor_tensor(both, both, rope_c[:, None, :].to_broadcast([P, 2, S]), ALU.mult).then_inc(sem("rot_cos"), 1)
            pool.wait_ge(sem("rot_add"), 8)
            pool.wait_ge(sem("bank_free"), BANK0["l0_wo"])
            attention("att0", "diff", 8)
            layer_norm("ln0", "t_ln0", 1, 2, ["ln2g0", "ln2b0"])
            layer_norm("ln1", "t_ln1", 2, 4, ["ln1g1", "ln1b1"])
            pool.wait_ge(sem("x_new2"), 2)
            pool.dma_start(fw[:, :, :], A["fw"]).then_inc(sem("fw_loaded"), 16)
            pool.dma_start(f_b[:, :], A["fb"].to_broadcast([P, 16])).then_inc(sem("fw_loaded"), 16)
            pool.wait_ge(sem("fox_c"), 8)
            pool.wait_ge(sem("bank_free"), BANK0["l1_wo"])
            attention("att1", "fox", 8)
            layer_norm("ln2", "t_ln2", 3, 6, ["ln2g1", "ln2b1"])
            layer_norm("ln3", "t_none", 4, 8, [])
            for dst, src in ((zembT, "zembT"), (hw1, "hw1"), (hw2, "hw2"), (hw3, "hw3")):
                pool.dma_start(dst[:, :], A[src]).then_inc(sem("hin_loaded"), 16)
            pool.dma_start(decay[:, :, :, :], A["decay"]).then_inc(sem("hin_loaded"), 16)
            pool.dma_start(dft[:, :, :, :], A["dft"]).then_inc(sem("hin_loaded"), 16)
            inverse_wait = sem("sq_r0")
            pool.wait_ge(inverse_wait, 2)
            inverse_root("r0", ssq[:, :], 1e-6, 1 / D)
            highs("t_r0", aT_hi)
            pool.wait_ge(sem("bank_free"), BANK0["naqkv"])

            def short(first, name, w0, src, buf):
                x = src[:, first:first + 4, :]
                t3 = col(name).rearrange("p (k j) -> p k j", j=3)

                def tap(j, n):
                    return t3[:, w0:w0 + 4, j][:, :, None].to_broadcast([P, 4, n])

                a, b = buf
                link(pool.tensor_tensor(a[:, :, :], x, tap(1, S), ALU.mult))
                link(pool.tensor_tensor(b[:, :, 1:S], x[:, :, 0:S - 1], tap(0, S - 1), ALU.mult))
                link(pool.tensor_tensor(a[:, :, 1:S], a[:, :, 1:S], b[:, :, 1:S], ALU.add))
                link(pool.tensor_tensor(b[:, :, 0:S - 1], x[:, :, 1:S], tap(2, S - 1), ALU.mult))
                link(pool.tensor_tensor(x[:, :, 0:S - 1], a[:, :, 0:S - 1], b[:, :, 0:S - 1], ALU.add))
                return pool.tensor_copy(x[:, :, S - 1:S], a[:, :, S - 1:S])

            short(4, "hyw", 4, hysc, cp).then_inc(sem("gate_conv"), 1)
            pool.wait_ge(sem("gate_conv"), 1)
            short(8, "hyw", 8, hysc, cp).then_inc(sem("gate_conv"), 1)
            pool.wait_ge(sem("gate_conv"), 2)
            link(pool.tensor_tensor(hysc[:, 16:20, :], hysc[:, 16:20, :], hysc[:, 20:24, :], ALU.mult))
            link(short(16, "scw", 0, hysc, cp))
            link(pool.tensor_tensor(hysc[:, 16:20, :], hysc[:, 16:20, :], hysc[:, 12:16, :], ALU.mult))
            pool.wait_ge(sem("ya"), 1)
            pool.tensor_copy(yc_hi[:, :, :], hysc[:, 16:20, :]).then_inc(sem("yc_split"), 1)
            pool.wait_ge(sem("yc_split"), 1)
            pool.tensor_tensor(yc_lo[:, :, :], hysc[:, 16:20, :], yc_hi[:, :, :], ALU.subtract).then_inc(sem("yc_split"), 1)
            pool.wait_ge(sem("bank_free"), BANK0["gates"])
            pool.wait_ge(sem("nabias"), 16 * 32)
            load_map(gmap, "ng1")
            attention("attn", "na", 4)
            pool.wait_ge(sem("m_acc"), 2)
            pool.dma_start(mem_tok[:, :, :], A["mem"].rearrange("(t p) d -> p t d", p=P)).then_inc(sem("mem_loaded"), 16)
            pool.wait_ge(sem("sq_mem"), 2)
            inverse_root("mem", mx[0][:, 0:NT], 1e-6, 1 / D, dst=mx[1])
            pool.wait_ge(sem("sq_p0"), 1)
            inverse_root("p0", ssq[:, :], 1e-6, 1 / D)
            highs("t_mem", memT_hi)
            pool.wait_ge(sem("x_res0"), 2)
            load_map(gmap, "ng3")
            pool.wait_ge(sem("sq_r1"), 2)
            inverse_root("r1", ssq[:, :], 1e-6, 1 / D)
            highs("t_r1", aT_hi)
            pool.wait_ge(sem("bank_free"), BANK0["xo"])
            attention("attx", "xa", 4)
            pool.wait_ge(sem("sq_p1"), 1)
            inverse_root("p1", ssq[:, :], 1e-6, 1 / D)
            pool.wait_ge(sem("x_res1"), 2)
            load_map(gmap, "ng5")
            pool.wait_ge(sem("sq_r2"), 2)
            inverse_root("r2", ssq[:, :], 1e-6, 1 / D)
            highs("t_r2", aT_hi)
            pool.wait_ge(sem("sq_p2"), 1)
            inverse_root("p2", ssq[:, :], 1e-6, 1 / D)


def b_units(w):
    n = w.shape[1]
    return w.reshape(KC, P, n // 256, 256).transpose(2, 1, 0, 3).reshape(n // 256, P, UNIT)


def ffn_units(w_in, w_out):
    gate, up = b_units(w_in[:, :DFF]), b_units(w_in[:, DFF:])
    down = w_out.reshape(FI, 2, P, D).transpose(0, 2, 1, 3).reshape(FI, P, UNIT)
    seq = [gate[0], up[0], gate[1], up[1], down[0]]
    for k in range(2, FI):
        seq += [gate[k], up[k], down[k - 1]]
    return np.stack(seq + [down[FI - 1]])


def branch_units(w):
    return w.reshape(3, 4, P, 2, 512).transpose(3, 0, 2, 1, 4).reshape(6, P, UNIT)


def constants():
    f = np.float32
    out = {"ident": np.eye(P, dtype=f), "mean": np.full((P, P), 1 / P, f), "ones16": np.ones((P, P), f),
           "eye16": np.eye(P, 16, dtype=f)}
    rot = np.zeros((P, P), f)
    for base in (0, 64):
        for j in range(8):
            rot[base + j, base + 8 + j] = -1
            rot[base + 8 + j, base + j] = 1
    out["rotT"] = rot.T
    tri = np.where(np.arange(P)[None, :] <= np.arange(P)[:, None], 0, NEG).astype(f)
    out["cmask"] = np.concatenate([tri, np.zeros((P, P), f), tri], 1)
    c = np.arange(64)
    start = np.clip(c - 8, 0, 48)
    win = np.where((c[None, :] >= start[:, None]) & (c[None, :] < start[:, None] + 16), 0, NEG).astype(f)
    out["namask"] = np.tile(win, (2, 4))
    inv = 500000.0 ** (-np.arange(0, 16, 2) / 16)
    invf = np.zeros((P, 1), f)
    for base in (0, 64):
        invf[base:base + 8, 0] = invf[base + 8:base + 16, 0] = inv
    out["invf"] = invf
    out["eps_rms"] = np.full((P, 1), 1e-6, f)
    out["halfpi"] = np.full((P, 1), np.pi / 2, f)
    return out


def fourier():
    j, q = np.arange(S)[:, None], np.arange(S)[None, :] + 0.5
    th = 2 * np.pi * j * q / (2 * S)
    m = [np.cos(th), -np.sin(th), np.cos(th).T / S, -np.sin(th).T / S]
    return np.stack([x.reshape(2, P, S).transpose(1, 0, 2) for x in m], 1).astype(np.float32)


def filter_inputs():
    L = S
    t = np.linspace(0.0, 1.0, L)[:, None]
    w = 2.0 * np.pi * np.arange(L)[:, None] / L
    f = np.linspace(1e-4, 15, 16)[None, :]
    z = np.concatenate([t, np.cos(f * w), -np.sin(f * w)], 1)
    deltas = np.abs(np.linspace(np.log(1e-2) / 1.5, np.log(1e-2) / 0.3, 512))
    dec = np.exp(-t * deltas)
    back = dec.copy()
    back[0] = 0
    d = np.stack([x.reshape(2, P, 512).transpose(1, 0, 2) for x in (dec, back)], 1)
    return np.ascontiguousarray(z.T).astype(np.float32), d.astype(np.float32)


def cols_of(v):
    return v.reshape(-1, P).T


def kernel(**a):
    import concourse.bacc as _bacc
    from concourse import mybir as _mybir
    from concourse.bass_utils import run_bass_kernel_spmd as _run

    a = {k: np.asarray(x) for k, x in a.items()}
    w_in = a["w_in_2"][0]
    hy, na, sc, ga = w_in[:, :1536], w_in[:, 1536:3072], w_in[:, 3072:4608], w_in[:, 4608:]
    fox = a["fox_w_in"][0]
    stream = np.concatenate([
        b_units(a["diff_w_qkv"][0]), b_units(a["diff_w_o"][0]), ffn_units(a["ffn_w_in"][0], a["ffn_w_out"][0]),
        b_units(fox[:, :3072]), b_units(a["fox_w_o"][0]), ffn_units(a["ffn_w_in"][1], a["ffn_w_out"][1]),
        b_units(hy), b_units(sc), b_units(na), b_units(ga), branch_units(a["w_branch_2"][0]), b_units(a["w_out_2"][0]),
        b_units(a["xa_wkv_2"][0]), b_units(a["xa_wq_2"][0]), b_units(a["xa_wo_2"][0]),
        ffn_units(a["ffn_up_2"][0], a["ffn_down_2"][0])])
    assert stream.shape == (NUNITS, P, UNIT)

    con = constants()
    con.update(ln1g=cols_of(a["ln1_g"]), ln1b=cols_of(a["ln1_b"]), ln2g=cols_of(a["ln2_g"]), ln2b=cols_of(a["ln2_b"]),
               ng=cols_of(a["norm_gains_2"][0]), memg=cols_of(a["mem_norm_2"][0]),
               hyw=a["hy_short_w_2"][0].reshape(3, 12, P).transpose(2, 1, 0).reshape(P, 36),
               hyb=cols_of(a["hy_bias_2"][0]), scw=a["sc_conv_w_2"][0].reshape(3, 4, P).transpose(2, 1, 0).reshape(P, 12),
               gateb=cols_of(a["gate_bias_2"][0]), subg=cols_of(a["diff_subln_g"][0]))
    for l in range(2):
        w = np.concatenate([a["ffn_conv_w"][l], a["ffn_conv_b"][l][None]])
        con[f"conv{l}"] = w.reshape(4, 2 * FI, P).transpose(2, 1, 0).reshape(P, 8 * FI)
    w = a["ffn_conv_2"][0].reshape(3, 2, 2 * FI, P)
    con["conv2"] = w.transpose(3, 2, 1, 0).reshape(P, 12 * FI)
    for name, src in (("hb1", a["hy_b1_2"][0]), ("hb2", a["hy_b2_2"][0]), ("hf1", a["hy_freq_2"][0, 0]),
                      ("hf2", a["hy_freq_2"][0, 1])):
        con[name] = np.concatenate([src, np.zeros(64, np.float32)])[:, None]
    cst = np.concatenate([con[n] for n in COLS], 1).astype(np.float32)
    assert cst.shape == (P, NCOLS)

    rows = np.stack([a["ln1_g"][0], a["ln1_b"][0], a["ln2_g"][0], a["ln2_b"][0], a["ln1_g"][1], a["ln1_b"][1],
                     a["ln2_g"][1], a["ln2_b"][1]] + [a["norm_gains_2"][0, n] for n in (1, 3, 5)])
    zembT, decay = filter_inputs()
    arrays = {
        "x": a["x"][0], "positions": a["positions"].reshape(1, S), "mem": a["mem_2"][0], "wstream": stream, "cst": cst,
        "rows": rows,
        "lam": np.concatenate([a["diff_lambda_q1"], a["diff_lambda_k1"], a["diff_lambda_q2"], a["diff_lambda_k2"]], 1),
        "fw": fox[:, 3072:].reshape(KC, P, 16).transpose(1, 0, 2), "fb": a["fox_b_f"],
        "rpb": np.pad(a["na_rpb_2"][0][:, 4:11], ((0, 0), (0, 0), (48, 48))).reshape(1, -1),
        "zembT": zembT, "hw1": a["hy_w1_2"][0], "hw2": a["hy_w2_2"][0], "hw3": a["hy_w3_2"][0], "decay": decay,
        "dft": fourier(),
    }
    arrays = {k: np.ascontiguousarray(x) for k, x in arrays.items()}
    nc = _bacc.Bacc("TRN2", target_bir_lowering=False, num_devices=1)
    A = {k: nc.dram_tensor("in_" + k, x.shape, _mybir.dt.from_np(x.dtype), kind="ExternalInput").ap()
         for k, x in arrays.items()}
    A["narep"] = nc.dram_tensor("narep", (64, arrays["rpb"].shape[1]), F32, kind="Internal").ap()
    A["nabias"] = nc.dram_tensor("nabias", (8, S, S), F32, kind="Internal").ap()
    A["out"] = nc.dram_tensor("out_0", (S, D), F32, kind="ExternalOutput").ap()
    two_blocks_kernel(nc, A)
    r = _run(nc, [{"in_" + k: x for k, x in arrays.items()}], core_ids=[0])
    return r.results[0]["out_0"].reshape(1, S, D)
```

```python
import math
from contextlib import ExitStack

import numpy as np

import concourse.bass as bass
from concourse import mybir

F32 = mybir.dt.float32
F32R = mybir.dt.float32r
ALU = mybir.AluOpType
ACT = mybir.ActivationFunctionType
AX = mybir.AxisListType.X

P = 128
S = 256
NT = S // P
D = 1024
KC = D // P
DFF = 2816
FI = DFF // 256
UNIT = 2048
DEPTH = 2
ALPHA = (2 * DEPTH) ** 0.25
LAMBDA_INIT = 0.8 - 0.6 * math.exp(-0.3 * 0)
NEG = -1e30

PHASES = [("l0_qkv", 12), ("l0_wo", 4), ("ffn0", 3 * FI),
          ("l1_qkv", 12), ("l1_wo", 4), ("ffn1", 3 * FI),
          ("hysc", 12), ("naqkv", 6), ("gates", 12), ("branch", 6), ("wout", 4),
          ("xk", 4), ("xv", 4), ("xq", 4), ("xo", 4), ("ffn2", 3 * FI)]
UNITS = dict(PHASES)
FIRST, _n = {}, 0
for _name, _k in PHASES:
    FIRST[_name] = _n
    _n += _k
NUNITS = _n
RAW, HI, LO = 3, 3, 2
LOOP = 6

BANK_STAGES = [("l0_qkv", 12), ("l0_wo", 4), ("ffn0", 2 * FI),
               ("l1_qkv", 12), ("l1_wo", 4), ("ffn1", 2 * FI),
               ("hysc", 12), ("naqkv", 6), ("gates", 12), ("branch", 12), ("wout", 4),
               ("xk", 4), ("xv", 4), ("xq", 4), ("xo", 4), ("ffn2", 2 * FI)]
BANK0, _n = {}, 0
for _name, _k in BANK_STAGES:
    BANK0[_name] = _n
    _n += _k

NORMS = ["t_ln0", "t_ln1", "t_ln2", "ln3", "t_r0", "t_mem", "t_r1", "t_r2"]
LN_STAGES = ["t_ln0", "t_ln1", "t_ln2"]
T_STAGES = ["t_x", "t_ln0", "t_ln1", "t_ln2", "t_r0", "t_mem", "t_r1", "t_r2"]

QKV_HEADS = [[[("u", 3)], [("u", 4), ("r", 2)]], [[("u", 5), ("r", 3)], []], [[("u", 6)], []],
             [[("u", 7), ("r", 4)], [("u", 8), ("r", 5)]], [[("u", 9)], []], [[("u", 10), ("r", 6)], [("u", 11), ("r", 7)]],
             [[], []], [[], []], [[], []]]
ALONGSIDE = {
    "att0": QKV_HEADS,
    "att1": [[[x for x in part if x[0] == "u"] for part in step] for step in QKV_HEADS],
    "attn": [[[("u", 0)], [("u", 1)]], [[("u", 2)], [("u", 3), ("u", 4)]], [[("u", 5)], [("u", 6), ("u", 7)]],
             [[("u", 8)], [("u", 9), ("u", 10)]], [[("u", 11)], []]],
    "attx": [[[("u", 2)], []], [[("u", 3)], []], [[], []], [[], []], [[], []]],
}

FILTERS_ALONGSIDE = {1: [("layer", 0)], 3: [("layer", 1)], 5: [("taps", 0, 0)], 6: [("taps", 0, 1)],
                     7: [("spectrum", 0, 0)], 8: [("spectrum", 0, 1), ("taps", 1, 0)], 9: [("taps", 1, 1)],
                     10: [("spectrum", 1, 0)], 11: [("spectrum", 1, 1)]}

def counts_before(stages):
    before, total = {}, {}
    for tag, per_step, steps in stages:
        before[tag] = dict(total)
        for name, k in per_step.items():
            total[name] = total.get(name, 0) + k * steps
    for b in before.values():
        for name in total:
            b.setdefault(name, 0)
    return before


def attention_signals(kind):
    maps = 1 if kind == "xa" else 2
    npt = 1 if kind == "diff" else maps
    out = dict(st=1, sc=maps, sc_read=2 * maps, nb=1, ex=2 * maps, rs=1, pn=1, pt=npt, pt_read=npt, o=1, o_hi=1, o_read=1)
    if kind == "diff":
        out.update(rl=1, p2=2, sq=1, ms=1, ln=1, ov=1)
        out["or"] = 1
    return out


ATT0 = counts_before([("att0", attention_signals("diff"), 8), ("att1", attention_signals("fox"), 8),
                      ("attn", attention_signals("na"), 4), ("attx", attention_signals("xa"), 4)])
FFN0 = counts_before([("f0", dict(fa=2, fc=4, ft=1, fh=1, h=1), FI), ("f1", dict(fa=2, fc=4, ft=1, fh=1, h=1), FI),
                      ("f2", dict(fa=2, fb=2, fc=4, fe=4, fs=1, fm=1, ft=1, fd=1, fh=1, h=1), FI)])

COLS, _n = {}, 0
for _name, _k in [("ident", P), ("rotT", P), ("mean", P), ("cmask", 384), ("namask", 256), ("ones16", P), ("eye16", 16),
                  ("ln1g", 16), ("ln1b", 16), ("ln2g", 16), ("ln2b", 16), ("ng", 48), ("memg", 8),
                  ("conv0", FI * 8), ("conv1", FI * 8), ("conv2", FI * 12), ("hyw", 36), ("hyb", 8), ("scw", 12),
                  ("gateb", 24), ("hb1", 1), ("hb2", 1), ("hf1", 1), ("hf2", 1), ("invf", 1), ("subg", 1),
                  ("eps_rms", 1), ("halfpi", 1)]:
    COLS[_name] = (_n, _n + _k)
    _n += _k
NCOLS = _n
ROWS = ["ln1g0", "ln1b0", "ln2g0", "ln2b0", "ln1g1", "ln1b1", "ln2g1", "ln2b1", "ng1", "ng3", "ng5"]


class Unit:

    def __init__(self, g, i=None):
        self.g, self.i = g, i

    def plus(self, k):
        return Unit(self.g + k, self.i)

    def count(self, k=0):
        return self.g + k if self.i is None else self.i * LOOP + (self.g + k)

    @property
    def slot(self):
        return self.g % RAW

    @property
    def loaded(self):
        n = 16 * (self.g // RAW + 1)
        return n if self.i is None else self.i * (16 * LOOP // RAW) + n


def two_blocks_kernel(nc, A):
    ctx = ExitStack()
    with ctx:
        sems = {}

        def sem(name):
            if name not in sems:
                sems[name] = ctx.enter_context(nc.semaphore(name))
            return sems[name]

        at = [16512]

        def region(nbytes):
            r = at[0]
            at[0] += nbytes
            assert at[0] <= 229344, at[0]
            return r

        def place(name, shape, off, dt=F32):
            return nc.alloc_sbuf_tensor_at(name, shape, dt, offset=off)

        KB = 1024
        w_raw = [place(f"w_raw{j}", [P, UNIT], region(8 * KB)) for j in range(RAW)]
        w_hi = [place(f"w_hi{j}", [P, UNIT], region(8 * KB), F32R) for j in range(HI)]
        w_lo = [place(f"w_lo{j}", [P, UNIT], region(8 * KB), F32R) for j in range(LO)]
        x_tok = place("x_tok", [P, NT, D], region(8 * KB))
        scr = region(28 * KB)
        aT_hi = place("aT_hi", [P, KC, S], region(8 * KB), F32R)
        aT_lo = place("aT_lo", [P, KC, S], region(8 * KB), F32R)
        qkv_at = region(24 * KB)
        hysc_at = region(24 * KB)
        yT_at = region(24 * KB)
        maps_at = region(8 * KB)
        cst = place("cst", [P, NCOLS], region((NCOLS * 4 + 31) // 32 * 32))
        small_at = region(2 * KB)

        def col(name, a=0, b=None):
            lo, hi = COLS[name]
            return cst[:, lo + a:hi if b is None else lo + b]

        ident = col("ident")
        qkv = place("qkv", [P, 8, 768], qkv_at)
        xqkv = place("xqkv", [P, 4, 1536], qkv_at)
        hysc = place("hysc", [P, 24, S], hysc_at)
        gates = place("gates", [P, 24, S], hysc_at)
        mem_tok = place("mem_tok", [P, NT, D], qkv_at)
        fox_c = place("fox_c", [P, 16, S], hysc_at)
        fox_d = place("fox_d", [16, 16, S], yT_at)
        ya_hi = place("ya_hi", [P, 4, S], yT_at, F32R)
        ya_lo = place("ya_lo", [P, 4, S], yT_at + 4 * KB, F32R)
        yb_hi = place("yb_hi", [P, 4, S], yT_at + 8 * KB, F32R)
        yb_lo = place("yb_lo", [P, 4, S], yT_at + 12 * KB, F32R)
        yc_hi = place("yc_hi", [P, 4, S], yT_at + 16 * KB, F32R)
        yc_lo = place("yc_lo", [P, 4, S], yT_at + 20 * KB, F32R)
        oT_hi = place("oT_hi", [P, KC, S], yT_at, F32R)
        oT_lo = place("oT_lo", [P, KC, S], yT_at + 8 * KB, F32R)
        memT_hi = place("memT_hi", [P, KC, S], yT_at, F32R)
        memT_lo = place("memT_lo", [P, KC, S], yT_at + 8 * KB, F32R)
        spec = place("spec", [P, 2, 2, 2, 512], yT_at + 8 * KB)
        gmap = place("gmap", [P, D], maps_at)
        bmap = place("bmap", [P, D], maps_at + 4 * KB)
        dft = place("dft", [P, 4, 2, S], maps_at)
        rope_c = place("rope_c", [P, S], small_at)
        rope_s = place("rope_s", [P, S], small_at + KB)

        nrm = place("nrm", [P, NT, D], scr)
        vT = place("vT", [P, KC, S], scr + 8 * KB)
        junk = [place(f"junk{t}", [P, D], scr + (16 + 4 * t) * KB) for t in range(NT)]
        tiny = region(KB)
        stat = place("stat", [P, NT, 4, 6], tiny)
        mv = place("mv", [P, NT, 2], tiny + 192)
        rstd = place("rstd", [P, NT], tiny + 224)
        ssum = place("ssum", [P, NT, 4], tiny + 256)
        ssq = place("ssq", [P, NT], tiny + 320)
        mhalf = place("mhalf", [P, NT], tiny + 384)
        ff = scr + 8 * KB
        f_a = [place(f"f_a{j}", [P, 2, S], ff + 2 * KB * j) for j in range(2)]
        f_u = [place(f"f_u{j}", [P, 2, S], ff + (4 + 2 * j) * KB) for j in range(2)]
        f_t = place("f_t", [P, 2, S], ff + 8 * KB)
        f_v = place("f_v", [P, 2, S], ff + 10 * KB)
        hT_hi = [place(f"hT_hi{j}", [P, 2, S], ff + (12 + 2 * j) * KB, F32R) for j in range(2)]
        hT_lo = [place(f"hT_lo{j}", [P, 2, S], ff + (16 + 2 * j) * KB, F32R) for j in range(2)]
        mc = [place(f"mc{j}", [P, 2, 512], scr + 4 * j * KB) for j in range(2)]
        pb = [place(f"pb{j}", [P, 2, 512], scr + (8 + 4 * j) * KB) for j in range(2)]
        pT = place("pT", [P, 2, 512], scr + 16 * KB)
        o_v = place("o_v", [P, S], scr + 20 * KB)
        o_r = place("o_r", [P, S], scr + 21 * KB)
        o_q = place("o_q", [P, S], scr + 22 * KB)
        mx = [place(f"mx{j}", [P, 4], tiny + 448 + 32 * j) for j in range(2)]
        nb = [place(f"nb{j}", [P, 4], tiny + 576 + 32 * j) for j in range(2)]
        sm = [place(f"sm{j}", [P, 4], tiny + 704 + 32 * j) for j in range(2)]
        rs = [place(f"rs{j}", [P, 4], tiny + 832 + 32 * j) for j in range(2)]
        ang = place("ang", [P, S], scr + 0)
        ang_k = place("ang_k", [P, S], scr + KB)
        ang_a = place("ang_a", [P, S], scr + 2 * KB)
        pos_i = place("pos_i", [P, S], scr + 3 * KB, mybir.dt.int32)
        lam_in = place("lam_in", [P, 4, 64], scr + 4 * KB)
        lam_j = place("lam_j", [P, 2, 64], scr + 5 * KB)
        lam = place("lam", [P, 4], region(32))
        sub_g = place("sub_g", [P, 1], region(32))
        rot_t = place("rot_t", [P, 2, S], scr + 24 * KB)
        fox_at = hysc_at + 16 * KB
        fw = place("fw", [P, KC, 16], fox_at + 0)
        fw_hi = place("fw_hi", [P, KC, 16], fox_at + 512, F32R)
        fw_lo = place("fw_lo", [P, KC, 16], fox_at + 1024, F32R)
        f_b = place("f_b", [P, 16], fox_at + 1536)
        f_tok = place("f_tok", [P, NT, 16], fox_at + 1664)
        f_z = place("f_z", [16, S], fox_at + 2 * KB)
        f_abs = place("f_abs", [16, S], fox_at + 3 * KB)
        f_min = place("f_min", [16, S], fox_at + 4 * KB)
        f_ones = place("f_ones", [16, S], fox_at + 5 * KB)
        f_cum = place("f_cum", [16, S], fox_at + 6 * KB)
        h_t = place("h_t", [P, 512], qkv_at)
        h_u = place("h_u", [P, 512], qkv_at + 2 * KB)
        h_a = place("h_a", [64, S], qkv_at + 4 * KB)
        h_x = place("h_x", [64, S], qkv_at + 5 * KB)
        h_k = place("h_k", [64, S], qkv_at + 6 * KB)
        hw1 = place("hw1", [33, 64], qkv_at + 7 * KB)
        hw2 = place("hw2", [64, 64], qkv_at + 7 * KB + 256)
        hw3 = place("hw3", [64, 2048], qkv_at + 8 * KB)
        h_s = place("h_s", [P, 2, NT, 512], qkv_at + 16 * KB)
        zembT = place("zembT", [33, S], scr + 26 * KB)
        decay = place("decay", [P, 2, NT, 512], yT_at)
        z_tok = place("z_tok", [P, NT, 512], scr + 0)
        y_f = place("y_f", [P, 2, 2, 512], scr + 4 * KB)
        y_t = place("y_t", [P, 512], scr + 12 * KB)
        cv = [place(f"cv{j}", [P, 4, S], scr + (14 + 4 * j) * KB) for j in range(2)]
        cp = [place(f"cp{j}", [P, 4, S], qkv_at + (12 + 4 * j) * KB) for j in range(2)]
        z_s = place("z_s", [P, 4, S], scr + 22 * KB)
        m_acc = place("m_acc", [P, KC, S], scr + 0)
        m_t = place("m_t", [P, 2, S], scr + 8 * KB)

        ps = ctx.enter_context(nc.psum_tensor("ps", [P, 8, 512], F32))

        block = ctx.enter_context(nc.Block())

        def convert_hi(act, u):
            act.wait_ge(sem(f"w_loaded{u.slot}"), u.loaded)
            if u.g >= HI:
                act.wait_ge(sem("w_used"), u.count(1 - HI))
            act.activation(w_hi[u.g % HI][:, :], w_raw[u.slot][:, :], ACT.Copy).then_inc(sem("hi_ready"), 1)

        def convert_lo(dve, u):
            dve.wait_ge(sem("hi_ready"), u.count(1))
            if u.g >= LO:
                dve.wait_ge(sem("w_used"), u.count(1 - LO))
            dve.tensor_tensor(w_lo[u.g % LO][:, :], w_raw[u.slot][:, :], w_hi[u.g % HI][:, :], ALU.subtract)\
               .then_inc(sem("lo_ready"), 1)

        def next_hi(act, u):
            if u.g + HI < NUNITS:
                convert_hi(act, u.plus(HI))

        def next_lo(dve, u):
            if u.g + LO < NUNITS:
                convert_lo(dve, u.plus(LO))

        def run_units(eng, phase, one):
            n, g0 = UNITS[phase], FIRST[phase]
            if n % LOOP == 0 and n > LOOP:
                with eng.Fori(0, n // LOOP) as i:
                    for j in range(LOOP):
                        one(Unit(g0 + j, i), j, i)
            else:
                for j in range(n):
                    one(Unit(g0 + j), j, None)

        def bank(stage, j):
            return j % 2

        def bank_value(stage, j, i=None, body=LOOP, k=0):
            v = BANK0[stage] + j + k
            return v if i is None else i * body + v

        def wait_bank(pe, stage, j, i=None, body=LOOP):
            if BANK0[stage] + j >= 2:
                pe.wait_ge(sem("bank_free"), bank_value(stage, j, i, body, k=-1))

        def t_count(stage, per, k):
            return T_STAGES.index(stage) * per + k

        def projected(tag, kind, head):
            if tag in ("att0", "att1"):
                j = 3 * (head // 2) + (head % 2 if kind == "scores" else 2)
                return BANK0["l0_qkv" if tag == "att0" else "l1_qkv"] + j + 1
            return BANK0["gates"] if tag == "attn" else BANK0["xq"] + head + 1

        def v(u, k, m, i=None):
            return (u + m) * k if i is None else i * (2 * k) + (u + m) * k

        def ffn_iterations(eng, g0, iteration, output_unit):
            iteration(Unit(g0), 0, third=False)
            iteration(Unit(g0 + 2), 1)
            with eng.Fori(0, (FI - 3) // 2) as i:
                iteration(Unit(g0 + 5, i), 2, i)
                iteration(Unit(g0 + 8, i), 3, i)
            iteration(Unit(g0 + 3 * FI - 4), FI - 1)
            output_unit(Unit(g0 + 3 * FI - 1))

        def last_unit(phase):
            return FIRST[phase] + UNITS[phase]

        @block.sync
        def _(sp):
            def load(u):
                if u.g >= RAW:
                    sp.wait_ge(sem("lo_ready"), u.count(1 - RAW))
                src = A["wstream"][u.count()]
                sp.dma_start(w_raw[u.slot][:, :], src).then_inc(sem(f"w_loaded{u.slot}"), 16)

            sp.dma_start(x_tok[:, :, :], A["x"].rearrange("(t p) d -> p t d", p=P)).then_inc(sem("x_loaded"), 16)
            sp.dma_start(cst[:, :], A["cst"]).then_inc(sem("cst_loaded"), 16)
            for name, n in PHASES:
                g0 = FIRST[name]
                if name.startswith("ffn"):
                    for j in range(5):
                        load(Unit(g0 + j))
                    with sp.Fori(0, (n - 9) // LOOP) as i:
                        for j in range(LOOP):
                            load(Unit(g0 + 5 + j, i))
                    for j in range(n - 4, n):
                        load(Unit(g0 + j))
                elif g0 == 0:
                    for j in range(n):
                        load(Unit(j))
                else:
                    run_units(sp, name, lambda u, j, i: load(u))
            for t in range(NT):
                sp.wait_ge(sem("out_ready"), t + 1)
                sp.dma_start(A["out"][t * P:(t + 1) * P, :], x_tok[:, t, :]).then_inc(sem("out_stored"), 16)
            sp.wait_ge(sem("out_stored"), 16 * NT)

        @block.tensor
        def _(pe):
            def three(out, l_hi, l_lo, r_hi, r_lo, start, stop):
                pe.matmul(out, l_hi, r_hi, start=start, stop=False)
                pe.matmul(out, l_hi, r_lo, start=False, stop=False)
                return pe.matmul(out, l_lo, r_hi, start=False, stop=stop)

            def transposes(stage, src):
                for b in range(4):
                    if stage == "t_x":
                        pe.wait_ge(sem("x_loaded"), 16)
                    else:
                        pe.wait_ge(sem("src"), 8 * NORMS.index(stage) + 2 * b + 2)
                    for c in range(2):
                        for t in range(NT):
                            k = 2 * b + c
                            mm = pe.transpose(ps[:, 4 + b, c * S + t * P:c * S + t * P + P],
                                              src[:, t, k * P:(k + 1) * P], ident)
                    mm.then_inc(sem("transposed"), 1)

            def three_ways(hi, lo):
                return (hi[:, :].rearrange("p (k n) -> p k n", k=KC), lo[:, :].rearrange("p (k n) -> p k n", k=KC))

            def fresh_chunk(t_stage, k):
                if t_stage and k % 2 == 0:
                    pe.wait_ge(sem("split"), t_count(t_stage, 4, k // 2 + 1))

            def unit_b(u, stage, j, i=None, a=(aT_hi, aT_lo), t_stage=None, body=LOOP):
                pe.wait_ge(sem("lo_ready"), u.count(1))
                wait_bank(pe, stage, j, i, body)
                hi, lo = three_ways(w_hi[u.g % HI], w_lo[u.g % LO])
                for c in range(2):
                    for k in range(KC):
                        if c == 0:
                            fresh_chunk(t_stage, k)
                        mm = three(ps[:, bank(stage, j), c * S:(c + 1) * S], hi[:, k, c * P:(c + 1) * P],
                                   lo[:, k, c * P:(c + 1) * P], a[0][:, k, :], a[1][:, k, :], k == 0, k == KC - 1)
                mm.then_inc(sem("w_used"), 1)

            def unit_a(u, stage, j, i=None, a=(aT_hi, aT_lo), t_stage=None, body=LOOP):
                pe.wait_ge(sem("lo_ready"), u.count(1))
                wait_bank(pe, stage, j, i, body)
                hi, lo = three_ways(w_hi[u.g % HI], w_lo[u.g % LO])
                for t in range(NT):
                    for k in range(KC):
                        if t == 0:
                            fresh_chunk(t_stage, k)
                        mm = three(ps[:, bank(stage, j), t * S:(t + 1) * S], a[0][:, k, t * P:(t + 1) * P],
                                   a[1][:, k, t * P:(t + 1) * P], hi[:, k, :], lo[:, k, :], k == 0, k == KC - 1)
                mm.then_inc(sem("w_used"), 1)

            def units(stage, unit, a=(aT_hi, aT_lo), t_stage=None):
                run_units(pe, stage, lambda u, j, i: unit(u, stage, j, i, a, t_stage if j == 0 else None))

            def ffn(stage, tag, t_stage):
                g0 = FIRST[stage]

                def up(u, k, i=None):
                    for j in range(2):
                        unit_b(u.plus(j), stage, 2 * k + j, i, t_stage=t_stage if k + j == 0 else None, body=4)

                def down(u, k, first=False, last=False, i=None):
                    pe.wait_ge(sem("lo_ready"), u.count(1))
                    pe.wait_ge(sem("ffn_h"), FFN0[tag]["h"] + (i * 2 if i is not None else 0) + k + 1)
                    hi = w_hi[u.g % HI][:, :].rearrange("p (k n) -> p k n", k=2)
                    lo = w_lo[u.g % LO][:, :].rearrange("p (k n) -> p k n", k=2)
                    q = k % 2
                    for t in range(NT):
                        for h in range(2):
                            for c in range(2):
                                mm = three(ps[:, 4 + 2 * t + h, :], hT_hi[q][:, c, t * P:(t + 1) * P],
                                           hT_lo[q][:, c, t * P:(t + 1) * P], hi[:, c, h * 512:(h + 1) * 512],
                                           lo[:, c, h * 512:(h + 1) * 512], first and c == 0, last and c == 1)
                        if last and t == 0:
                            mm.then_inc(sem("rows_done"), 1)
                    mm.then_inc(sem("w_used"), 1)

                up(Unit(g0), 0)
                up(Unit(g0 + 2), 1)
                down(Unit(g0 + 4), 0, first=True)
                trips = (FI - 3) // 2
                with pe.Fori(0, trips) as i:
                    for j in range(2):
                        up(Unit(g0 + 5 + 3 * j, i), 2 + j, i)
                        down(Unit(g0 + 7 + 3 * j, i), 1 + j, i=i)
                up(Unit(g0 + 5 + 6 * trips), FI - 1)
                down(Unit(g0 + 7 + 6 * trips), FI - 2)
                down(Unit(g0 + 8 + 6 * trips), FI - 1, last=True)

            def attention(tag, kind, n, unit):
                causal = kind in ("diff", "fox")
                maps = 1 if kind == "xa" else 2
                npt = 1 if kind == "diff" else maps
                q_cols = [(0, 128), (128, 256)] if causal else [(0, 256), (256, 256)]
                base = ATT0[tag]
                heads = qkv if kind != "xa" else xqkv

                def scores(u):
                    if kind == "diff":
                        pe.wait_ge(sem("rot_add"), u + 1)
                    else:
                        pe.wait_ge(sem("bank_free"), projected(tag, "scores", u))
                    if u > 0:
                        pe.wait_ge(sem("att_sc_read"), base["sc_read"] + u * 2 * maps)
                    for m in range(maps):
                        for t in range(NT):
                            c0, n_k = q_cols[t]
                            out = ps[:, 4 + m, c0:c0 + n_k]
                            if kind == "xa":
                                for c in range(2):
                                    mm = pe.matmul(out, heads[:, u, c * S + t * P:c * S + t * P + P],
                                                   heads[:, u, 512 + c * S:512 + (c + 1) * S], start=c == 0, stop=c == 1)
                            else:
                                r = slice(64 * m, 64 * m + 64)
                                mm = pe.matmul(out, heads[r, u, t * P:(t + 1) * P], heads[r, u, S:S + n_k], start=True, stop=True)
                        mm.then_inc(sem("att_sc"), 1)

                def transposed(u):
                    pe.wait_ge(sem("att_pn"), base["pn"] + u + 1)
                    if u > 0:
                        pe.wait_ge(sem("att_pt_read"), base["pt_read"] + u * npt)
                    for m in range(npt):
                        for kt in range(NT):
                            for t in range(NT):
                                if causal and kt > t:
                                    continue
                                c0 = q_cols[t][0] + kt * P
                                to = (0 if kt == 0 else S) + (t * P if not (causal and kt == 1) else 0)
                                mm = pe.transpose(ps[:, 6 + m, to:to + P], pb[u % 2][:, m, c0:c0 + P], ident)
                        mm.then_inc(sem("att_pt"), 1)

                def values(u):
                    pe.wait_ge(sem("bank_free"), projected(tag, "values", u))
                    if u > 1:
                        pe.wait_ge(sem("att_o_read"), base["o_read"] + u - 1)
                    ob = ps[:, 2 + u % 2, :]
                    for m in range(npt):
                        pe.wait_ge(sem("att_pt_read"), base["pt_read"] + u * npt + m + 1)
                        if kind == "diff":
                            outs = [(slice(0, P), 0, 2 * S, P, P)]
                        elif kind == "xa":
                            outs = [(slice(0, P), c * S, 1024 + c * P, P, S) for c in range(2)]
                        else:
                            outs = [(slice(64 * m, 64 * m + 64), 0, 2 * S + 64 * m, 64, P)]
                        for rows, o0, v0, width, step in outs:
                            for kt in range(NT):
                                lhs = heads[:, u, v0 + kt * step:v0 + kt * step + width]
                                if kt == 0:
                                    mm = pe.matmul(ob[rows, o0:o0 + S], lhs, pT[:, m, 0:S], start=True, stop=False)
                                elif causal:
                                    mm = pe.matmul(ob[rows, o0 + P:o0 + S], lhs, pT[:, m, S:S + P], start=False, stop=True)
                                else:
                                    mm = pe.matmul(ob[rows, o0:o0 + S], lhs, pT[:, m, S:2 * S], start=False, stop=True)
                    mm.then_inc(sem("att_o"), 1)

                def alongside(part):
                    for what, j in part:
                        if what == "u":
                            unit(j)
                        else:
                            rotate(j)

                for step, (first, second) in enumerate(ALONGSIDE[tag]):
                    if step > 0:
                        transposed(step - 1)
                    if step < n:
                        scores(step)
                    if step > 0:
                        values(step - 1)
                    alongside(first)
                    if step > 0 and kind == "diff":
                        pe.wait_ge(sem("att_sq"), base["sq"] + step)
                        pe.matmul(ps[:, 2 + (step - 1) % 2, S:2 * S], col("mean"), o_q[:, :], start=True, stop=True)\
                          .then_inc(sem("att_ms"), 1)
                    alongside(second)

            def rotate(h):
                pe.wait_ge(sem("bank_free"), projected("att0", "scores", h))
                if h > 0:
                    pe.wait_ge(sem("rot_read"), h)
                pe.matmul(ps[:, 7, :], col("rotT"), qkv[:, h, 0:512], start=True, stop=True).then_inc(sem("rot_done"), 1)

            def qkv_unit(stage, t_stage):
                return lambda j: (unit_a if j % 3 == 2 else unit_b)(Unit(FIRST[stage] + j), stage, j,
                                                                    t_stage=t_stage if j == 0 else None)

            pe.wait_ge(sem("cst_loaded"), 16)
            transposes("t_x", x_tok)
            unit = qkv_unit("l0_qkv", "t_x")
            unit(0)
            unit(1)
            rotate(0)
            unit(2)
            rotate(1)
            attention("att0", "diff", 8, unit)
            pe.wait_ge(sem("att_o_read"), ATT0["att0"]["o_read"] + 8)
            units("l0_wo", unit_a, (oT_hi, oT_lo))
            transposes("t_ln0", nrm)
            ffn("ffn0", "f0", "t_ln0")
            transposes("t_ln1", nrm)
            pe.wait_ge(sem("split"), t_count("t_ln1", 4, 4))
            unit = qkv_unit("l1_qkv", None)
            pe.wait_ge(sem("fw_split"), 1)
            for t in range(NT):
                for k in range(KC):
                    mm = three(ps[:, 4, t * 16:t * 16 + 16], aT_hi[:, k, t * P:(t + 1) * P], aT_lo[:, k, t * P:(t + 1) * P],
                               fw_hi[:, k, :], fw_lo[:, k, :], k == 0, k == KC - 1)
            mm.then_inc(sem("f_done"), 1)
            unit(0)
            pe.wait_ge(sem("f_tok"), 1)
            for t in range(NT):
                mm = pe.transpose(ps[0:16, 5, t * P:(t + 1) * P], f_tok[:, t, :], ident)
            mm.then_inc(sem("f_done"), 1)
            unit(1)
            unit(2)
            pe.wait_ge(sem("fox_d"), 1)
            for j in range(8):
                if j >= 4:
                    pe.wait_ge(sem("fox_c"), j - 3)
                pe.matmul(ps[:, 4 + j % 4, :], col("ones16")[0:16, :],
                          fox_d[:, 2 * j:2 * j + 2, :].rearrange("p a b -> p (a b)"), start=True, stop=True)\
                  .then_inc(sem("fox_pe"), 1)
            pe.wait_ge(sem("fox_c"), 8)
            attention("att1", "fox", 8, unit)
            pe.wait_ge(sem("att_o_read"), ATT0["att1"]["o_read"] + 8)
            units("l1_wo", unit_a, (oT_hi, oT_lo))
            transposes("t_ln2", nrm)
            ffn("ffn1", "f1", "t_ln2")
            def filter_layer(layer):
                if layer == 0:
                    pe.wait_ge(sem("hin_loaded"), 16 * 6)
                    pe.wait_ge(sem("split"), t_count("t_r0", 4, 4))
                    pe.matmul(ps[0:64, 4, 0:S], hw1[:, :], zembT[:, :], start=True, stop=True).then_inc(sem("h_pe"), 1)
                else:
                    pe.wait_ge(sem("h_sin"), 1)
                    pe.matmul(ps[0:64, 5, 0:S], hw2[:, :], h_x[:, :], start=True, stop=True).then_inc(sem("h_pe"), 1)

            def filter_taps(o, t):
                pe.wait_ge(sem("h_sin"), 2)
                if o + t > 0:
                    pe.wait_ge(sem("h_mix"), 2 * (2 * o + t))
                for d in range(2):
                    mm = pe.matmul(ps[:, 4 + d, :], h_x[:, t * P:(t + 1) * P],
                                   hw3[:, (2 * d + o) * 512:(2 * d + o + 1) * 512], start=True, stop=True)
                mm.then_inc(sem("h_pe"), 1)

            def spectrum(o, part):
                pe.wait_ge(sem("h_mix"), 4 * (o + 1))
                for f in range(2):
                    n = 4 * o + 2 * part + f
                    if n >= 2:
                        pe.wait_ge(sem("spec_read"), n - 1)
                    for t in range(NT):
                        mm = pe.matmul(ps[:, 6 + f, :], dft[:, part, t, f * P:(f + 1) * P], h_s[:, part, t, :],
                                       start=t == 0, stop=t == NT - 1)
                    mm.then_inc(sem("spec_pe"), 1)

            transposes("t_r0", nrm)
            for j in range(12):
                unit_b(Unit(FIRST["hysc"] + j), "hysc", j, t_stage="t_r0" if j == 0 else None)
                for what, *args in FILTERS_ALONGSIDE.get(j, []):
                    {"layer": filter_layer, "taps": filter_taps, "spectrum": spectrum}[what](*args)
            def naqkv_unit(j):
                (unit_b if j < 4 else unit_a)(Unit(FIRST["naqkv"] + j), "naqkv", j)

            pe.wait_ge(sem("spec_read"), 8)
            for o in range(2):
                pe.wait_ge(sem("z_ready"), o + 1)
                for k in range(4):
                    for t in range(NT):
                        src = (z_s if o else hysc)[:, k, t * P:(t + 1) * P]
                        mm = pe.transpose(ps[:, 4 + t, k * P:(k + 1) * P], src, ident)
                mm.then_inc(sem("zt_pe"), 1)
                naqkv_unit(3 * o)
                pe.wait_ge(sem("z_tok"), 2 * (o + 1))
                for part in range(2):
                    for f in range(2):
                        for t in range(NT):
                            mm = pe.matmul(ps[:, 4 + 2 * part + f, :], dft[:, part, t, f * P:(f + 1) * P], z_tok[:, t, :],
                                           start=t == 0, stop=t == NT - 1)
                mm.then_inc(sem("zf_pe"), 1)
                naqkv_unit(3 * o + 1)
                pe.wait_ge(sem("y_f"), o + 1)
                for k in range(4):
                    for part in range(2):
                        for f in range(2):
                            mm = pe.matmul(ps[:, 4 + k // 2, (k % 2) * S:(k % 2 + 1) * S],
                                           y_f[:, part, f, k * P:(k + 1) * P], dft[:, 2 + part, f, :],
                                           start=part + f == 0, stop=part + f == 2)
                mm.then_inc(sem("yt_pe"), 1)
                naqkv_unit(3 * o + 2)
            pe.wait_ge(sem("ya"), 1)
            attention("attn", "na", 4, lambda j: unit_b(Unit(FIRST["gates"] + j), "gates", j))
            pe.wait_ge(sem("att_o_read"), ATT0["attn"]["o_read"] + 4)
            pe.wait_ge(sem("yc_split"), 2)
            for j in range(6):
                u, half, br = Unit(FIRST["branch"] + j), j // 3, j % 3
                a_hi, a_lo = [(ya_hi, ya_lo), (yb_hi, yb_lo), (yc_hi, yc_lo)][br]
                pe.wait_ge(sem("lo_ready"), u.count(1))
                hi = w_hi[u.g % HI][:, :].rearrange("p (k n) -> p k n", k=4)
                lo = w_lo[u.g % LO][:, :].rearrange("p (k n) -> p k n", k=4)
                for b in range(2):
                    wait_bank(pe, "branch", 2 * j + b)
                    for c in range(2):
                        m = 2 * b + c
                        for k in range(4):
                            mm = three(ps[:, bank("branch", 2 * j + b), c * S:(c + 1) * S], hi[:, k, m * P:(m + 1) * P],
                                       lo[:, k, m * P:(m + 1) * P], a_hi[:, k, :], a_lo[:, k, :], k == 0, k == 3)
                mm.then_inc(sem("w_used"), 1)
            transposes("t_mem", mem_tok)
            pe.wait_ge(sem("merged"), 4)
            units("wout", unit_a)
            units("xk", unit_b, (memT_hi, memT_lo), t_stage="t_mem")
            for j in range(4):
                if j == 2:
                    transposes("t_r1", nrm)
                unit_a(Unit(FIRST["xv"] + j), "xv", j, a=(memT_hi, memT_lo))
            xq_unit = lambda j: unit_b(Unit(FIRST["xq"] + j), "xq", j, t_stage="t_r1" if j == 0 else None)
            xq_unit(0)
            xq_unit(1)
            attention("attx", "xa", 4, xq_unit)
            pe.wait_ge(sem("att_o_read"), ATT0["attx"]["o_read"] + 4)
            units("xo", unit_a, (oT_hi, oT_lo))
            transposes("t_r2", nrm)
            ffn("ffn2", "f2", "t_r2")

        @block.scalar
        def _(act):
            def follow(phase, extra=None):
                def one(u, j, i):
                    next_hi(act, u)
                    if extra:
                        extra(u, j, i)

                run_units(act, phase, one)

            def gains(stage, g, b=None, hi=aT_hi):
                if b is None:
                    for k in range(KC):
                        act.wait_ge(sem("transposed"), t_count(stage, 4, k // 2 + 1))
                        c = (k % 2) * S
                        act.activation(hi[:, k, :], ps[:, 4 + k // 2, c:c + S], ACT.Identity, scale=g[:, k:k + 1])\
                           .then_inc(sem("split_hi"), 1)
                    return
                ln = LN_STAGES.index(stage)
                for n, hi_banks in ((0, (0,)), (2, (1, 2, 3))):
                    act.wait_ge(sem("transposed"), t_count(stage, 4, n + 1))
                    for k in (n, n + 1):
                        c = (k % 2) * S
                        act.activation(vT[:, n + k, :], ps[:, 4 + n, c:c + S], ACT.Identity, scale=g[:, n + k:n + k + 1],
                                       bias=b[:, n + k:n + k + 1]).then_inc(sem("whole_act"), 1)
                    for bank_ in hi_banks:
                        if bank_ % 2:
                            act.wait_ge(sem("whole_dve"), 4 * ln + bank_ + 1)
                        else:
                            act.wait_ge(sem("whole_act"), 4 * ln + bank_ + 2)
                        both = slice(2 * bank_, 2 * bank_ + 2)
                        act.activation(hi[:, both, :], vT[:, both, :], ACT.Copy).then_inc(sem("split_hi"), 2)

            def ffn(phase, tag, second=False):
                g0 = FIRST[phase]
                w = col("conv" + tag[1])
                cols = 12 if second else 8

                def iteration(u, k, i=None, third=True):
                    q = k % 2
                    K = lambda a, c=0: v(k, a, 0, i) + c
                    gb, ub = bank(phase, 2 * k), bank(phase, 2 * k + 1)
                    act.wait_ge(sem("w_used"), u.count(1))
                    if k >= 2:
                        act.wait_ge(sem("ffn_h"), FFN0[tag]["h"] + K(1, -1))
                    for c in range(2):
                        o = 6 * c if second else 4 * c
                        tap = w[:, bass.ds(K(cols, o + (1 if second else 2)), 1)]
                        off = 0.0 if second else w[:, bass.ds(K(cols, o + 3), 1)]
                        act.activation(f_a[q][:, c, :], ps[:, gb, c * S:(c + 1) * S], ACT.Identity, scale=tap, bias=off)\
                           .then_inc(sem("ffn_fa"), 1)
                    next_hi(act, u)
                    act.wait_ge(sem("ffn_fc"), FFN0[tag]["fc"] + K(4, 4))
                    if k >= 1:
                        act.wait_ge(sem("ffn_h"), FFN0[tag]["h"] + K(1))
                    if second:
                        act.activation(f_t[:, :, :], f_a[q][:, :, :], ACT.Square).then_inc(sem("ffn_fs"), 1)
                        act.wait_ge(sem("w_used"), u.count(2))
                        for c in range(2):
                            tap = w[:, bass.ds(K(cols, 6 * c + 4), 1)]
                            act.activation(f_u[q][:, c, :], ps[:, ub, c * S:(c + 1) * S], ACT.Identity, scale=tap)\
                               .then_inc(sem("ffn_fb"), 1)
                        act.wait_ge(sem("ffn_fm"), FFN0[tag]["fm"] + K(1, 1))
                        act.activation(f_t[:, :, :], f_t[:, :, :], ACT.Tanh).then_inc(sem("ffn_ft"), 1)
                    else:
                        act.activation(f_t[:, :, :], f_a[q][:, :, :], ACT.Tanh, scale=0.5).then_inc(sem("ffn_ft"), 1)
                    next_hi(act, u.plus(1))
                    act.wait_ge(sem("bank_free"), bank_value(phase, 2 * k + 2, i, body=4))
                    act.activation(hT_hi[q][:, :, :], f_v[:, :, :], ACT.Copy).then_inc(sem("ffn_fh"), 1)
                    if third:
                        next_hi(act, u.plus(2))

                ffn_iterations(act, g0, iteration, lambda u: next_hi(act, u))

            def attention(tag, kind, n, unit=None):
                maps = 1 if kind == "xa" else 2
                npt = 1 if kind == "diff" else maps
                causal = kind in ("diff", "fox")
                q_cols = [(0, 128), (128, 256)] if causal else [(0, 256), (256, 256)]
                scale = 1 / 16 if kind == "xa" else 1 / 8
                base = ATT0[tag]
                out_hi = yb_hi if kind == "na" else oT_hi

                def alongside(part):
                    for what, j in part:
                        if what == "u":
                            unit(j)

                for step, (first, second) in enumerate(ALONGSIDE[tag]):
                    u = step - 1
                    if u >= 0:
                        for m in range(npt):
                            act.wait_ge(sem("att_pt"), base["pt"] + u * npt + m + 1)
                            if u > 0:
                                act.wait_ge(sem("att_o"), base["o"] + u)
                            w = 384 if causal else 512
                            act.activation(pT[:, m, 0:w], ps[:, 6 + m, 0:w], ACT.Copy).then_inc(sem("att_pt_read"), 1)
                    if u >= 0 and kind == "diff":
                        act.wait_ge(sem("att_o"), base["o"] + u + 1)
                        act.activation(o_q[:, :], ps[:, 2 + u % 2, 0:S], ACT.Square).then_inc(sem("att_sq"), 1)
                    if step < n:
                        p = step % 2
                        act.wait_ge(sem("att_nb"), base["nb"] + step + 1)
                        for m in range(maps):
                            for t in range(NT):
                                c0, n_k = q_cols[t]
                                row = pb[p][:, m, c0:c0 + n_k]
                                act.activation(row, row, ACT.Exp, scale=scale, bias=nb[p][:, 2 * m + t:2 * m + t + 1],
                                               accum_out=sm[p][:, 2 * m + t:2 * m + t + 1]).then_inc(sem("att_ex"), 1)
                    alongside(first)
                    if u >= 0:
                        ob = ps[:, 2 + u % 2, :]
                        if kind == "diff":
                            act.wait_ge(sem("att_ms"), base["ms"] + u + 1)
                            act.activation(o_r[:, :], ob[:, S:2 * S], ACT.Ln, bias=col("eps_rms")).then_inc(sem("att_ln"), 1)
                            act.wait_ge(sem("att_ln"), base["ln"] + u + 1)
                            act.activation(o_r[:, :], o_r[:, :], ACT.Exp, scale=-0.5).then_inc(sem("att_or"), 1)
                            act.wait_ge(sem("att_ov"), base["ov"] + u + 1)
                            dst, src = out_hi[:, u, :], o_v[:, :]
                        else:
                            act.wait_ge(sem("att_o"), base["o"] + u + 1)
                            if kind == "xa":
                                dst, src = out_hi[:, 2 * u:2 * u + 2, :].rearrange("p a b -> p (a b)"), ob
                            else:
                                dst, src = out_hi[:, u, :], ob[:, 0:S]
                        act.activation(dst, src, ACT.Copy).then_inc(sem("att_o_hi"), 1)
                    alongside(second)

            def plain_unit(phase):
                return lambda j: next_hi(act, Unit(FIRST[phase] + j))

            def unit_squares(u, j, i):
                act.wait_ge(sem("w_used"), u.count(1))
                for t in range(NT):
                    act.activation(junk[t][:, j * S:(j + 1) * S], ps[:, j % 2, t * S:(t + 1) * S], ACT.Square,
                                   accum_out=ssum[:, t, j:j + 1]).then_inc(sem("ss"), 1)

            def row_squares(tag, src, need, value):
                for t in range(NT):
                    act.wait_ge(sem(need), value + t)
                    act.activation(junk[t][:, :], src[:, t, :], ACT.Square, accum_out=ssq[:, t:t + 1])\
                       .then_inc(sem("sq_" + tag), 1)

            act.dma_start(A["narep"], A["rpb"].to_broadcast([64, A["rpb"].shape[1]])).then_inc(sem("narep"), 16)
            act.wait_ge(sem("ang_red"), 1)
            act.activation(rope_s[:, :], ang[:, :], ACT.Sin).then_inc(sem("rope"), 1)
            act.activation(ang_a[:, :], ang[:, :], ACT.Abs).then_inc(sem("rope"), 1)
            act.wait_ge(sem("rope"), 2)
            act.activation(rope_c[:, :], ang_a[:, :], ACT.Sin, scale=-1.0, bias=col("halfpi")).then_inc(sem("rope"), 1)
            act.wait_ge(sem("lam_dot"), 2)
            act.activation(lam[:, 0:2], lam[:, 0:2], ACT.Exp).then_inc(sem("lam_exp"), 1)
            for b in range(4):
                act.wait_ge(sem("transposed"), b + 1)
                act.activation(aT_hi[:, 2 * b:2 * b + 2, :].rearrange("p a b -> p (a b)"), ps[:, 4 + b, :], ACT.Copy)\
                   .then_inc(sem("split_hi"), 2)
                if b < 3:
                    convert_hi(act, Unit(b))
            for j in range(3):
                plain_unit("l0_qkv")(j)
            attention("att0", "diff", 8, plain_unit("l0_qkv"))
            follow("l0_wo")
            act.wait_ge(sem("fw_loaded"), 32)
            act.activation(fw_hi[:, :, :], fw[:, :, :], ACT.Copy).then_inc(sem("fw_hi"), 1)
            act.wait_ge(sem("narep"), 16)
            for h in range(8):
                for r in range(4):
                    src = bass.AP(tensor=A["narep"].tensor, offset=(h * 7 + 3 - r) * 127 + 63,
                                  ap=[[A["rpb"].shape[1] - 1, 64], [127, 4], [1, 64]])
                    act.dma_start(A["nabias"][h, r * 64:(r + 1) * 64, :].rearrange("q (a b) -> q a b", a=4), src)\
                       .then_inc(sem("nabias"), 16)
            gains("t_ln0", col("ln1g")[:, 0:8], col("ln1b")[:, 0:8])
            ffn("ffn0", "f0")
            gains("t_ln1", col("ln2g")[:, 0:8], col("ln2b")[:, 0:8])
            plain_unit("l1_qkv")(0)
            act.wait_ge(sem("f_z"), 1)
            act.activation(f_abs[:, :], f_z[:, :], ACT.Abs).then_inc(sem("f_act"), 1)
            act.wait_ge(sem("f_act"), 1)
            act.activation(f_abs[:, :], f_abs[:, :], ACT.Exp, scale=-1.0).then_inc(sem("f_act"), 1)
            act.wait_ge(sem("f_act"), 2)
            act.activation(f_abs[:, :], f_abs[:, :], ACT.Ln, bias=1.0).then_inc(sem("f_act"), 1)
            plain_unit("l1_qkv")(1)
            plain_unit("l1_qkv")(2)
            for j in range(8):
                act.wait_ge(sem("fox_pe"), j + 1)
                act.activation(fox_c[:, 2 * j:2 * j + 2, :].rearrange("p a b -> p (a b)"), ps[:, 4 + j % 4, :], ACT.Copy)\
                   .then_inc(sem("fox_c"), 1)
            attention("att1", "fox", 8, plain_unit("l1_qkv"))
            follow("l1_wo")
            gains("t_ln2", col("ln1g")[:, 8:16], col("ln1b")[:, 8:16])
            ffn("ffn1", "f1")
            row_squares("r0", x_tok, "x_new4", 1)
            gains("t_r0", col("ng")[:, 0:8])

            def filter_sine(layer):
                act.wait_ge(sem("h_red"), layer + 1)
                act.activation(h_x[:, :], h_k[:, :], ACT.Sin).then_inc(sem("h_sin"), 1)

            def spectrum(o, part):
                for f in range(2):
                    act.wait_ge(sem("spec_pe"), 4 * o + 2 * part + f + 1)
                    act.activation(spec[:, o, part, f, :], ps[:, 6 + f, :], ACT.Copy).then_inc(sem("spec_read"), 1)

            for j in range(12):
                next_hi(act, Unit(FIRST["hysc"] + j))
                for what, *args in FILTERS_ALONGSIDE.get(j, []):
                    if what != "taps":
                        {"layer": filter_sine, "spectrum": spectrum}[what](*args)
            for o in range(2):
                act.wait_ge(sem("zt_pe"), o + 1)
                for t in range(NT):
                    act.activation(z_tok[:, t, :], ps[:, 4 + t, :], ACT.Copy).then_inc(sem("z_tok"), 1)
                for j in range(3 * o, 3 * o + 3):
                    plain_unit("naqkv")(j)

            def gate_unit(j):
                plain_unit("gates")(j)
                act.wait_ge(sem("bank_free"), bank_value("gates", j, k=1))
                g = gates[:, 2 * j:2 * j + 2, :]
                act.activation(g, g, ACT.Tanh, scale=0.5).then_inc(sem("gate_t"), 1)

            attention("attn", "na", 4, gate_unit)
            act.wait_ge(sem("mem_loaded"), 16)
            for t in range(NT):
                act.activation(junk[t][:, :], mem_tok[:, t, :], ACT.Square, accum_out=mx[0][:, t:t + 1]).then_inc(sem("sq_mem"), 1)
            follow("branch")
            for b in range(4):
                act.wait_ge(sem("m_acc"), 1 + b // 2)
                act.activation(aT_hi[:, 2 * b:2 * b + 2, :], m_acc[:, 2 * b:2 * b + 2, :], ACT.Copy, scale=0.5)\
                   .then_inc(sem("merged_hi"), 1)
            gains("t_mem", col("memg"), hi=memT_hi)
            act.wait_ge(sem("sq_mem"), 2)
            follow("wout", unit_squares)
            follow("xk")
            act.wait_ge(sem("ss"), 8)
            row_squares("r1", x_tok, "x_res0", 1)
            plain_unit("xv")(0)
            plain_unit("xv")(1)
            gains("t_r1", col("ng")[:, 16:24])
            plain_unit("xv")(2)
            plain_unit("xv")(3)
            plain_unit("xq")(0)
            plain_unit("xq")(1)
            attention("attx", "xa", 4, plain_unit("xq"))
            follow("xo", unit_squares)
            act.wait_ge(sem("ss"), 16)
            row_squares("r2", x_tok, "x_res1", 1)
            gains("t_r2", col("ng")[:, 32:40])
            ffn("ffn2", "f2", second=True)
            for t in range(NT):
                if t == 0:
                    act.wait_ge(sem("rows_done"), 3)
                else:
                    act.wait_ge(sem("w_used"), NUNITS)
                for h in range(2):
                    act.activation(junk[t][:, h * 512:(h + 1) * 512], ps[:, 4 + 2 * t + h, :], ACT.Square,
                                   accum_out=ssum[:, t, h:h + 1]).then_inc(sem("ss"), 1)

        @block.vector
        def _(dve):
            def stt(out, in0, scalar, in1, op0, op1):
                return dve.scalar_tensor_tensor(out=out, in0=in0, scalar=scalar, in1=in1, op0=op0, op1=op1)

            chain = [0]
            ss_before = [0]

            def link(ins):
                chain[0] += 1
                ins.then_inc(sem("dve_chain"), 1)
                dve.wait_ge(sem("dve_chain"), chain[0])

            def follow(phase, evacuate):
                def one(u, j, i):
                    next_lo(dve, u)
                    dve.wait_ge(sem("w_used"), u.count(1))
                    evacuate(j, i)

                run_units(dve, phase, one)

            def unit_with(phase, evacuate):
                def unit(j):
                    u = Unit(FIRST[phase] + j)
                    next_lo(dve, u)
                    dve.wait_ge(sem("w_used"), u.count(1))
                    evacuate(j, None)
                return unit

            def v_out(phase, j, pair):
                src = ps[:, bank(phase, j), :].rearrange("p (t h d) -> p t h d", t=NT, h=2)
                for t in range(NT):
                    mm = dve.tensor_copy(qkv[:, 2 * pair:2 * pair + 2, 512 + t * P:512 + (t + 1) * P], src[:, t])
                mm.then_inc(sem("bank_free"), 1)

            def qkv_out(phase):
                def out(j, i):
                    if j % 3 == 2:
                        v_out(phase, j, j // 3)
                    else:
                        dve.tensor_copy(qkv[:, 2 * (j // 3) + j % 3, 0:512], ps[:, bank(phase, j), :]).then_inc(sem("bank_free"), 1)
                return out

            def rotate(h):
                dve.wait_ge(sem("rot_done"), h + 1)
                if h:
                    dve.wait_ge(sem("rot_add"), h)
                dve.tensor_tensor(rot_t[:, :, :], ps[:, 7, :].rearrange("p (a s) -> p a s", a=2),
                                  rope_s[:, None, :].to_broadcast([P, 2, S]), ALU.mult).then_inc(sem("rot_read"), 1)
                dve.wait_ge(sem("rot_read"), h + 1)
                dve.wait_ge(sem("rot_cos"), h + 1)
                both = qkv[:, h, 0:512].rearrange("p (a s) -> p a s", a=2)
                dve.tensor_tensor(both, both, rot_t[:, :, :], ALU.add).then_inc(sem("rot_add"), 1)

            def lows(stage, lo=aT_lo, hi=aT_hi, g=None, offset=None):
                def whole(b):
                    dve.wait_ge(sem("transposed"), t_count(stage, 4, b + 1))
                    for k in (2 * b, 2 * b + 1):
                        c = (k % 2) * S
                        dve.tensor_scalar(vT[:, k, :], ps[:, 4 + b, c:c + S], g[:, k:k + 1], offset[:, k:k + 1], ALU.mult, ALU.add)\
                           .then_inc(sem("whole_dve"), 1)

                for b in range(4):
                    if offset is not None and b % 2 == 0:
                        whole(b + 1)
                    dve.wait_ge(sem("split_hi"), t_count(stage, 8, 2 * b + 2))
                    both = slice(2 * b, 2 * b + 2)
                    if offset is not None:
                        dve.tensor_tensor(lo[:, both, :], vT[:, both, :], hi[:, both, :], ALU.subtract).then_inc(sem("split"), 1)
                    elif g is None:
                        dve.tensor_tensor(lo[:, both, :], ps[:, 4 + b, :].rearrange("p (c s) -> p c s", c=2), hi[:, both, :],
                                          ALU.subtract).then_inc(sem("split"), 1)
                    else:
                        for k in (2 * b, 2 * b + 1):
                            c = (k % 2) * S
                            mm = stt(lo[:, k, :], ps[:, 4 + b, c:c + S], g[:, k:k + 1], hi[:, k, :], ALU.mult, ALU.subtract)
                        mm.then_inc(sem("split"), 1)

            def attention(tag, kind, n, unit):
                maps = 1 if kind == "xa" else 2
                npt = 1 if kind == "diff" else maps
                causal = kind in ("diff", "fox")
                q_cols = [(0, 128), (128, 256)] if causal else [(0, 256), (256, 256)]
                scale = 1 / 16 if kind == "xa" else 1 / 8
                base = ATT0[tag]
                out_hi, out_lo = (yb_hi, yb_lo) if kind == "na" else (oT_hi, oT_lo)

                def maxima(u):
                    p = u % 2
                    if u > 1:
                        dve.wait_ge(sem("att_pt"), base["pt"] + (u - 1) * npt)
                    for m in range(maps):
                        dve.wait_ge(sem("att_sc"), base["sc"] + u * maps + m + 1)
                        if kind in ("fox", "na") and m == 0:
                            dve.wait_ge(sem("mask_ready"), (0 if kind == "fox" else 8) + u + 1)
                        for t in range(NT):
                            c0, n_k = q_cols[t]
                            src, to, top = ps[:, 4 + m, c0:c0 + n_k], pb[p][:, m, c0:c0 + n_k], mx[p][:, 2 * m + t:2 * m + t + 1]
                            if kind == "xa":
                                mm = dve.tensor_scalar(to, src, 1.0, None, ALU.mult, ALU.max, accum_out=top)
                            else:
                                add = col("cmask")[:, c0:c0 + n_k] if kind == "diff" else mc[p][:, m, c0:c0 + n_k]
                                mm = dve.tensor_tensor_reduce(out=to, in0=src, in1=add, scale=1.0, scalar=-3e38,
                                                              op0=ALU.add, op1=ALU.max, accum_out=top)
                            mm.then_inc(sem("att_sc_read"), 1)
                    dve.wait_ge(sem("att_sc_read"), base["sc_read"] + (u + 1) * 2 * maps)
                    dve.tensor_scalar(nb[p][:, 0:2 * maps], mx[p][:, 0:2 * maps], -scale, None, ALU.mult)\
                       .then_inc(sem("att_nb"), 1)

                def normalise_rows(u):
                    p = u % 2
                    dve.wait_ge(sem("att_ex"), base["ex"] + (u + 1) * 2 * maps)
                    dve.reciprocal(rs[p][:, 0:2 * maps], sm[p][:, 0:2 * maps]).then_inc(sem("att_rs"), 1)
                    dve.wait_ge(sem("att_rs"), base["rs"] + u + 1)
                    if kind == "diff":
                        dve.tensor_scalar(rs[p][:, 2:4], rs[p][:, 2:4], lam[:, 2:3], None, ALU.mult)\
                           .then_inc(sem("att_rl"), 1)
                        dve.wait_ge(sem("att_rl"), base["rl"] + u + 1)
                        for t in range(NT):
                            c0, n_k = q_cols[t]
                            row = pb[p][:, 1, c0:c0 + n_k]
                            dve.tensor_scalar(row, row, rs[p][:, 2 + t:3 + t], None, ALU.mult).then_inc(sem("att_p2"), 1)
                        dve.wait_ge(sem("att_p2"), base["p2"] + 2 * u + 2)
                        for t in range(NT):
                            c0, n_k = q_cols[t]
                            row = pb[p][:, 0, c0:c0 + n_k]
                            mm = stt(row, row, rs[p][:, t:t + 1], pb[p][:, 1, c0:c0 + n_k], ALU.mult, ALU.add)
                    else:
                        for m in range(maps):
                            for t in range(NT):
                                c0, n_k = q_cols[t]
                                row = pb[p][:, m, c0:c0 + n_k]
                                mm = dve.tensor_scalar(row, row, rs[p][:, 2 * m + t:2 * m + t + 1], None, ALU.mult)
                    mm.then_inc(sem("att_pn"), 1)

                def outputs(u):
                    ob = ps[:, 2 + u % 2, :]
                    if kind == "diff":
                        dve.wait_ge(sem("att_or"), base["or"] + u + 1)
                        if u:
                            dve.wait_ge(sem("att_o_read"), base["o_read"] + u)
                        stt(o_v[:, :], ob[:, 0:S], sub_g[:, 0:1], o_r[:, :], ALU.mult, ALU.mult).then_inc(sem("att_ov"), 1)
                        src = o_v[:, :]
                    elif kind != "xa":
                        src = ob[:, 0:S]
                    dve.wait_ge(sem("att_o_hi"), base["o_hi"] + u + 1)
                    if kind == "xa":
                        to = slice(2 * u, 2 * u + 2)
                        dve.tensor_tensor(out_lo[:, to, :], ob.rearrange("p (a b) -> p a b", a=2), out_hi[:, to, :], ALU.subtract)\
                           .then_inc(sem("att_o_read"), 1)
                    else:
                        dve.tensor_tensor(out_lo[:, u, :], src, out_hi[:, u, :], ALU.subtract).then_inc(sem("att_o_read"), 1)

                def alongside(part):
                    for what, j in part:
                        if what == "u":
                            unit(j)
                        else:
                            rotate(j)

                for step, (first, second) in enumerate(ALONGSIDE[tag]):
                    if step < n:
                        maxima(step)
                        normalise_rows(step)
                    alongside(first)
                    if step > 0:
                        outputs(step - 1)
                    alongside(second)

            def statistics(t, h):
                return dve.bn_stats(stat[:, t, h, :], nrm[:, t, h * S:(h + 1) * S])

            def residual(j, i):
                cs = slice(j * S, (j + 1) * S)
                link(stt(nrm[:, :, cs], x_tok[:, :, cs], ALPHA, ps[:, j % 2, :].rearrange("p (t s) -> p t s", t=NT),
                         ALU.mult, ALU.add))
                statistics(0, j)
                statistics(1, j).then_inc(sem("bank_free"), 1)

            def residual_ffn(n):
                for t in range(NT):
                    if t == 0:
                        dve.wait_ge(sem("rows_done"), n + 1)
                    else:
                        dve.wait_ge(sem("w_used"), last_unit(f"ffn{n}"))
                    for h in range(2):
                        cs = slice(h * 512, (h + 1) * 512)
                        mm = stt(nrm[:, t, cs], x_tok[:, t, cs], ALPHA, ps[:, 4 + 2 * t + h, :], ALU.mult, ALU.add)
                    link(mm)
                    for h in range(4):
                        mm = statistics(t, h)
                mm.then_inc(sem("acc_read"), 1)

            def normalise(src, mean):
                for b in range(4):
                    cs = slice(b * S, (b + 1) * S)
                    for t in range(NT):
                        if mean:
                            mm = dve.tensor_scalar(nrm[:, t, cs], src[:, t, cs], mv[:, t, 0:1], rstd[:, t:t + 1], ALU.subtract, ALU.mult)
                        else:
                            mm = dve.tensor_scalar(nrm[:, t, cs], src[:, t, cs], rstd[:, t:t + 1], None, ALU.mult)
                        mm.then_inc(sem("src"), 1)

            def layer_norm(tag, needed):
                dve.wait_ge(*needed)
                for t in range(NT):
                    mm = dve.bn_aggr(mv[:, t, :], stat[:, t, :, :])
                mm.then_inc(sem("mv"), 1)
                dve.wait_ge(sem("rstd_" + tag), 1)
                normalise(nrm, True)

            def scaled(j, i):
                cs = slice(j * S, (j + 1) * S)
                dve.wait_ge(sem("ss"), ss_before[0] + 2 * j + 2)
                dve.tensor_tensor(nrm[:, :, cs], ps[:, j % 2, :].rearrange("p (t s) -> p t s", t=NT),
                                  gmap[:, None, cs].to_broadcast([P, NT, S]), ALU.mult).then_inc(sem("bank_free"), 1)

            def post_norm(tag, done, n_ss, needed):
                link(dve.tensor_reduce(ssq[:, :], ssum[:, :, 0:n_ss], AX, ALU.add))
                dve.tensor_copy(ssq[:, :], ssq[:, :]).then_inc(sem("sq_" + tag), 1)
                dve.wait_ge(sem("rstd_" + tag), 1)
                dve.wait_ge(*needed)
                for t in range(NT):
                    stt(x_tok[:, t, :], nrm[:, t, :], rstd[:, t:t + 1], x_tok[:, t, :], ALU.mult, ALU.add).then_inc(sem(done), 1)

            def pre_norm(tag):
                dve.wait_ge(sem("rstd_" + tag), 1)
                normalise(x_tok, False)

            def ffn(phase, tag, second=False):
                g0 = FIRST[phase]
                w = col("conv" + tag[1])
                cols = 12 if second else 8

                def iteration(u, k, i=None, third=True):
                    q = k % 2
                    K = lambda a, c=0: v(k, a, 0, i) + c
                    gb, ub = bank(phase, 2 * k), bank(phase, 2 * k + 1)

                    def side_taps(buf, b, at_, signal):
                        for back in (True, False):
                            for c in range(2):
                                tap = w[:, bass.ds(K(cols, 6 * c + at_ + (0 if back else 2)), 1)]
                                dst = buf[q][:, c, 1:S] if back else buf[q][:, c, 0:S - 1]
                                src = ps[:, b, c * S:c * S + S - 1] if back else ps[:, b, c * S + 1:c * S + S]
                                stt(dst, src, tap, dst, ALU.mult, ALU.add).then_inc(sem("ffn_" + signal), 1)
                            if back:
                                dve.wait_ge(sem("ffn_" + signal), FFN0[tag][signal] + K(4, 2))

                    next_lo(dve, u)
                    dve.wait_ge(sem("ffn_fa"), FFN0[tag]["fa"] + K(2, 2))
                    if second:
                        side_taps(f_a, gb, 0, "fc")
                        c1 = math.sqrt(2 / math.pi)
                        dve.wait_ge(sem("ffn_fs"), FFN0[tag]["fs"] + K(1, 1))
                        dve.tensor_scalar(f_t[:, :, :], f_t[:, :, :], 0.044715 * c1, c1, ALU.mult, ALU.add)\
                           .then_inc(sem("bank_free"), 1)
                        dve.wait_ge(sem("bank_free"), bank_value(phase, 2 * k + 1, i, body=4))
                        dve.tensor_tensor(f_t[:, :, :], f_t[:, :, :], f_a[q][:, :, :], ALU.mult).then_inc(sem("ffn_fm"), 1)
                        next_lo(dve, u.plus(1))
                        dve.wait_ge(sem("ffn_fb"), FFN0[tag]["fb"] + K(2, 2))
                        side_taps(f_u, ub, 3, "fe")
                        dve.wait_ge(sem("ffn_ft"), FFN0[tag]["ft"] + K(1, 1))
                        stt(f_t[:, :, :], f_t[:, :, :], 1.0, f_a[q][:, :, :], ALU.add, ALU.mult).then_inc(sem("ffn_fd"), 1)
                        dve.wait_ge(sem("ffn_fd"), FFN0[tag]["fd"] + K(1, 1))
                        stt(f_v[:, :, :], f_t[:, :, :], 0.5, f_u[q][:, :, :], ALU.mult, ALU.mult).then_inc(sem("bank_free"), 1)
                    else:
                        for tap in (1, 0):
                            for c in range(2):
                                back = 2 - tap
                                dst = f_a[q][:, c, back:S]
                                stt(dst, ps[:, gb, c * S:c * S + S - back], w[:, bass.ds(K(cols, 4 * c + tap), 1)], dst,
                                    ALU.mult, ALU.add).then_inc(sem("ffn_fc"), 1)
                            if tap:
                                dve.wait_ge(sem("ffn_fc"), FFN0[tag]["fc"] + K(4, 2))
                        next_lo(dve, u.plus(1))
                        dve.wait_ge(sem("ffn_ft"), FFN0[tag]["ft"] + K(1, 1))
                        stt(f_t[:, :, :], f_t[:, :, :], 1.0, f_a[q][:, :, :], ALU.add, ALU.mult).then_inc(sem("bank_free"), 1)
                        dve.wait_ge(sem("bank_free"), bank_value(phase, 2 * k + 1, i, body=4))
                        dve.wait_ge(sem("w_used"), u.count(2))
                        stt(f_v[:, :, :], f_t[:, :, :], 0.5, ps[:, ub, :].rearrange("p (c s) -> p c s", c=2), ALU.mult, ALU.mult)\
                            .then_inc(sem("bank_free"), 1)
                    dve.wait_ge(sem("ffn_fh"), FFN0[tag]["fh"] + K(1, 1))
                    dve.tensor_tensor(hT_lo[q][:, :, :], f_v[:, :, :], hT_hi[q][:, :, :], ALU.subtract)\
                       .then_inc(sem("ffn_h"), 1)
                    if third:
                        next_lo(dve, u.plus(2))

                ffn_iterations(dve, g0, iteration, lambda u: next_lo(dve, u))

            MAGIC = 1.5 * 2.0 ** 23
            TWO_PI = [6.28125, 0.0019350051879882812, 3.0199159819e-07]
            assert abs(sum(TWO_PI) - 2 * math.pi) < 1e-15

            def reduce_angle(x, k, out):
                link(dve.tensor_scalar(k, x, 1 / (2 * math.pi), MAGIC, ALU.mult, ALU.add))
                link(dve.tensor_scalar(k, k, MAGIC, None, ALU.subtract))
                for part in TWO_PI:
                    link(stt(x, k, -part, x, ALU.mult, ALU.add))
                return dve.tensor_scalar(out, x, 3.1415925, -3.1415925, ALU.min, ALU.max)

            dve.wait_ge(sem("cst_loaded"), 16)
            dve.wait_ge(sem("pos_loaded"), 16)
            link(dve.tensor_scalar(ang[:, :], pos_i[:, :], col("invf"), None, ALU.mult))
            reduce_angle(ang[:, :], ang_k[:, :], ang[:, :]).then_inc(sem("ang_red"), 1)
            dve.wait_ge(sem("lam_loaded"), 16)
            for n in range(2):
                dve.tensor_tensor_reduce(out=lam_j[:, n, :], in0=lam_in[:, 2 * n, :], in1=lam_in[:, 2 * n + 1, :], scale=1.0,
                                         scalar=0.0, op0=ALU.mult, op1=ALU.add, accum_out=lam[:, n:n + 1])\
                   .then_inc(sem("lam_dot"), 1)
            dve.wait_ge(sem("lam_exp"), 1)
            dve.tensor_scalar(lam[:, 2:3], lam[:, 1:2], lam[:, 0:1], -LAMBDA_INIT, ALU.subtract, ALU.add)\
               .then_inc(sem("lam_ready"), 1)
            dve.tensor_scalar(sub_g[:, :], col("subg"), 1.0 - LAMBDA_INIT, None, ALU.mult).then_inc(sem("lam_ready"), 1)
            lows("t_x")
            convert_lo(dve, Unit(0))
            convert_lo(dve, Unit(1))
            unit = unit_with("l0_qkv", qkv_out("l0_qkv"))
            unit(0)
            unit(1)
            dve.wait_ge(sem("rope"), 3)
            rotate(0)
            unit(2)
            rotate(1)
            dve.wait_ge(sem("lam_ready"), 2)
            attention("att0", "diff", 8, unit)
            follow("l0_wo", residual)
            dve.wait_ge(sem("fw_hi"), 1)
            dve.tensor_tensor(fw_lo[:, :, :], fw[:, :, :], fw_hi[:, :, :], ALU.subtract).then_inc(sem("fw_split"), 1)
            layer_norm("ln0", (sem("bank_free"), BANK0["ffn0"]))
            lows("t_ln0", g=col("ln1g")[:, 0:8], offset=col("ln1b")[:, 0:8])
            ffn("ffn0", "f0")
            dve.wait_ge(sem("x_new1"), 2)
            residual_ffn(0)
            layer_norm("ln1", (sem("acc_read"), 1))
            lows("t_ln1", g=col("ln2g")[:, 0:8], offset=col("ln2b")[:, 0:8])
            unit = unit_with("l1_qkv", qkv_out("l1_qkv"))
            dve.wait_ge(sem("f_done"), 1)
            dve.tensor_tensor(f_tok[:, :, :], ps[:, 4, 0:32].rearrange("p (t h) -> p t h", t=NT),
                              f_b[:, None, :].to_broadcast([P, NT, 16]), ALU.add).then_inc(sem("f_tok"), 1)
            unit(0)
            dve.wait_ge(sem("f_done"), 2)
            dve.tensor_copy(f_z[:, :], ps[0:16, 5, 0:S]).then_inc(sem("f_z"), 1)
            dve.tensor_scalar(f_min[:, :], ps[0:16, 5, 0:S], 0.0, None, ALU.min).then_inc(sem("f_min"), 1)
            link(dve.memset(f_ones[:, :], 1.0))
            dve.wait_ge(sem("f_min"), 1)
            dve.wait_ge(sem("f_act"), 3)
            link(dve.tensor_tensor(f_min[:, :], f_min[:, :], f_abs[:, :], ALU.subtract))
            link(dve.tensor_tensor_scan(f_cum[:, :], f_ones[:, :], f_min[:, :], 0.0, ALU.mult, ALU.add))
            link(dve.tensor_scalar(f_cum[:, :], f_cum[:, :], -8.0, None, ALU.mult))
            dve.tensor_tensor(fox_d[:, :, :], f_cum[:, None, :].to_broadcast([16, 16, S]),
                              col("eye16")[0:16, :, None].to_broadcast([16, 16, S]), ALU.mult).then_inc(sem("fox_d"), 1)
            unit(1)
            unit(2)
            attention("att1", "fox", 8, unit)
            dve.wait_ge(sem("x_new2"), 2)
            follow("l1_wo", residual)
            layer_norm("ln2", (sem("bank_free"), BANK0["ffn1"]))
            lows("t_ln2", g=col("ln1g")[:, 8:16], offset=col("ln1b")[:, 8:16])
            ffn("ffn1", "f1")
            dve.wait_ge(sem("x_new3"), 2)
            residual_ffn(1)
            layer_norm("ln3", (sem("acc_read"), 2))
            pre_norm("r0")
            lows("t_r0", g=col("ng")[:, 0:8])
            dve.wait_ge(sem("hin_loaded"), 16 * 6)

            def filter_layer(layer):
                dve.wait_ge(sem("h_pe"), layer + 1)
                link(dve.tensor_scalar(h_a[:, :], ps[0:64, 4 + layer, 0:S], col("hb1" if layer == 0 else "hb2")[0:64, :],
                                       col("hf1" if layer == 0 else "hf2")[0:64, :], ALU.add, ALU.mult))
                if layer:
                    dve.wait_ge(sem("h_sin"), 1)
                reduce_angle(h_a[:, :], h_k[:, :], h_k[:, :]).then_inc(sem("h_red"), 1)

            def filter_taps(o, t):
                n = 2 * o + t
                dve.wait_ge(sem("h_pe"), 3 + n)
                if n == 2:
                    dve.wait_ge(sem("spec_pe"), 4)
                if n:
                    dve.wait_ge(sem("h_mix"), 2 * n)
                link(dve.tensor_tensor(h_t[:, :], ps[:, 4, :], decay[:, 0, t, :], ALU.mult))
                link(dve.tensor_tensor(h_u[:, :], ps[:, 5, :], decay[:, 1, t, :], ALU.mult))
                dve.tensor_tensor(h_s[:, 0, t, :], h_t[:, :], h_u[:, :], ALU.add).then_inc(sem("h_mix"), 1)
                dve.tensor_tensor(h_s[:, 1, t, :], h_t[:, :], h_u[:, :], ALU.subtract).then_inc(sem("h_mix"), 1)

            def hysc_out(j, i):
                dve.tensor_copy(hysc[:, 2 * j:2 * j + 2, :], ps[:, bank("hysc", j), :].rearrange("p (c s) -> p c s", c=2))\
                   .then_inc(sem("bank_free"), 1)

            unit = unit_with("hysc", hysc_out)
            for j in range(12):
                unit(j)
                for what, *args in FILTERS_ALONGSIDE.get(j, []):
                    if what != "spectrum":
                        {"layer": filter_layer, "taps": filter_taps}[what](*args)
            dve.wait_ge(sem("h_mix"), 8)

            def na_out(j, i):
                if j < 4:
                    kind, jj = j // 2, j % 2
                    dve.tensor_copy(qkv[:, 2 * jj:2 * jj + 2, kind * S:(kind + 1) * S],
                                    ps[:, bank("naqkv", j), :].rearrange("p (c s) -> p c s", c=2)).then_inc(sem("bank_free"), 1)
                else:
                    v_out("naqkv", j, j - 4)

            unit = unit_with("naqkv", na_out)
            dve.wait_ge(sem("bank_free"), BANK0["naqkv"])

            def w3(name, first, tap, n=4):
                t3 = col(name).rearrange("p (k j) -> p k j", j=3)
                return t3[:, first:first + n, tap][:, :, None]

            vv = hysc[:, 0:4, :]
            link(dve.tensor_tensor(cv[0][:, :, :], vv, w3("hyw", 0, 1).to_broadcast([P, 4, S]), ALU.mult))
            link(dve.tensor_tensor(cv[1][:, :, 1:S], vv[:, :, 0:S - 1], w3("hyw", 0, 0).to_broadcast([P, 4, S - 1]), ALU.mult))
            link(dve.tensor_tensor(cv[0][:, :, 1:S], cv[0][:, :, 1:S], cv[1][:, :, 1:S], ALU.add))
            link(dve.tensor_tensor(cv[1][:, :, 0:S - 1], vv[:, :, 1:S], w3("hyw", 0, 2).to_broadcast([P, 4, S - 1]), ALU.mult))
            link(dve.tensor_tensor(vv[:, :, 0:S - 1], cv[0][:, :, 0:S - 1], cv[1][:, :, 0:S - 1], ALU.add))
            dve.tensor_copy(vv[:, :, S - 1:S], cv[0][:, :, S - 1:S]).then_inc(sem("z_ready"), 1)
            dve.wait_ge(sem("z_ready"), 1)
            dve.wait_ge(sem("spec_read"), 8)
            for o in range(2):
                src = z_s if o else hysc
                unit(3 * o)
                dve.wait_ge(sem("zf_pe"), o + 1)
                for f in range(2):
                    zr, zi = ps[:, 4 + f, :], ps[:, 6 + f, :]
                    kr, ki = spec[:, o, 0, f, :], spec[:, o, 1, f, :]
                    if f == 0 and o == 1:
                        dve.wait_ge(sem("yt_pe"), 1)
                    link(dve.tensor_tensor(y_f[:, 0, f, :], zr, kr, ALU.mult))
                    link(dve.tensor_tensor(y_t[:, :], zi, ki, ALU.mult))
                    link(dve.tensor_tensor(y_f[:, 0, f, :], y_f[:, 0, f, :], y_t[:, :], ALU.subtract))
                    link(dve.tensor_tensor(y_f[:, 1, f, :], zr, ki, ALU.mult))
                    link(dve.tensor_tensor(y_t[:, :], zi, kr, ALU.mult))
                    mm = dve.tensor_tensor(y_f[:, 1, f, :], y_f[:, 1, f, :], y_t[:, :], ALU.add)
                    if f == 0:
                        link(mm)
                mm.then_inc(sem("y_f"), 1)
                unit(3 * o + 1)
                dve.wait_ge(sem("yt_pe"), o + 1)
                for k in range(4):
                    mm = stt(cv[0][:, k, :], src[:, k, :], col("hyb")[:, 4 * o + k:4 * o + k + 1],
                             ps[:, 4 + k // 2, (k % 2) * S:(k % 2 + 1) * S], ALU.mult, ALU.add)
                link(mm)
                dve.wait_ge(sem("gate_conv"), o + 1)
                if o == 0:
                    dve.tensor_tensor(z_s[:, :, :], cv[0][:, :, :], hysc[:, 4:8, :], ALU.mult).then_inc(sem("z_ready"), 1)
                    dve.wait_ge(sem("z_ready"), 2)
                    unit(2)
                else:
                    dve.tensor_tensor(cv[1][:, :, :], cv[0][:, :, :], hysc[:, 8:12, :], ALU.mult).then_inc(sem("ya"), 1)
                    dve.wait_ge(sem("ya"), 1)
                    link(dve.tensor_copy(ya_hi[:, :, :], cv[1][:, :, :]))
                    link(dve.tensor_tensor(ya_lo[:, :, :], cv[1][:, :, :], ya_hi[:, :, :], ALU.subtract))

            unit(5)
            dve.wait_ge(sem("yc_split"), 2)

            def gates_out(j, i):
                c = slice(2 * j, 2 * j + 2)
                dve.tensor_tensor(gates[:, c, :], ps[:, bank("gates", j), :].rearrange("p (c s) -> p c s", c=2),
                                  col("gateb")[:, c][:, :, None].to_broadcast([P, 2, S]), ALU.add)\
                   .then_inc(sem("bank_free"), 1)

            attention("attn", "na", 4, unit_with("gates", gates_out))
            dve.wait_ge(sem("gate_t"), 12)
            for j in range(6):
                u, half, br = Unit(FIRST["branch"] + j), j // 3, j % 3
                next_lo(dve, u)
                dve.wait_ge(sem("w_used"), u.count(1))
                for b in range(2):
                    c = 4 * half + 2 * b
                    g = gates[:, 8 * br + c:8 * br + c + 2, :]
                    src = ps[:, bank("branch", 2 * j + b), :].rearrange("p (c s) -> p c s", c=2)
                    acc = m_acc[:, c:c + 2, :]
                    if br == 0:
                        stt(acc, g, 1.0, src, ALU.add, ALU.mult).then_inc(sem("bank_free"), 1)
                    else:
                        stt(m_t[:, :, :], g, 1.0, src, ALU.add, ALU.mult).then_inc(sem("bank_free"), 1)
                        dve.wait_ge(sem("bank_free"), BANK0["branch"] + 2 * j + b + 1)
                        mm = dve.tensor_tensor(acc, acc, m_t[:, :, :], ALU.add)
                        if br == 2 and b == 1:
                            mm.then_inc(sem("m_acc"), 1)
                            dve.wait_ge(sem("m_acc"), half + 1)
                        else:
                            link(mm)
            dve.wait_ge(sem("rstd_mem"), 1)
            for b in range(4):
                cs = slice(b * S, (b + 1) * S)
                for t in range(NT):
                    dve.tensor_scalar(mem_tok[:, t, cs], mem_tok[:, t, cs], mx[1][:, t:t + 1], None, ALU.mult)\
                       .then_inc(sem("src"), 1)
            for b in range(4):
                dve.wait_ge(sem("merged_hi"), b + 1)
                stt(aT_lo[:, 2 * b:2 * b + 2, :], m_acc[:, 2 * b:2 * b + 2, :], 0.5, aT_hi[:, 2 * b:2 * b + 2, :],
                    ALU.mult, ALU.subtract).then_inc(sem("merged"), 1)
            lows("t_mem", memT_lo, memT_hi, g=col("memg"))
            dve.wait_ge(sem("maps_loaded"), 16 * 9)
            follow("wout", scaled)
            post_norm("p0", "x_res0", 4, (sem("bank_free"), BANK0["xk"]))

            def x_out(at_, phase):
                def out(j, i):
                    dve.tensor_copy(xqkv[:, j, at_:at_ + 512], ps[:, bank(phase, j), :]).then_inc(sem("bank_free"), 1)
                return out

            follow("xk", x_out(512, "xk"))
            pre_norm("r1")
            unit = unit_with("xv", x_out(1024, "xv"))
            unit(0)
            unit(1)
            lows("t_r1", g=col("ng")[:, 16:24])
            unit(2)
            unit(3)
            unit = unit_with("xq", x_out(0, "xq"))
            unit(0)
            unit(1)
            attention("attx", "xa", 4, unit)
            dve.wait_ge(sem("maps_loaded"), 16 * 10)
            ss_before[0] = 8
            follow("xo", scaled)
            post_norm("p1", "x_res1", 4, (sem("bank_free"), BANK0["ffn2"]))
            pre_norm("r2")
            lows("t_r2", g=col("ng")[:, 32:40])
            ffn("ffn2", "f2", second=True)
            dve.wait_ge(sem("maps_loaded"), 16 * 11)
            for t in range(NT):
                for h in range(2):
                    dve.wait_ge(sem("ss"), 16 + 2 * t + h + 1)
                    cs = slice(h * 512, (h + 1) * 512)
                    dve.tensor_tensor(nrm[:, t, cs], ps[:, 4 + 2 * t + h, :], gmap[:, cs], ALU.mult).then_inc(sem("acc_read"), 1)
            post_norm("p2", "out_ready", 2, (sem("acc_read"), 2 + 4))

        @block.gpsimd
        def _(pool):
            chain = [0]

            def link(ins):
                chain[0] += 1
                ins.then_inc(sem("pool_chain"), 1)
                pool.wait_ge(sem("pool_chain"), chain[0])

            def load_map(dst, row):
                r = ROWS.index(row)
                pool.dma_start(dst[:, :], A["rows"][r:r + 1, :].to_broadcast([P, D])).then_inc(sem("maps_loaded"), 16)

            def inverse_root(tag, src, eps, scale=1.0, dst=None):
                dst = rstd if dst is None else dst
                link(pool.tensor_scalar(dst[:, 0:NT], src, scale, eps, ALU.mult, ALU.add))
                pool.tensor_tensor(dst[:, 0:NT], dst[:, 0:NT], mhalf[:, :], ALU.pow).then_inc(sem("rstd_" + tag), 1)

            def layer_norm(tag, n, maps, nxt):
                pool.wait_ge(sem("mv"), n)
                inverse_root(tag, mv[:, :, 1], 1e-5)
                pool.wait_ge(sem("maps_loaded"), 16 * maps)
                pool.wait_ge(sem("src"), 8 * n)
                for t in range(NT):
                    link(pool.tensor_tensor(x_tok[:, t, :], nrm[:, t, :], gmap[:, :], ALU.mult))
                    pool.tensor_tensor(x_tok[:, t, :], x_tok[:, t, :], bmap[:, :], ALU.add).then_inc(sem(f"x_new{n}"), 1)
                pool.wait_ge(sem(f"x_new{n}"), 2)
                for dst, row in zip((gmap, bmap), nxt):
                    load_map(dst, row)

            def fox_masks():
                base = ATT0["att1"]
                for u in range(8):
                    p = u % 2
                    if u > 1:
                        pool.wait_ge(sem("att_sc_read"), base["sc_read"] + 4 * (u - 1))
                    for m in range(2):
                        c = fox_c[:, 2 * u + m, :]
                        pool.tensor_tensor(mc[p][:, m, 0:P], col("cmask")[:, 0:P], c[:, 0:P], ALU.add)
                        mm = pool.tensor_tensor(mc[p][:, m, P:384], col("cmask")[:, P:384], c, ALU.add)
                    mm.then_inc(sem("mask_ready"), 1)

            def window_masks():
                base = ATT0["attn"]
                for u in range(4):
                    p = u % 2
                    if u > 1:
                        pool.wait_ge(sem("att_sc_read"), base["sc_read"] + 4 * (u - 1))
                    pool.dma_start(mc[p][:, :, :].rearrange("p m (t k) -> p (m t) k", t=NT),
                                   A["nabias"].rearrange("h (t q) k -> q (h t) k", q=P)[:, 4 * u:4 * u + 4, :])\
                        .then_inc(sem(f"bias_in{p}"), 16)
                    pool.wait_ge(sem(f"bias_in{p}"), 16 * (u // 2 + 1))
                    b4 = mc[p][:, :, :].rearrange("p m (t k) -> p (m t) k", t=NT)
                    link(pool.tensor_scalar(b4, b4, 8.0, 0.0, ALU.mult, ALU.add))
                    pool.tensor_tensor(b4, b4, col("namask")[:, None, :].to_broadcast([P, 4, S]), ALU.add)\
                        .then_inc(sem("mask_ready"), 1)

            link(pool.memset(mhalf[:, :], -0.5))
            pool.dma_start(fw[:, :, :], A["fw"]).then_inc(sem("fw_loaded"), 16)
            pool.dma_start(f_b[:, :], A["fb"].to_broadcast([P, 16])).then_inc(sem("fw_loaded"), 16)
            pool.dma_start(pos_i[:, :], A["positions"].to_broadcast([P, S])).then_inc(sem("pos_loaded"), 16)
            pool.dma_start(lam_in[:, :, :].rearrange("p a b -> p (a b)"), A["lam"].to_broadcast([P, 256]))\
                .then_inc(sem("lam_loaded"), 16)
            load_map(gmap, "ln1g0")
            load_map(bmap, "ln1b0")
            pool.wait_ge(sem("rope"), 3)
            for h in range(8):
                pool.wait_ge(sem("rot_done"), h + 1)
                both = qkv[:, h, 0:512].rearrange("p (a s) -> p a s", a=2)
                pool.tensor_tensor(both, both, rope_c[:, None, :].to_broadcast([P, 2, S]), ALU.mult).then_inc(sem("rot_cos"), 1)
            layer_norm("ln0", 1, 2, ["ln2g0", "ln2b0"])
            layer_norm("ln1", 2, 4, ["ln1g1", "ln1b1"])
            pool.wait_ge(sem("fox_c"), 8)
            fox_masks()
            pool.wait_ge(sem("att_o"), ATT0["att1"]["o"] + 8)
            for dst, src in ((hw1, "hw1"), (hw2, "hw2"), (hw3, "hw3")):
                pool.dma_start(dst[:, :], A[src]).then_inc(sem("hin_loaded"), 16)
            layer_norm("ln2", 3, 6, ["ln2g1", "ln2b1"])
            layer_norm("ln3", 4, 8, [])
            pool.wait_ge(sem("w_used"), FIRST["ffn1"])
            pool.dma_start(decay[:, :, :, :], A["decay"]).then_inc(sem("hin_loaded"), 16)
            pool.dma_start(dft[:, :, :, :], A["dft"]).then_inc(sem("hin_loaded"), 16)
            pool.wait_ge(sem("w_used"), FIRST["hysc"])
            pool.dma_start(zembT[:, :], A["zembT"]).then_inc(sem("hin_loaded"), 16)
            pool.wait_ge(sem("sq_r0"), 2)
            inverse_root("r0", ssq[:, :], 1e-6, 1 / D)
            pool.wait_ge(sem("bank_free"), BANK0["naqkv"])

            def short(first, name, w0, src, buf):
                x = src[:, first:first + 4, :]
                t3 = col(name).rearrange("p (k j) -> p k j", j=3)

                def tap(j, n):
                    return t3[:, w0:w0 + 4, j][:, :, None].to_broadcast([P, 4, n])

                a, b = buf
                link(pool.tensor_tensor(a[:, :, :], x, tap(1, S), ALU.mult))
                link(pool.tensor_tensor(b[:, :, 1:S], x[:, :, 0:S - 1], tap(0, S - 1), ALU.mult))
                link(pool.tensor_tensor(a[:, :, 1:S], a[:, :, 1:S], b[:, :, 1:S], ALU.add))
                link(pool.tensor_tensor(b[:, :, 0:S - 1], x[:, :, 1:S], tap(2, S - 1), ALU.mult))
                link(pool.tensor_tensor(x[:, :, 0:S - 1], a[:, :, 0:S - 1], b[:, :, 0:S - 1], ALU.add))
                return pool.tensor_copy(x[:, :, S - 1:S], a[:, :, S - 1:S])

            pool.wait_ge(sem("spec_pe"), 8)
            short(4, "hyw", 4, hysc, cp).then_inc(sem("gate_conv"), 1)
            pool.wait_ge(sem("gate_conv"), 1)
            short(8, "hyw", 8, hysc, cp).then_inc(sem("gate_conv"), 1)
            pool.wait_ge(sem("gate_conv"), 2)
            link(pool.tensor_tensor(hysc[:, 16:20, :], hysc[:, 16:20, :], hysc[:, 20:24, :], ALU.mult))
            link(short(16, "scw", 0, hysc, cp))
            link(pool.tensor_tensor(hysc[:, 16:20, :], hysc[:, 16:20, :], hysc[:, 12:16, :], ALU.mult))
            pool.wait_ge(sem("ya"), 1)
            pool.tensor_copy(yc_hi[:, :, :], hysc[:, 16:20, :]).then_inc(sem("yc_split"), 1)
            pool.wait_ge(sem("yc_split"), 1)
            pool.tensor_tensor(yc_lo[:, :, :], hysc[:, 16:20, :], yc_hi[:, :, :], ALU.subtract).then_inc(sem("yc_split"), 1)
            pool.wait_ge(sem("nabias"), 16 * 32)
            load_map(gmap, "ng1")
            window_masks()
            pool.wait_ge(sem("att_o"), ATT0["attn"]["o"] + 4)
            pool.dma_start(mem_tok[:, :, :], A["mem"].rearrange("(t p) d -> p t d", p=P)).then_inc(sem("mem_loaded"), 16)
            pool.wait_ge(sem("sq_mem"), 2)
            inverse_root("mem", mx[0][:, 0:NT], 1e-6, 1 / D, dst=mx[1])
            pool.wait_ge(sem("sq_p0"), 1)
            inverse_root("p0", ssq[:, :], 1e-6, 1 / D)
            pool.wait_ge(sem("x_res0"), 2)
            load_map(gmap, "ng3")
            pool.wait_ge(sem("sq_r1"), 2)
            inverse_root("r1", ssq[:, :], 1e-6, 1 / D)
            pool.wait_ge(sem("sq_p1"), 1)
            inverse_root("p1", ssq[:, :], 1e-6, 1 / D)
            pool.wait_ge(sem("x_res1"), 2)
            load_map(gmap, "ng5")
            pool.wait_ge(sem("sq_r2"), 2)
            inverse_root("r2", ssq[:, :], 1e-6, 1 / D)
            pool.wait_ge(sem("sq_p2"), 1)
            inverse_root("p2", ssq[:, :], 1e-6, 1 / D)


def b_units(w):
    n = w.shape[1]
    return w.reshape(KC, P, n // 256, 256).transpose(2, 1, 0, 3).reshape(n // 256, P, UNIT)


def qkv_units(w):
    q, k, v = (w[:, j * D:(j + 1) * D].reshape(D, KC, P) for j in range(3))
    seq = []
    for j in range(0, KC, 2):
        seq += [q[:, j], k[:, j], q[:, j + 1], k[:, j + 1], v[:, j], v[:, j + 1]]
    return b_units(np.concatenate(seq, 1))


def ffn_units(w_in, w_out):
    gate, up = b_units(w_in[:, :DFF]), b_units(w_in[:, DFF:])
    down = w_out.reshape(FI, 2, P, D).transpose(0, 2, 1, 3).reshape(FI, P, UNIT)
    seq = [gate[0], up[0], gate[1], up[1], down[0]]
    for k in range(2, FI):
        seq += [gate[k], up[k], down[k - 1]]
    return np.stack(seq + [down[FI - 1]])


def branch_units(w):
    return w.reshape(3, 4, P, 2, 512).transpose(3, 0, 2, 1, 4).reshape(6, P, UNIT)


def constants():
    f = np.float32
    out = {"ident": np.eye(P, dtype=f), "mean": np.full((P, P), 1 / P, f), "ones16": np.ones((P, P), f),
           "eye16": np.eye(P, 16, dtype=f)}
    rot = np.zeros((P, P), f)
    for base in (0, 64):
        for j in range(8):
            rot[base + j, base + 8 + j] = -1
            rot[base + 8 + j, base + j] = 1
    out["rotT"] = rot.T
    tri = np.where(np.arange(P)[None, :] <= np.arange(P)[:, None], 0, NEG).astype(f)
    out["cmask"] = np.concatenate([tri, np.zeros((P, P), f), tri], 1)
    c = np.arange(64)
    start = np.clip(c - 8, 0, 48)
    win = np.where((c[None, :] >= start[:, None]) & (c[None, :] < start[:, None] + 16), 0, NEG).astype(f)
    out["namask"] = np.tile(win, (2, 4))
    inv = 500000.0 ** (-np.arange(0, 16, 2) / 16)
    invf = np.zeros((P, 1), f)
    for base in (0, 64):
        invf[base:base + 8, 0] = invf[base + 8:base + 16, 0] = inv
    out["invf"] = invf
    out["eps_rms"] = np.full((P, 1), 1e-6, f)
    out["halfpi"] = np.full((P, 1), np.pi / 2, f)
    return out


def fourier():
    j, q = np.arange(S)[:, None], np.arange(S)[None, :] + 0.5
    th = 2 * np.pi * j * q / (2 * S)
    m = [np.cos(th), -np.sin(th), np.cos(th).T / S, -np.sin(th).T / S]
    return np.stack([x.reshape(2, P, S).transpose(1, 0, 2) for x in m], 1).astype(np.float32)


def filter_inputs():
    L = S
    t = np.linspace(0.0, 1.0, L)[:, None]
    w = 2.0 * np.pi * np.arange(L)[:, None] / L
    f = np.linspace(1e-4, 15, 16)[None, :]
    z = np.concatenate([t, np.cos(f * w), -np.sin(f * w)], 1)
    deltas = np.abs(np.linspace(np.log(1e-2) / 1.5, np.log(1e-2) / 0.3, 512))
    dec = np.exp(-t * deltas)
    back = dec.copy()
    back[0] = 0
    d = np.stack([x.reshape(2, P, 512).transpose(1, 0, 2) for x in (dec, back)], 1)
    return np.ascontiguousarray(z.T).astype(np.float32), d.astype(np.float32)


def cols_of(v):
    return v.reshape(-1, P).T


def kernel(**a):
    import concourse.bacc as _bacc
    from concourse import mybir as _mybir
    from concourse.bass_utils import run_bass_kernel_spmd as _run

    a = {k: np.asarray(x) for k, x in a.items()}
    w_in = a["w_in_2"][0]
    hy, na, sc, ga = w_in[:, :1536], w_in[:, 1536:3072], w_in[:, 3072:4608], w_in[:, 4608:]
    fox = a["fox_w_in"][0]
    stream = np.concatenate([
        qkv_units(a["diff_w_qkv"][0]), b_units(a["diff_w_o"][0]), ffn_units(a["ffn_w_in"][0], a["ffn_w_out"][0]),
        qkv_units(fox[:, :3072]), b_units(a["fox_w_o"][0]), ffn_units(a["ffn_w_in"][1], a["ffn_w_out"][1]),
        b_units(hy), b_units(sc), b_units(na), b_units(ga), branch_units(a["w_branch_2"][0]), b_units(a["w_out_2"][0]),
        b_units(a["xa_wkv_2"][0]), b_units(a["xa_wq_2"][0]), b_units(a["xa_wo_2"][0]),
        ffn_units(a["ffn_up_2"][0], a["ffn_down_2"][0])])
    assert stream.shape == (NUNITS, P, UNIT)

    con = constants()
    con.update(ln1g=cols_of(a["ln1_g"]), ln1b=cols_of(a["ln1_b"]), ln2g=cols_of(a["ln2_g"]), ln2b=cols_of(a["ln2_b"]),
               ng=cols_of(a["norm_gains_2"][0]), memg=cols_of(a["mem_norm_2"][0]),
               hyw=a["hy_short_w_2"][0].reshape(3, 12, P).transpose(2, 1, 0).reshape(P, 36),
               hyb=cols_of(a["hy_bias_2"][0]), scw=a["sc_conv_w_2"][0].reshape(3, 4, P).transpose(2, 1, 0).reshape(P, 12),
               gateb=cols_of(a["gate_bias_2"][0]), subg=cols_of(a["diff_subln_g"][0]))
    for l in range(2):
        w = np.concatenate([a["ffn_conv_w"][l], a["ffn_conv_b"][l][None]])
        con[f"conv{l}"] = w.reshape(4, 2 * FI, P).transpose(2, 1, 0).reshape(P, 8 * FI)
    w = a["ffn_conv_2"][0].reshape(3, 2, 2 * FI, P)
    con["conv2"] = w.transpose(3, 2, 1, 0).reshape(P, 12 * FI)
    for name, src in (("hb1", a["hy_b1_2"][0]), ("hb2", a["hy_b2_2"][0]), ("hf1", a["hy_freq_2"][0, 0]),
                      ("hf2", a["hy_freq_2"][0, 1])):
        con[name] = np.concatenate([src, np.zeros(64, np.float32)])[:, None]
    cst = np.concatenate([con[n] for n in COLS], 1).astype(np.float32)
    assert cst.shape == (P, NCOLS)

    rows = np.stack([a["ln1_g"][0], a["ln1_b"][0], a["ln2_g"][0], a["ln2_b"][0], a["ln1_g"][1], a["ln1_b"][1],
                     a["ln2_g"][1], a["ln2_b"][1]] + [a["norm_gains_2"][0, n] for n in (1, 3, 5)])
    zembT, decay = filter_inputs()
    arrays = {
        "x": a["x"][0], "positions": a["positions"].reshape(1, S), "mem": a["mem_2"][0], "wstream": stream, "cst": cst,
        "rows": rows,
        "lam": np.concatenate([a["diff_lambda_q1"], a["diff_lambda_k1"], a["diff_lambda_q2"], a["diff_lambda_k2"]], 1),
        "fw": fox[:, 3072:].reshape(KC, P, 16).transpose(1, 0, 2), "fb": a["fox_b_f"],
        "rpb": np.pad(a["na_rpb_2"][0][:, 4:11], ((0, 0), (0, 0), (48, 48))).reshape(1, -1),
        "zembT": zembT, "hw1": a["hy_w1_2"][0], "hw2": a["hy_w2_2"][0], "hw3": a["hy_w3_2"][0], "decay": decay,
        "dft": fourier(),
    }
    arrays = {k: np.ascontiguousarray(x) for k, x in arrays.items()}
    nc = _bacc.Bacc("TRN2", target_bir_lowering=False, num_devices=1)
    A = {k: nc.dram_tensor("in_" + k, x.shape, _mybir.dt.from_np(x.dtype), kind="ExternalInput").ap()
         for k, x in arrays.items()}
    A["narep"] = nc.dram_tensor("narep", (64, arrays["rpb"].shape[1]), F32, kind="Internal").ap()
    A["nabias"] = nc.dram_tensor("nabias", (8, S, S), F32, kind="Internal").ap()
    A["out"] = nc.dram_tensor("out_0", (S, D), F32, kind="ExternalOutput").ap()
    two_blocks_kernel(nc, A)
    r = _run(nc, [{"in_" + k: x for k, x in arrays.items()}], core_ids=[0])
    return r.results[0]["out_0"].reshape(1, S, D)
```

```python
import math
from contextlib import ExitStack

import numpy as np

import concourse.bass as bass
from concourse import mybir

F32 = mybir.dt.float32
F32R = mybir.dt.float32r
ALU = mybir.AluOpType
ACT = mybir.ActivationFunctionType
AX = mybir.AxisListType.X

P = 128
S = 256
NT = S // P
D = 1024
KC = D // P
DFF = 2816
FI = DFF // 256
UNIT = 2048
DEPTH = 2
ALPHA = (2 * DEPTH) ** 0.25
LAMBDA_INIT = 0.8 - 0.6 * math.exp(-0.3 * 0)
NEG = -1e30

PHASES = [("l0_qkv", 12), ("l0_wo", 4), ("ffn0", 3 * FI),
          ("l1_qkv", 12), ("l1_wo", 4), ("ffn1", 3 * FI),
          ("hysc", 12), ("naqkv", 6), ("gates", 12), ("branch", 6), ("wout", 4),
          ("xkvq", 12), ("xo", 4), ("ffn2", 3 * FI)]
UNITS = dict(PHASES)
FIRST, _n = {}, 0
for _name, _k in PHASES:
    FIRST[_name] = _n
    _n += _k
NUNITS = _n
RAW, HI, LO = 3, 3, 2
LOOP = 6

BANK_STAGES = [("l0_qkv", 12), ("l0_wo", 4), ("ffn0", 2 * FI),
               ("l1_qkv", 12), ("l1_wo", 4), ("ffn1", 2 * FI),
               ("hysc", 12), ("naqkv", 6), ("gates", 12), ("branch", 12), ("wout", 4),
               ("xkvq", 12), ("xo", 4), ("ffn2", 2 * FI)]
BANK0, _n = {}, 0
for _name, _k in BANK_STAGES:
    BANK0[_name] = _n
    _n += _k

XKVQ = [("k", 0), ("k", 1), ("k", 2), ("k", 3), ("v", 0), ("q", 0), ("q", 1), ("q", 2), ("v", 1), ("q", 3), ("v", 2), ("v", 3)]

NORMS = ["t_ln0", "t_ln1", "t_ln2", "t_r0", "t_mem", "t_r1", "t_r2"]
LN_STAGES = ["t_ln0", "t_ln1", "t_ln2"]
T_STAGES = ["t_x", "t_ln0", "t_ln1", "t_ln2", "t_r0", "t_mem", "t_r1", "t_r2"]

QKV_HEADS = [[[("u", 1)], [("r", 1), ("u", 2)]], [[("u", 3)], [("r", 2), ("u", 4)]], [[("r", 3), ("u", 5)], []],
             [[("u", 6)], [("r", 4), ("u", 7)]], [[("r", 5), ("u", 8)], []], [[("u", 9)], [("r", 6)]],
             [[("u", 10)], [("r", 7)]], [[("u", 11)], []], [[], []], [[], []]]
ALONGSIDE = {
    "att0": QKV_HEADS,
    "att1": [[[x for x in part if x[0] == "u" and x[1] > 1] for part in step] for step in QKV_HEADS],
    "attn": [[[("u", 1)], [("u", 2)]], [[("u", 3)], [("u", 4), ("u", 5)]], [[("u", 6)], [("u", 7)]],
             [[("u", 8)], [("u", 9)]], [[("u", 10)], [("u", 11)]], [[], []]],
    "attx": [[[("u", 6)], []], [[("u", 7)], [("u", 8)]], [[("u", 9)], [("u", 10)]], [[("u", 11)], []], [[], []], [[], []]],
}

FILTERS_ALONGSIDE = {1: [("layer", 0)], 3: [("layer", 1)], 5: [("taps", 0, 0)], 6: [("taps", 0, 1)],
                     7: [("spectrum", 0, 0)], 8: [("spectrum", 0, 1), ("taps", 1, 0)], 9: [("taps", 1, 1)],
                     10: [("spectrum", 1, 0)], 11: [("spectrum", 1, 1)]}

def counts_before(stages):
    before, total = {}, {}
    for tag, per_step, steps in stages:
        before[tag] = dict(total)
        for name, k in per_step.items():
            total[name] = total.get(name, 0) + k * steps
    for b in before.values():
        for name in total:
            b.setdefault(name, 0)
    return before


def attention_signals(kind):
    maps = 1 if kind == "xa" else 2
    npt = 1 if kind == "diff" else maps
    out = dict(st=1, sc=maps, sc_read=2 * maps, nb=1, ex=2 * maps, rs=1, pn=1, pt=npt, pt_read=npt, o=1, o_hi=1, o_read=1)
    if kind == "diff":
        out.update(rl=1, p2=2, sq=1, ms=1, ln=1, ov=1)
        out["or"] = 1
    return out


ATT0 = counts_before([("att0", attention_signals("diff"), 8), ("att1", attention_signals("fox"), 8),
                      ("attn", attention_signals("na"), 4), ("attx", attention_signals("xa"), 4)])
FFN0 = counts_before([("f0", dict(fa=2, fc=3, ft=1, fd=1, fh=1, h=1), FI),
                      ("f1", dict(fa=2, fc=3, ft=1, fd=1, fh=1, h=1), FI),
                      ("f2", dict(fa=2, fb=2, fc=3, fe=3, fs=1, fp=1, fm=1, ft=1, fd=1, fv=1, fh=1, h=1), FI)])

COLS, _n = {}, 0
for _name, _k in [("ident", P), ("rotT", P), ("mean", P), ("cmask", 384), ("namask", 256),
                  ("ln1g", 16), ("ln1b", 16), ("ln2g", 16), ("ln2b", 16), ("ng", 48), ("memg", 8),
                  ("conv0", FI * 8), ("conv1", FI * 8), ("conv2", FI * 12), ("hyw", 36), ("hyb", 8), ("scw", 12),
                  ("gateb", 24), ("hb1", 1), ("hb2", 1), ("hf1", 1), ("hf2", 1), ("invf", 1), ("subg", 1),
                  ("eps_rms", 1), ("halfpi", 1)]:
    COLS[_name] = (_n, _n + _k)
    _n += _k
NCOLS = _n
ROWS = ["ln1g0", "ln1b0", "ln2g0", "ln2b0", "ln1g1", "ln1b1", "ln2g1", "ln2b1", "ng1", "ng3", "ng5"]


class Unit:

    def __init__(self, g, i=None):
        self.g, self.i = g, i

    def plus(self, k):
        return Unit(self.g + k, self.i)

    def count(self, k=0):
        return self.g + k if self.i is None else self.i * LOOP + (self.g + k)

    @property
    def slot(self):
        return self.g % RAW

    @property
    def loaded(self):
        n = 16 * (self.g // RAW + 1)
        return n if self.i is None else self.i * (16 * LOOP // RAW) + n


def two_blocks_kernel(nc, A):
    ctx = ExitStack()
    with ctx:
        sems = {}

        def sem(name):
            if name not in sems:
                sems[name] = ctx.enter_context(nc.semaphore(name))
            return sems[name]

        at = [16512]

        def region(nbytes):
            r = at[0]
            at[0] += nbytes
            assert at[0] <= 229344, at[0]
            return r

        def place(name, shape, off, dt=F32):
            return nc.alloc_sbuf_tensor_at(name, shape, dt, offset=off)

        KB = 1024
        w_raw = [place(f"w_raw{j}", [P, UNIT], region(8 * KB)) for j in range(RAW)]
        w_hi = [place(f"w_hi{j}", [P, UNIT], region(8 * KB), F32R) for j in range(HI)]
        w_lo = [place(f"w_lo{j}", [P, UNIT], region(8 * KB), F32R) for j in range(LO)]
        x_tok = place("x_tok", [P, NT, D], region(8 * KB))
        scr = region(28 * KB)
        aT_hi = place("aT_hi", [P, KC, S], region(8 * KB), F32R)
        aT_lo = place("aT_lo", [P, KC, S], region(8 * KB), F32R)
        qkv_at = region(24 * KB)
        hysc_at = region(24 * KB)
        yT_at = region(24 * KB)
        maps_at = region(8 * KB)
        cst = place("cst", [P, NCOLS], region((NCOLS * 4 + 31) // 32 * 32))
        small_at = region(2 * KB)
        first_ident = place("first_ident", [P, P], qkv_at)

        def col(name, a=0, b=None):
            lo, hi = COLS[name]
            return cst[:, lo + a:hi if b is None else lo + b]

        ident = col("ident")
        qkv = place("qkv", [P, 8, 768], qkv_at)
        xqkv = place("xqkv", [P, 4, 1536], qkv_at)
        hysc = place("hysc", [P, 24, S], hysc_at)
        gates = place("gates", [P, 24, S], hysc_at)
        mem_tok = place("mem_tok", [P, NT, D], qkv_at)
        fox_c = place("fox_c", [P, 16, S], hysc_at)
        head_row = place("head_row", [16, 16, P], yT_at + 16 * KB)
        ya_hi = place("ya_hi", [P, 4, S], yT_at, F32R)
        ya_lo = place("ya_lo", [P, 4, S], yT_at + 4 * KB, F32R)
        yb_hi = place("yb_hi", [P, 4, S], yT_at + 8 * KB, F32R)
        yb_lo = place("yb_lo", [P, 4, S], yT_at + 12 * KB, F32R)
        yc_hi = place("yc_hi", [P, 4, S], yT_at + 16 * KB, F32R)
        yc_lo = place("yc_lo", [P, 4, S], yT_at + 20 * KB, F32R)
        oT_hi = place("oT_hi", [P, KC, S], yT_at, F32R)
        oT_lo = place("oT_lo", [P, KC, S], yT_at + 8 * KB, F32R)
        ox_hi = place("ox_hi", [P, KC, S], hysc_at, F32R)
        ox_lo = place("ox_lo", [P, KC, S], hysc_at + 8 * KB, F32R)
        memT_hi = place("memT_hi", [P, KC, S], yT_at, F32R)
        memT_lo = place("memT_lo", [P, KC, S], yT_at + 8 * KB, F32R)
        spec = place("spec", [P, 2, 2, 2, 512], yT_at + 8 * KB)
        gmap = place("gmap", [P, D], maps_at)
        bmap = place("bmap", [P, D], maps_at + 4 * KB)
        dft = place("dft", [P, 4, 2, S], maps_at)
        rope_c = place("rope_c", [P, S], small_at)
        rope_s = place("rope_s", [P, S], small_at + KB)

        nrm = place("nrm", [P, NT, D], scr)
        vT = place("vT", [P, KC, S], scr + 8 * KB)
        junk = [place(f"junk{t}", [P, D], scr + (16 + 4 * t) * KB) for t in range(NT)]
        tiny = region(KB)
        stat = place("stat", [P, NT, 4, 6], tiny)
        mv = place("mv", [P, NT, 2], tiny + 192)
        rstd = place("rstd", [P, NT], tiny + 224)
        ssum = place("ssum", [P, NT, 4], tiny + 256)
        ssq = place("ssq", [P, NT], tiny + 320)
        mhalf = place("mhalf", [P, NT], tiny + 384)
        ff = scr + 8 * KB
        f_a = [place(f"f_a{j}", [P, 2, S], ff + 2 * KB * j) for j in range(2)]
        f_u = [place(f"f_u{j}", [P, 2, S], ff + (4 + 2 * j) * KB) for j in range(2)]
        f_t = place("f_t", [P, 2, S], ff + 8 * KB)
        f_v = place("f_v", [P, 2, S], ff + 10 * KB)
        hT_hi = [place(f"hT_hi{j}", [P, 2, S], ff + (12 + 2 * j) * KB, F32R) for j in range(2)]
        hT_lo = [place(f"hT_lo{j}", [P, 2, S], ff + (16 + 2 * j) * KB, F32R) for j in range(2)]
        mc = [place(f"mc{j}", [P, 2, 512], scr + 4 * j * KB) for j in range(2)]
        pb = [place(f"pb{j}", [P, 2, 512], scr + (8 + 4 * j) * KB) for j in range(2)]
        pT = place("pT", [P, 2, 512], scr + 16 * KB)
        o_v = place("o_v", [P, S], scr + 20 * KB)
        o_r = place("o_r", [P, S], scr + 21 * KB)
        o_q = place("o_q", [P, S], scr + 22 * KB)
        mx = [place(f"mx{j}", [P, 4], tiny + 448 + 32 * j) for j in range(2)]
        nb = [place(f"nb{j}", [P, 4], tiny + 576 + 32 * j) for j in range(2)]
        sm = [place(f"sm{j}", [P, 4], tiny + 704 + 32 * j) for j in range(2)]
        rs = [place(f"rs{j}", [P, 4], tiny + 832 + 32 * j) for j in range(2)]
        ang = place("ang", [P, S], scr + 0)
        ang_k = place("ang_k", [P, S], scr + KB)
        ang_a = place("ang_a", [P, S], scr + 2 * KB)
        pos_i = place("pos_i", [P, S], scr + 3 * KB, mybir.dt.int32)
        lam_in = place("lam_in", [P, 4, 64], scr + 4 * KB)
        lam_j = place("lam_j", [P, 2, 64], scr + 5 * KB)
        lam = place("lam", [P, 4], region(32))
        sub_g = place("sub_g", [P, 1], region(32))
        rot_t = place("rot_t", [P, 2, S], scr + 24 * KB)
        fox_at = hysc_at + 16 * KB
        fw = place("fw", [P, KC, 16], fox_at + 0)
        fw_hi = place("fw_hi", [P, KC, 16], fox_at + 512, F32R)
        fw_lo = place("fw_lo", [P, KC, 16], fox_at + 1024, F32R)
        f_b = place("f_b", [P, 16], fox_at + 1536)
        f_tok = place("f_tok", [P, NT, 16], fox_at + 1664)
        f_z = place("f_z", [16, S], fox_at + 2 * KB)
        f_abs = place("f_abs", [16, S], fox_at + 3 * KB)
        f_min = place("f_min", [16, S], fox_at + 4 * KB)
        f_ones = place("f_ones", [16, S], fox_at + 5 * KB)
        f_cum = place("f_cum", [16, S], fox_at + 6 * KB)
        h_t = place("h_t", [P, 512], qkv_at)
        h_u = place("h_u", [P, 512], qkv_at + 2 * KB)
        h_a = place("h_a", [64, S], qkv_at + 4 * KB)
        h_x = place("h_x", [64, S], qkv_at + 5 * KB)
        h_k = place("h_k", [64, S], qkv_at + 6 * KB)
        hw1 = place("hw1", [33, 64], qkv_at + 7 * KB)
        hw2 = place("hw2", [64, 64], qkv_at + 7 * KB + 256)
        hw3 = place("hw3", [64, 2048], qkv_at + 8 * KB)
        h_s = place("h_s", [P, 2, NT, 512], qkv_at + 16 * KB)
        zembT = place("zembT", [33, S], scr + 26 * KB)
        decay = place("decay", [P, 2, NT, 512], yT_at)
        z_tok = place("z_tok", [P, NT, 512], scr + 0)
        y_f = place("y_f", [P, 2, 2, 512], scr + 4 * KB)
        y_t = place("y_t", [P, 512], scr + 12 * KB)
        cv = [place(f"cv{j}", [P, 4, S], scr + (14 + 4 * j) * KB) for j in range(2)]
        cp = [place(f"cp{j}", [P, 4, S], qkv_at + (12 + 4 * j) * KB) for j in range(2)]
        z_s = place("z_s", [P, 4, S], scr + 22 * KB)
        m_acc = place("m_acc", [P, KC, S], scr + 0)
        m_t = place("m_t", [P, 2, S], scr + 8 * KB)

        ps = ctx.enter_context(nc.psum_tensor("ps", [P, 8, 512], F32))

        block = ctx.enter_context(nc.Block())

        def convert_hi(act, u):
            act.wait_ge(sem(f"w_loaded{u.slot}"), u.loaded)
            if u.g >= HI:
                act.wait_ge(sem("w_used"), u.count(1 - HI))
            act.activation(w_hi[u.g % HI][:, :], w_raw[u.slot][:, :], ACT.Copy).then_inc(sem("hi_ready"), 1)

        def convert_lo(dve, u):
            dve.wait_ge(sem("hi_ready"), u.count(1))
            if u.g >= LO:
                dve.wait_ge(sem("w_used"), u.count(1 - LO))
            dve.tensor_tensor(w_lo[u.g % LO][:, :], w_raw[u.slot][:, :], w_hi[u.g % HI][:, :], ALU.subtract)\
               .then_inc(sem("lo_ready"), 1)

        def next_hi(act, u):
            if u.g + HI < NUNITS:
                convert_hi(act, u.plus(HI))

        def next_lo(dve, u):
            if u.g + LO < NUNITS:
                convert_lo(dve, u.plus(LO))

        def run_units(eng, phase, one):
            n, g0 = UNITS[phase], FIRST[phase]
            if n % LOOP == 0 and n > LOOP:
                with eng.Fori(0, n // LOOP) as i:
                    for j in range(LOOP):
                        one(Unit(g0 + j, i), j, i)
            else:
                for j in range(n):
                    one(Unit(g0 + j), j, None)

        def bank(stage, j):
            return j % 2

        def bank_value(stage, j, i=None, body=LOOP, k=0):
            v = BANK0[stage] + j + k
            return v if i is None else i * body + v

        def wait_bank(pe, stage, j, i=None, body=LOOP):
            if BANK0[stage] + j >= 2:
                pe.wait_ge(sem("bank_free"), bank_value(stage, j, i, body, k=-1))

        def branch_bank(j, b):
            return (2 * j + b) % 4

        def t_count(stage, per, k):
            return T_STAGES.index(stage) * per + k

        def projected(tag, kind, head):
            if tag in ("att0", "att1"):
                j = 3 * (head // 2) + (head % 2 if kind == "scores" else 2)
                return BANK0["l0_qkv" if tag == "att0" else "l1_qkv"] + j + 1
            if tag == "attx":
                return BANK0["xkvq"] + XKVQ.index(("q" if kind == "scores" else "v", head)) + 1
            return BANK0["gates"]

        def per_iteration(k, i, n, more=0):
            return n * k + more if i is None else i * (2 * n) + (n * k + more)

        def ffn_iterations(eng, g0, iteration, output_unit):
            iteration(Unit(g0), 0, third=False)
            iteration(Unit(g0 + 2), 1)
            with eng.Fori(0, (FI - 3) // 2) as i:
                iteration(Unit(g0 + 5, i), 2, i)
                iteration(Unit(g0 + 8, i), 3, i)
            iteration(Unit(g0 + 3 * FI - 4), FI - 1)
            output_unit(Unit(g0 + 3 * FI - 1))

        def last_unit(phase):
            return FIRST[phase] + UNITS[phase]

        @block.sync
        def _(sp):
            def load(u):
                if u.g >= RAW:
                    sp.wait_ge(sem("lo_ready"), u.count(1 - RAW))
                src = A["wstream"][u.count()]
                sp.dma_start(w_raw[u.slot][:, :], src).then_inc(sem(f"w_loaded{u.slot}"), 16)

            sp.dma_start(x_tok[:, :, :], A["x"].rearrange("(t p) d -> p t d", p=P)).then_inc(sem("x_loaded"), 16)
            for name, n in PHASES:
                g0 = FIRST[name]
                if name.startswith("ffn"):
                    for j in range(5):
                        load(Unit(g0 + j))
                    with sp.Fori(0, (n - 9) // LOOP) as i:
                        for j in range(LOOP):
                            load(Unit(g0 + 5 + j, i))
                    for j in range(n - 4, n):
                        load(Unit(g0 + j))
                elif g0 == 0:
                    for j in range(n):
                        load(Unit(j))
                else:
                    run_units(sp, name, lambda u, j, i: load(u))
            for t in range(NT):
                sp.wait_ge(sem("out_ready"), t + 1)
                sp.dma_start(A["out"][t * P:(t + 1) * P, :], x_tok[:, t, :]).then_inc(sem("out_stored"), 16)
            sp.wait_ge(sem("out_stored"), 16 * NT)

        @block.tensor
        def _(pe):
            def three(out, l_hi, l_lo, r_hi, r_lo, start, stop):
                pe.matmul(out, l_hi, r_hi, start=start, stop=False)
                pe.matmul(out, l_hi, r_lo, start=False, stop=False)
                return pe.matmul(out, l_lo, r_hi, start=False, stop=stop)

            def transposes(stage, src):
                for b in range(4):
                    if stage == "t_x":
                        pe.wait_ge(sem("x_loaded"), 16)
                    else:
                        pe.wait_ge(sem("src"), 8 * NORMS.index(stage) + 2 * b + 2)
                    for c in range(2):
                        for t in range(NT):
                            k = 2 * b + c
                            mm = pe.transpose(ps[:, 4 + b, c * S + t * P:c * S + t * P + P], src[:, t, k * P:(k + 1) * P],
                                              first_ident[:, :] if stage == "t_x" else ident)
                    mm.then_inc(sem("transposed"), 1)

            def by_chunks(hi, lo):
                return (hi[:, :].rearrange("p (k n) -> p k n", k=KC), lo[:, :].rearrange("p (k n) -> p k n", k=KC))

            def split_of(stage):
                def wait(k):
                    if k % 2 == 0:
                        pe.wait_ge(sem("split"), t_count(stage, 4, k // 2 + 1))
                return wait

            def heads_of(tag, chunks):
                def wait(k):
                    if k % chunks == 0:
                        pe.wait_ge(sem("att_o_read"), ATT0[tag]["o_read"] + k // chunks + 1)
                return wait

            def unit_b(u, stage, j, i=None, a=(aT_hi, aT_lo), fresh=None, body=LOOP):
                pe.wait_ge(sem("lo_ready"), u.count(1))
                wait_bank(pe, stage, j, i, body)
                hi, lo = by_chunks(w_hi[u.g % HI], w_lo[u.g % LO])
                for c in range(2):
                    for k in range(KC):
                        if c == 0 and fresh:
                            fresh(k)
                        mm = three(ps[:, bank(stage, j), c * S:(c + 1) * S], hi[:, k, c * P:(c + 1) * P],
                                   lo[:, k, c * P:(c + 1) * P], a[0][:, k, :], a[1][:, k, :], k == 0, k == KC - 1)
                mm.then_inc(sem("w_used"), 1)

            def unit_a(u, stage, j, i=None, a=(aT_hi, aT_lo), fresh=None, body=LOOP):
                pe.wait_ge(sem("lo_ready"), u.count(1))
                wait_bank(pe, stage, j, i, body)
                hi, lo = by_chunks(w_hi[u.g % HI], w_lo[u.g % LO])
                for t in range(NT):
                    for k in range(KC):
                        if t == 0 and fresh:
                            fresh(k)
                        mm = three(ps[:, bank(stage, j), t * S:(t + 1) * S], a[0][:, k, t * P:(t + 1) * P],
                                   a[1][:, k, t * P:(t + 1) * P], hi[:, k, :], lo[:, k, :], k == 0, k == KC - 1)
                mm.then_inc(sem("w_used"), 1)

            def units(stage, unit, a=(aT_hi, aT_lo), fresh=None):
                run_units(pe, stage, lambda u, j, i: unit(u, stage, j, i, a, fresh if j == 0 else None))

            def ffn(stage, tag, t_stage):
                g0 = FIRST[stage]

                def up(u, k, i=None):
                    for j in range(2):
                        unit_b(u.plus(j), stage, 2 * k + j, i, fresh=split_of(t_stage) if k + j == 0 else None, body=4)

                def down(u, k, first=False, last=False, i=None):
                    pe.wait_ge(sem("lo_ready"), u.count(1))
                    pe.wait_ge(sem("ffn_h"), FFN0[tag]["h"] + (i * 2 if i is not None else 0) + k + 1)
                    hi = w_hi[u.g % HI][:, :].rearrange("p (k n) -> p k n", k=2)
                    lo = w_lo[u.g % LO][:, :].rearrange("p (k n) -> p k n", k=2)
                    q = k % 2
                    for t in range(NT):
                        for h in range(2):
                            for c in range(2):
                                mm = three(ps[:, 4 + 2 * t + h, :], hT_hi[q][:, c, t * P:(t + 1) * P],
                                           hT_lo[q][:, c, t * P:(t + 1) * P], hi[:, c, h * 512:(h + 1) * 512],
                                           lo[:, c, h * 512:(h + 1) * 512], first and c == 0, last and c == 1)
                        if last and t == 0:
                            mm.then_inc(sem("rows_done"), 1)
                    mm.then_inc(sem("w_used"), 1)

                up(Unit(g0), 0)
                up(Unit(g0 + 2), 1)
                down(Unit(g0 + 4), 0, first=True)
                trips = (FI - 3) // 2
                with pe.Fori(0, trips) as i:
                    for j in range(2):
                        up(Unit(g0 + 5 + 3 * j, i), 2 + j, i)
                        down(Unit(g0 + 7 + 3 * j, i), 1 + j, i=i)
                up(Unit(g0 + 5 + 6 * trips), FI - 1)
                down(Unit(g0 + 7 + 6 * trips), FI - 2)
                down(Unit(g0 + 8 + 6 * trips), FI - 1, last=True)

            def attention(tag, kind, n, unit):
                causal = kind in ("diff", "fox")
                maps = 1 if kind == "xa" else 2
                npt = 1 if kind == "diff" else maps
                q_cols = [(0, 128), (128, 256)] if causal else [(0, 256), (256, 256)]
                base = ATT0[tag]
                heads = qkv if kind != "xa" else xqkv

                def scores(u):
                    if kind == "diff":
                        pe.wait_ge(sem("rot_add"), u + 1)
                    else:
                        pe.wait_ge(sem("bank_free"), projected(tag, "scores", u))
                    if u > 0:
                        pe.wait_ge(sem("att_sc_read"), base["sc_read"] + u * 2 * maps)
                    for m in range(maps):
                        for t in range(NT):
                            c0, n_k = q_cols[t]
                            out = ps[:, 4 + m, c0:c0 + n_k]
                            if kind == "xa":
                                for c in range(2):
                                    mm = pe.matmul(out, heads[:, u, c * S + t * P:c * S + t * P + P],
                                                   heads[:, u, 512 + c * S:512 + (c + 1) * S], start=c == 0, stop=c == 1)
                            else:
                                r = slice(64 * m, 64 * m + 64)
                                mm = pe.matmul(out, heads[r, u, t * P:(t + 1) * P], heads[r, u, S:S + n_k], start=True, stop=True)
                        mm.then_inc(sem("att_sc"), 1)

                def transposed(u):
                    pe.wait_ge(sem("att_pn"), base["pn"] + u + 1)
                    if u > 0:
                        pe.wait_ge(sem("att_pt_read"), base["pt_read"] + u * npt)
                    for m in range(npt):
                        for kt in range(NT):
                            for t in range(NT):
                                if causal and kt > t:
                                    continue
                                c0 = q_cols[t][0] + kt * P
                                to = (0 if kt == 0 else S) + (t * P if not (causal and kt == 1) else 0)
                                mm = pe.transpose(ps[:, 6 + m, to:to + P], pb[u % 2][:, m, c0:c0 + P], ident)
                        mm.then_inc(sem("att_pt"), 1)

                def values(u):
                    pe.wait_ge(sem("bank_free"), projected(tag, "values", u))
                    if u > 1:
                        pe.wait_ge(sem("att_o_read"), base["o_read"] + u - 1)
                    ob = ps[:, 2 + u % 2, :]
                    for m in range(npt):
                        pe.wait_ge(sem("att_pt_read"), base["pt_read"] + u * npt + m + 1)
                        if kind == "diff":
                            outs = [(slice(0, P), 0, 2 * S, P, P)]
                        elif kind == "xa":
                            outs = [(slice(0, P), c * S, 1024 + c * P, P, S) for c in range(2)]
                        else:
                            outs = [(slice(64 * m, 64 * m + 64), 0, 2 * S + 64 * m, 64, P)]
                        for rows, o0, v0, width, step in outs:
                            for kt in range(NT):
                                lhs = heads[:, u, v0 + kt * step:v0 + kt * step + width]
                                if kt == 0:
                                    mm = pe.matmul(ob[rows, o0:o0 + S], lhs, pT[:, m, 0:S], start=True, stop=False)
                                elif causal:
                                    mm = pe.matmul(ob[rows, o0 + P:o0 + S], lhs, pT[:, m, S:S + P], start=False, stop=True)
                                else:
                                    mm = pe.matmul(ob[rows, o0:o0 + S], lhs, pT[:, m, S:2 * S], start=False, stop=True)
                    mm.then_inc(sem("att_o"), 1)

                def alongside(part):
                    for what, j in part:
                        if what == "u":
                            unit(j)
                        else:
                            rotate(j)

                for step, (first, second) in enumerate(ALONGSIDE[tag]):
                    if 0 <= step - 1 < n:
                        transposed(step - 1)
                    if step < n:
                        scores(step)
                    alongside(first)
                    if 0 <= step - 1 < n:
                        values(step - 1)
                    alongside(second)
                    if 0 <= step - 1 < n and kind == "diff":
                        pe.wait_ge(sem("att_sq"), base["sq"] + step)
                        pe.matmul(ps[:, 2 + (step - 1) % 2, S:2 * S], col("mean"), o_q[:, :], start=True, stop=True)\
                          .then_inc(sem("att_ms"), 1)

            def rotate(h):
                pe.wait_ge(sem("bank_free"), projected("att0", "scores", h))
                if h > 0:
                    pe.wait_ge(sem("rot_read"), h)
                pe.matmul(ps[:, 7, :], col("rotT"), qkv[:, h, 0:512], start=True, stop=True).then_inc(sem("rot_done"), 1)

            def qkv_unit(stage, t_stage):
                return lambda j: (unit_a if j % 3 == 2 else unit_b)(Unit(FIRST[stage] + j), stage, j,
                                                                    fresh=split_of(t_stage) if t_stage and j == 0 else None)

            pe.wait_ge(sem("ident_loaded"), 16)
            transposes("t_x", x_tok)
            unit = qkv_unit("l0_qkv", "t_x")
            unit(0)
            pe.wait_ge(sem("cst_loaded"), 16)
            rotate(0)
            attention("att0", "diff", 8, unit)
            units("l0_wo", unit_a, (oT_hi, oT_lo), heads_of("att0", 1))
            transposes("t_ln0", nrm)
            ffn("ffn0", "f0", "t_ln0")
            transposes("t_ln1", nrm)
            pe.wait_ge(sem("split"), t_count("t_ln1", 4, 4))
            unit = qkv_unit("l1_qkv", None)
            pe.wait_ge(sem("fw_split"), 1)
            for t in range(NT):
                for k in range(KC):
                    mm = three(ps[:, 4, t * 16:t * 16 + 16], aT_hi[:, k, t * P:(t + 1) * P], aT_lo[:, k, t * P:(t + 1) * P],
                               fw_hi[:, k, :], fw_lo[:, k, :], k == 0, k == KC - 1)
            mm.then_inc(sem("f_done"), 1)
            unit(0)
            pe.wait_ge(sem("f_tok"), 1)
            for t in range(NT):
                mm = pe.transpose(ps[0:16, 5, t * P:(t + 1) * P], f_tok[:, t, :], ident)
            mm.then_inc(sem("f_done"), 1)
            unit(1)
            pe.wait_ge(sem("head_row"), 16)
            pe.wait_ge(sem("f_cum"), 1)
            for j in range(8):
                if j >= 4:
                    pe.wait_ge(sem("fox_c"), j - 3)
                for m in range(2):
                    mm = pe.matmul(ps[:, 4 + j % 4, m * S:(m + 1) * S], head_row[:, 2 * j + m, :], f_cum[:, :], start=True, stop=True)
                mm.then_inc(sem("fox_pe"), 1)
            pe.wait_ge(sem("fox_c"), 8)
            attention("att1", "fox", 8, unit)
            units("l1_wo", unit_a, (oT_hi, oT_lo), heads_of("att1", 1))
            transposes("t_ln2", nrm)
            ffn("ffn1", "f1", "t_ln2")
            def filter_layer(layer):
                if layer == 0:
                    pe.wait_ge(sem("hin_loaded"), 16 * 6)
                    pe.wait_ge(sem("split"), t_count("t_r0", 4, 4))
                    pe.matmul(ps[0:64, 4, 0:S], hw1[:, :], zembT[:, :], start=True, stop=True).then_inc(sem("h_pe"), 1)
                else:
                    pe.wait_ge(sem("h_sin"), 1)
                    pe.matmul(ps[0:64, 5, 0:S], hw2[:, :], h_x[:, :], start=True, stop=True).then_inc(sem("h_pe"), 1)

            def filter_taps(o, t):
                pe.wait_ge(sem("h_sin"), 2)
                if o + t > 0:
                    pe.wait_ge(sem("h_mix"), 2 * (2 * o + t))
                for d in range(2):
                    mm = pe.matmul(ps[:, 4 + d, :], h_x[:, t * P:(t + 1) * P],
                                   hw3[:, (2 * d + o) * 512:(2 * d + o + 1) * 512], start=True, stop=True)
                mm.then_inc(sem("h_pe"), 1)

            def spectrum(o, part):
                pe.wait_ge(sem("h_mix"), 4 * (o + 1))
                for f in range(2):
                    n = 4 * o + 2 * part + f
                    if n >= 2:
                        pe.wait_ge(sem("spec_read"), n - 1)
                    for t in range(NT):
                        mm = pe.matmul(ps[:, 6 + f, :], dft[:, part, t, f * P:(f + 1) * P], h_s[:, part, t, :],
                                       start=t == 0, stop=t == NT - 1)
                    mm.then_inc(sem("spec_pe"), 1)

            transposes("t_r0", nrm)
            for j in range(12):
                unit_b(Unit(FIRST["hysc"] + j), "hysc", j, fresh=split_of("t_r0") if j == 0 else None)
                for what, *args in FILTERS_ALONGSIDE.get(j, []):
                    {"layer": filter_layer, "taps": filter_taps, "spectrum": spectrum}[what](*args)
            def naqkv_unit(j):
                (unit_b if j < 4 else unit_a)(Unit(FIRST["naqkv"] + j), "naqkv", j)

            pe.wait_ge(sem("spec_read"), 8)
            for o in range(2):
                if o == 0:
                    pe.wait_ge(sem("hy_conv"), 1)
                else:
                    pe.wait_ge(sem("z_ready"), 1)
                for k in range(4):
                    for t in range(NT):
                        src = (z_s if o else hysc)[:, k, t * P:(t + 1) * P]
                        mm = pe.transpose(ps[:, 4 + t, k * P:(k + 1) * P], src, ident)
                mm.then_inc(sem("zt_pe"), 1)
                pe.wait_ge(sem("z_tok"), 2 * (o + 1))
                for part in range(2):
                    for f in range(2):
                        for t in range(NT):
                            mm = pe.matmul(ps[:, 4 + 2 * part + f, :], dft[:, part, t, f * P:(f + 1) * P], z_tok[:, t, :],
                                           start=t == 0, stop=t == NT - 1)
                mm.then_inc(sem("zf_pe"), 1)
                naqkv_unit(3 * o)
                naqkv_unit(3 * o + 1)
                pe.wait_ge(sem("y_f"), o + 1)
                for k in range(4):
                    for part in range(2):
                        for f in range(2):
                            mm = pe.matmul(ps[:, 4 + k // 2, (k % 2) * S:(k % 2 + 1) * S],
                                           y_f[:, part, f, k * P:(k + 1) * P], dft[:, 2 + part, f, :],
                                           start=part + f == 0, stop=part + f == 2)
                mm.then_inc(sem("yt_pe"), 1)
                naqkv_unit(3 * o + 2)
            gate_unit = lambda j: unit_b(Unit(FIRST["gates"] + j), "gates", j)
            gate_unit(0)
            pe.wait_ge(sem("ya"), 1)
            attention("attn", "na", 4, gate_unit)
            pe.wait_ge(sem("yc_split"), 2)
            for j in range(6):
                u, half, br = Unit(FIRST["branch"] + j), j // 3, j % 3
                a_hi, a_lo = [(ya_hi, ya_lo), (yb_hi, yb_lo), (yc_hi, yc_lo)][br]
                if j == 1:
                    pe.wait_ge(sem("att_o_read"), ATT0["attn"]["o_read"] + 4)
                pe.wait_ge(sem("lo_ready"), u.count(1))
                hi = w_hi[u.g % HI][:, :].rearrange("p (k n) -> p k n", k=4)
                lo = w_lo[u.g % LO][:, :].rearrange("p (k n) -> p k n", k=4)
                for b in range(2):
                    pe.wait_ge(sem("bank_free"), BANK0["branch"] + (b - 1 if j == 0 else 2 * j + b - 3))
                    for c in range(2):
                        m = 2 * b + c
                        for k in range(4):
                            mm = three(ps[:, branch_bank(j, b), c * S:(c + 1) * S], hi[:, k, m * P:(m + 1) * P],
                                       lo[:, k, m * P:(m + 1) * P], a_hi[:, k, :], a_lo[:, k, :], k == 0, k == 3)
                    mm.then_inc(sem("branch_half" if b == 0 else "w_used"), 1)
            transposes("t_mem", mem_tok)
            units("wout", unit_a, fresh=lambda k: pe.wait_ge(sem("merged"), k // 2 + 1) if k % 2 == 0 else None)

            def x_unit(j):
                what, head = XKVQ[j]
                fresh = {("k", 0): split_of("t_mem"), ("q", 0): split_of("t_r1")}.get((what, head))
                (unit_a if what == "v" else unit_b)(Unit(FIRST["xkvq"] + j), "xkvq", j, fresh=fresh,
                                                    a=(aT_hi, aT_lo) if what == "q" else (memT_hi, memT_lo))

            for j in range(4):
                x_unit(j)
            transposes("t_r1", nrm)
            x_unit(4)
            x_unit(5)
            attention("attx", "xa", 4, x_unit)
            units("xo", unit_a, (ox_hi, ox_lo), heads_of("attx", 2))
            transposes("t_r2", nrm)
            ffn("ffn2", "f2", "t_r2")

        @block.scalar
        def _(act):
            def follow(phase, also=None):
                def one(u, j, i):
                    if also:
                        also(u, j, i)
                    next_hi(act, u)

                run_units(act, phase, one)

            def gains(stage, g, b=None, hi=aT_hi):
                if b is None:
                    for k in range(KC):
                        act.wait_ge(sem("transposed"), t_count(stage, 4, k // 2 + 1))
                        c = (k % 2) * S
                        act.activation(hi[:, k, :], ps[:, 4 + k // 2, c:c + S], ACT.Identity, scale=g[:, k:k + 1])\
                           .then_inc(sem("split_hi"), 1)
                    return
                ln = LN_STAGES.index(stage)
                for even in (0, 2):
                    act.wait_ge(sem("transposed"), t_count(stage, 4, even + 1))
                    for k in (2 * even, 2 * even + 1):
                        c = (k % 2) * S
                        act.activation(vT[:, k, :], ps[:, 4 + even, c:c + S], ACT.Identity, scale=g[:, k:k + 1],
                                       bias=b[:, k:k + 1]).then_inc(sem("whole_act"), 1)
                    for n in (even, even + 1):
                        act.wait_ge(sem("whole_dve" if n % 2 else "whole_act"), 4 * ln + (n // 2 + 1) * 2)
                        both = slice(2 * n, 2 * n + 2)
                        act.activation(hi[:, both, :], vT[:, both, :], ACT.Copy).then_inc(sem("split_hi"), 2)

            def ffn(phase, tag, second=False):
                g0 = FIRST[phase]
                w = col("conv" + tag[1])
                cols = 12 if second else 8

                def iteration(u, k, i=None, third=True):
                    q = k % 2
                    K = lambda n, more=0: per_iteration(k, i, n, more)
                    gb, ub = bank(phase, 2 * k), bank(phase, 2 * k + 1)
                    act.wait_ge(sem("w_used"), u.count(1))
                    if k >= 2:
                        act.wait_ge(sem("ffn_h"), FFN0[tag]["h"] + K(1, -1))
                    for c in range(2):
                        o = 6 * c if second else 4 * c
                        tap = w[:, bass.ds(K(cols, o + (1 if second else 2)), 1)]
                        off = 0.0 if second else w[:, bass.ds(K(cols, o + 3), 1)]
                        act.activation(f_a[q][:, c, :], ps[:, gb, c * S:(c + 1) * S], ACT.Identity, scale=tap, bias=off)\
                           .then_inc(sem("ffn_fa"), 1)
                    next_hi(act, u)
                    act.wait_ge(sem("bank_free"), bank_value(phase, 2 * k + 1, i, body=4))
                    if k >= 1:
                        act.wait_ge(sem("ffn_h"), FFN0[tag]["h"] + K(1))
                    if second:
                        act.activation(f_t[:, :, :], f_a[q][:, :, :], ACT.Square).then_inc(sem("ffn_fs"), 1)
                        act.wait_ge(sem("w_used"), u.count(2))
                        for c in range(2):
                            tap = w[:, bass.ds(K(cols, 6 * c + 4), 1)]
                            act.activation(f_u[q][:, c, :], ps[:, ub, c * S:(c + 1) * S], ACT.Identity, scale=tap)\
                               .then_inc(sem("ffn_fb"), 1)
                        act.wait_ge(sem("ffn_fm"), FFN0[tag]["fm"] + K(1, 1))
                        act.activation(f_t[:, :, :], f_t[:, :, :], ACT.Tanh).then_inc(sem("ffn_ft"), 1)
                    else:
                        act.activation(f_t[:, :, :], f_a[q][:, :, :], ACT.Tanh, scale=0.5).then_inc(sem("ffn_ft"), 1)
                    next_hi(act, u.plus(1))
                    if second:
                        act.wait_ge(sem("ffn_fv"), FFN0[tag]["fv"] + K(1, 1))
                    else:
                        act.wait_ge(sem("bank_free"), bank_value(phase, 2 * k + 2, i, body=4))
                    act.activation(hT_hi[q][:, :, :], f_v[:, :, :], ACT.Copy).then_inc(sem("ffn_fh"), 1)
                    if third:
                        next_hi(act, u.plus(2))

                ffn_iterations(act, g0, iteration, lambda u: next_hi(act, u))

            def attention(tag, kind, n, unit=None):
                maps = 1 if kind == "xa" else 2
                npt = 1 if kind == "diff" else maps
                causal = kind in ("diff", "fox")
                q_cols = [(0, 128), (128, 256)] if causal else [(0, 256), (256, 256)]
                scale = 1 / 16 if kind == "xa" else 1 / 8
                base = ATT0[tag]
                out_hi = {"na": yb_hi, "xa": ox_hi}.get(kind, oT_hi)

                def alongside(part):
                    for what, j in part:
                        if what == "u":
                            unit(j)

                def squares(u):
                    act.wait_ge(sem("att_o"), base["o"] + u + 1)
                    act.activation(o_q[:, :], ps[:, 2 + u % 2, 0:S], ACT.Square).then_inc(sem("att_sq"), 1)

                def inverse_root(u):
                    act.wait_ge(sem("att_ms"), base["ms"] + u + 1)
                    act.activation(o_r[:, :], ps[:, 2 + u % 2, S:2 * S], ACT.Ln, bias=col("eps_rms")).then_inc(sem("att_ln"), 1)
                    act.wait_ge(sem("att_ln"), base["ln"] + u + 1)
                    act.activation(o_r[:, :], o_r[:, :], ACT.Exp, scale=-0.5).then_inc(sem("att_or"), 1)

                def outputs(u):
                    ob = ps[:, 2 + u % 2, :]
                    if kind == "diff":
                        act.wait_ge(sem("att_ov"), base["ov"] + u + 1)
                        dst, src = out_hi[:, u, :], o_v[:, :]
                    else:
                        act.wait_ge(sem("att_o"), base["o"] + u + 1)
                        if kind == "xa":
                            dst, src = out_hi[:, 2 * u:2 * u + 2, :].rearrange("p a b -> p (a b)"), ob
                        else:
                            dst, src = out_hi[:, u, :], ob[:, 0:S]
                    act.activation(dst, src, ACT.Copy).then_inc(sem("att_o_hi"), 1)

                for step, (first, second) in enumerate(ALONGSIDE[tag]):
                    u = step - 1
                    if 0 <= u < n:
                        for m in range(npt):
                            act.wait_ge(sem("att_pt"), base["pt"] + u * npt + m + 1)
                            if u > 0:
                                act.wait_ge(sem("att_o"), base["o"] + u)
                            w = 384 if causal else 512
                            act.activation(pT[:, m, 0:w], ps[:, 6 + m, 0:w], ACT.Copy).then_inc(sem("att_pt_read"), 1)
                    if step < n:
                        p = step % 2
                        act.wait_ge(sem("att_nb"), base["nb"] + step + 1)
                        for m in range(maps):
                            for t in range(NT):
                                c0, n_k = q_cols[t]
                                row = pb[p][:, m, c0:c0 + n_k]
                                act.activation(row, row, ACT.Exp, scale=scale, bias=nb[p][:, 2 * m + t:2 * m + t + 1],
                                               accum_out=sm[p][:, 2 * m + t:2 * m + t + 1]).then_inc(sem("att_ex"), 1)
                    if step >= 2:
                        outputs(step - 2)
                    alongside(first)
                    if 0 <= u < n and kind == "diff":
                        squares(u)
                    alongside(second)
                    if 0 <= u < n and kind == "diff":
                        inverse_root(u)

            def plain_unit(phase):
                return lambda j: next_hi(act, Unit(FIRST[phase] + j))

            def unit_squares(u, j, i):
                act.wait_ge(sem("w_used"), u.count(1))
                for t in range(NT):
                    act.activation(junk[t][:, j * S:(j + 1) * S], ps[:, j % 2, t * S:(t + 1) * S], ACT.Square,
                                   accum_out=ssum[:, t, j:j + 1]).then_inc(sem("ss"), 1)

            def row_squares(tag, src, ready):
                for t in range(NT):
                    act.wait_ge(sem(ready[t][0]), ready[t][1])
                    act.activation(junk[t][:, :], src[:, t, :], ACT.Square, accum_out=ssq[:, t:t + 1])\
                       .then_inc(sem("sq_" + tag), 1)

            act.dma_start(first_ident[:, :], A["cst"][:, 0:P]).then_inc(sem("ident_loaded"), 16)
            act.dma_start(cst[:, :], A["cst"]).then_inc(sem("cst_loaded"), 16)
            for b in range(4):
                act.wait_ge(sem("transposed"), b + 1)
                act.activation(aT_hi[:, 2 * b:2 * b + 2, :].rearrange("p a b -> p (a b)"), ps[:, 4 + b, :], ACT.Copy)\
                   .then_inc(sem("split_hi"), 2)
                if b in (1, 3):
                    convert_hi(act, Unit(b // 2))
            convert_hi(act, Unit(2))
            act.wait_ge(sem("ang_red"), 1)
            act.activation(rope_s[:, :], ang[:, :], ACT.Sin).then_inc(sem("rope"), 1)
            act.activation(ang_a[:, :], ang[:, :], ACT.Abs).then_inc(sem("rope"), 1)
            act.wait_ge(sem("rope"), 2)
            act.activation(rope_c[:, :], ang_a[:, :], ACT.Sin, scale=-1.0, bias=col("halfpi")).then_inc(sem("rope"), 1)
            act.wait_ge(sem("lam_dot"), 2)
            act.activation(lam[:, 0:2], lam[:, 0:2], ACT.Exp).then_inc(sem("lam_exp"), 1)
            plain_unit("l0_qkv")(0)
            attention("att0", "diff", 8, plain_unit("l0_qkv"))
            act.wait_ge(sem("fw_loaded"), 32)
            act.activation(fw_hi[:, :, :], fw[:, :, :], ACT.Copy).then_inc(sem("fw_hi"), 1)
            follow("l0_wo")
            gains("t_ln0", col("ln1g")[:, 0:8], col("ln1b")[:, 0:8])
            ffn("ffn0", "f0")
            gains("t_ln1", col("ln2g")[:, 0:8], col("ln2b")[:, 0:8])
            plain_unit("l1_qkv")(0)
            act.wait_ge(sem("f_z"), 1)
            act.activation(f_abs[:, :], f_z[:, :], ACT.Abs).then_inc(sem("f_act"), 1)
            act.wait_ge(sem("f_act"), 1)
            act.activation(f_abs[:, :], f_abs[:, :], ACT.Exp, scale=-1.0).then_inc(sem("f_act"), 1)
            act.wait_ge(sem("f_act"), 2)
            act.activation(f_abs[:, :], f_abs[:, :], ACT.Ln, bias=1.0).then_inc(sem("f_act"), 1)
            plain_unit("l1_qkv")(1)
            for j in range(8):
                act.wait_ge(sem("fox_pe"), j + 1)
                act.activation(fox_c[:, 2 * j:2 * j + 2, :].rearrange("p a b -> p (a b)"), ps[:, 4 + j % 4, :], ACT.Copy)\
                   .then_inc(sem("fox_c"), 1)
            attention("att1", "fox", 8, plain_unit("l1_qkv"))
            follow("l1_wo")
            gains("t_ln2", col("ln1g")[:, 8:16], col("ln1b")[:, 8:16])
            ffn("ffn1", "f1")
            row_squares("r0", x_tok, [("x_new4", 1), ("x_new4", 2)])
            gains("t_r0", col("ng")[:, 0:8])

            def filter_sine(layer):
                act.wait_ge(sem("h_red"), layer + 1)
                act.activation(h_x[:, :], h_k[:, :], ACT.Sin).then_inc(sem("h_sin"), 1)

            def spectrum(o, part):
                for f in range(2):
                    act.wait_ge(sem("spec_pe"), 4 * o + 2 * part + f + 1)
                    act.activation(spec[:, o, part, f, :], ps[:, 6 + f, :], ACT.Copy).then_inc(sem("spec_read"), 1)

            for j in range(12):
                next_hi(act, Unit(FIRST["hysc"] + j))
                for what, *args in FILTERS_ALONGSIDE.get(j, []):
                    if what != "taps":
                        {"layer": filter_sine, "spectrum": spectrum}[what](*args)
            for o in range(2):
                act.wait_ge(sem("zt_pe"), o + 1)
                for t in range(NT):
                    act.activation(z_tok[:, t, :], ps[:, 4 + t, :], ACT.Copy).then_inc(sem("z_tok"), 1)
                for j in range(3 * o, 3 * o + 3):
                    plain_unit("naqkv")(j)

            def gate_unit(j):
                plain_unit("gates")(j)
                act.wait_ge(sem("bank_free"), bank_value("gates", j, k=1))
                g = gates[:, 2 * j:2 * j + 2, :]
                act.activation(g, g, ACT.Tanh, scale=0.5).then_inc(sem("gate_t"), 1)

            gate_unit(0)
            attention("attn", "na", 4, gate_unit)
            act.wait_ge(sem("mem_loaded"), 16)
            for t in range(NT):
                act.activation(junk[t][:, :], mem_tok[:, t, :], ACT.Square, accum_out=mx[0][:, t:t + 1]).then_inc(sem("sq_mem"), 1)

            def merged_hi(half):
                act.wait_ge(sem("m_acc"), half + 1)
                for b in (2 * half, 2 * half + 1):
                    act.activation(aT_hi[:, 2 * b:2 * b + 2, :], m_acc[:, 2 * b:2 * b + 2, :], ACT.Copy, scale=0.5)\
                       .then_inc(sem("merged_hi"), 1)

            follow("branch", lambda u, j, i: merged_hi(0) if j == 3 else None)
            merged_hi(1)
            gains("t_mem", col("memg"), hi=memT_hi)
            act.wait_ge(sem("sq_mem"), 2)
            follow("wout", unit_squares)
            for j in range(3):
                plain_unit("xkvq")(j)
            act.wait_ge(sem("ss"), 8)
            row_squares("r1", x_tok, [("x_post0", 1), ("x_post0", 2)])
            plain_unit("xkvq")(3)
            gains("t_r1", col("ng")[:, 16:24])
            plain_unit("xkvq")(4)
            plain_unit("xkvq")(5)
            attention("attx", "xa", 4, plain_unit("xkvq"))
            follow("xo", unit_squares)
            act.wait_ge(sem("ss"), 16)
            row_squares("r2", x_tok, [("x_post1", 1), ("x_post1", 2)])
            gains("t_r2", col("ng")[:, 32:40])
            ffn("ffn2", "f2", second=True)
            for t in range(NT):
                if t == 0:
                    act.wait_ge(sem("rows_done"), 3)
                else:
                    act.wait_ge(sem("w_used"), NUNITS)
                for h in range(2):
                    act.activation(junk[t][:, h * 512:(h + 1) * 512], ps[:, 4 + 2 * t + h, :], ACT.Square,
                                   accum_out=ssum[:, t, h:h + 1]).then_inc(sem("ss"), 1)

        @block.vector
        def _(dve):
            def stt(out, in0, scalar, in1, op0, op1):
                return dve.scalar_tensor_tensor(out=out, in0=in0, scalar=scalar, in1=in1, op0=op0, op1=op1)

            chain = [0]
            ss_before = [0]

            def link(ins):
                chain[0] += 1
                ins.then_inc(sem("dve_chain"), 1)
                dve.wait_ge(sem("dve_chain"), chain[0])

            def follow(phase, evacuate):
                def one(u, j, i):
                    dve.wait_ge(sem("w_used"), u.count(1))
                    evacuate(j, i)
                    if j < UNITS[phase] - 1:
                        next_lo(dve, u)

                run_units(dve, phase, one)

            def unit_with(phase, evacuate):
                def unit(j, between=None):
                    u = Unit(FIRST[phase] + j)
                    dve.wait_ge(sem("w_used"), u.count(1))
                    evacuate(j, None)
                    if between:
                        between()
                    next_lo(dve, u)
                return unit

            def v_out(phase, j, pair):
                src = ps[:, bank(phase, j), :].rearrange("p (t h d) -> p t h d", t=NT, h=2)
                for t in range(NT):
                    mm = dve.tensor_copy(qkv[:, 2 * pair:2 * pair + 2, 512 + t * P:512 + (t + 1) * P], src[:, t])
                mm.then_inc(sem("bank_free"), 1)

            def qkv_out(phase):
                def out(j, i):
                    if j % 3 == 2:
                        v_out(phase, j, j // 3)
                    else:
                        dve.tensor_copy(qkv[:, 2 * (j // 3) + j % 3, 0:512], ps[:, bank(phase, j), :]).then_inc(sem("bank_free"), 1)
                return out

            def rotate(h):
                dve.wait_ge(sem("rot_done"), h + 1)
                if h:
                    dve.wait_ge(sem("rot_add"), h)
                dve.tensor_tensor(rot_t[:, :, :], ps[:, 7, :].rearrange("p (a s) -> p a s", a=2),
                                  rope_s[:, None, :].to_broadcast([P, 2, S]), ALU.mult).then_inc(sem("rot_read"), 1)
                dve.wait_ge(sem("rot_read"), h + 1)
                dve.wait_ge(sem("rot_cos"), h + 1)
                both = qkv[:, h, 0:512].rearrange("p (a s) -> p a s", a=2)
                dve.tensor_tensor(both, both, rot_t[:, :, :], ALU.add).then_inc(sem("rot_add"), 1)

            def convert_after(phase):
                next_lo(dve, Unit(last_unit(phase) - 1))

            def lows(stage, lo=aT_lo, hi=aT_hi, g=None, offset=None):
                def whole(b):
                    dve.wait_ge(sem("transposed"), t_count(stage, 4, b + 1))
                    for k in (2 * b, 2 * b + 1):
                        c = (k % 2) * S
                        dve.tensor_scalar(vT[:, k, :], ps[:, 4 + b, c:c + S], g[:, k:k + 1], offset[:, k:k + 1], ALU.mult, ALU.add)\
                           .then_inc(sem("whole_dve"), 1)

                for b in range(4):
                    if offset is not None and b % 2 == 0:
                        whole(b + 1)
                    dve.wait_ge(sem("split_hi"), t_count(stage, 8, 2 * b + 2))
                    both = slice(2 * b, 2 * b + 2)
                    if offset is not None:
                        dve.tensor_tensor(lo[:, both, :], vT[:, both, :], hi[:, both, :], ALU.subtract).then_inc(sem("split"), 1)
                    elif g is None:
                        dve.tensor_tensor(lo[:, both, :], ps[:, 4 + b, :].rearrange("p (c s) -> p c s", c=2), hi[:, both, :],
                                          ALU.subtract).then_inc(sem("split"), 1)
                    else:
                        for k in (2 * b, 2 * b + 1):
                            c = (k % 2) * S
                            mm = stt(lo[:, k, :], ps[:, 4 + b, c:c + S], g[:, k:k + 1], hi[:, k, :], ALU.mult, ALU.subtract)
                        mm.then_inc(sem("split"), 1)

            def attention(tag, kind, n, unit):
                maps = 1 if kind == "xa" else 2
                npt = 1 if kind == "diff" else maps
                causal = kind in ("diff", "fox")
                q_cols = [(0, 128), (128, 256)] if causal else [(0, 256), (256, 256)]
                scale = 1 / 16 if kind == "xa" else 1 / 8
                base = ATT0[tag]
                out_hi, out_lo = {"na": (yb_hi, yb_lo), "xa": (ox_hi, ox_lo)}.get(kind, (oT_hi, oT_lo))

                def maxima(u):
                    p = u % 2
                    if u > 1:
                        dve.wait_ge(sem("att_pt"), base["pt"] + (u - 1) * npt)
                    for m in range(maps):
                        dve.wait_ge(sem("att_sc"), base["sc"] + u * maps + m + 1)
                        if kind in ("fox", "na") and m == 0:
                            dve.wait_ge(sem("mask_ready"), (0 if kind == "fox" else 8) + u + 1)
                        for t in range(NT):
                            c0, n_k = q_cols[t]
                            src, to, top = ps[:, 4 + m, c0:c0 + n_k], pb[p][:, m, c0:c0 + n_k], mx[p][:, 2 * m + t:2 * m + t + 1]
                            if kind == "xa":
                                mm = dve.tensor_scalar(to, src, 1.0, None, ALU.mult, ALU.max, accum_out=top)
                            else:
                                add = col("cmask")[:, c0:c0 + n_k] if kind == "diff" else mc[p][:, m, c0:c0 + n_k]
                                mm = dve.tensor_tensor_reduce(out=to, in0=src, in1=add, scale=1.0, scalar=-3e38,
                                                              op0=ALU.add, op1=ALU.max, accum_out=top)
                            mm.then_inc(sem("att_sc_read"), 1)
                    dve.wait_ge(sem("att_sc_read"), base["sc_read"] + (u + 1) * 2 * maps)
                    dve.tensor_scalar(nb[p][:, 0:2 * maps], mx[p][:, 0:2 * maps], -scale, None, ALU.mult)\
                       .then_inc(sem("att_nb"), 1)

                def normalise_rows(u):
                    p = u % 2
                    dve.wait_ge(sem("att_ex"), base["ex"] + (u + 1) * 2 * maps)
                    dve.reciprocal(rs[p][:, 0:2 * maps], sm[p][:, 0:2 * maps]).then_inc(sem("att_rs"), 1)
                    dve.wait_ge(sem("att_rs"), base["rs"] + u + 1)
                    if kind == "diff":
                        dve.tensor_scalar(rs[p][:, 2:4], rs[p][:, 2:4], lam[:, 2:3], None, ALU.mult)\
                           .then_inc(sem("att_rl"), 1)
                        dve.wait_ge(sem("att_rl"), base["rl"] + u + 1)
                        for t in range(NT):
                            c0, n_k = q_cols[t]
                            row = pb[p][:, 1, c0:c0 + n_k]
                            dve.tensor_scalar(row, row, rs[p][:, 2 + t:3 + t], None, ALU.mult).then_inc(sem("att_p2"), 1)
                        dve.wait_ge(sem("att_p2"), base["p2"] + 2 * u + 2)
                        for t in range(NT):
                            c0, n_k = q_cols[t]
                            row = pb[p][:, 0, c0:c0 + n_k]
                            mm = stt(row, row, rs[p][:, t:t + 1], pb[p][:, 1, c0:c0 + n_k], ALU.mult, ALU.add)
                    else:
                        for m in range(maps):
                            for t in range(NT):
                                c0, n_k = q_cols[t]
                                row = pb[p][:, m, c0:c0 + n_k]
                                mm = dve.tensor_scalar(row, row, rs[p][:, 2 * m + t:2 * m + t + 1], None, ALU.mult)
                    mm.then_inc(sem("att_pn"), 1)

                def over_root(u):
                    dve.wait_ge(sem("att_or"), base["or"] + u + 1)
                    if u:
                        dve.wait_ge(sem("att_o_read"), base["o_read"] + u)
                    stt(o_v[:, :], ps[:, 2 + u % 2, 0:S], sub_g[:, 0:1], o_r[:, :], ALU.mult, ALU.mult)\
                        .then_inc(sem("att_ov"), 1)

                def outputs(u):
                    ob = ps[:, 2 + u % 2, :]
                    if kind == "diff":
                        src = o_v[:, :]
                    elif kind != "xa":
                        src = ob[:, 0:S]
                    dve.wait_ge(sem("att_o_hi"), base["o_hi"] + u + 1)
                    if kind == "xa":
                        to = slice(2 * u, 2 * u + 2)
                        dve.tensor_tensor(out_lo[:, to, :], ob.rearrange("p (a b) -> p a b", a=2), out_hi[:, to, :], ALU.subtract)\
                           .then_inc(sem("att_o_read"), 1)
                    else:
                        dve.tensor_tensor(out_lo[:, u, :], src, out_hi[:, u, :], ALU.subtract).then_inc(sem("att_o_read"), 1)

                def alongside(parts):
                    n_ = 0
                    while n_ < len(parts):
                        what, j = parts[n_]
                        turn = parts[n_ + 1][1] if what == "u" and n_ + 1 < len(parts) and parts[n_ + 1][0] == "r" else None
                        if what == "r":
                            rotate(j)
                        elif turn is None:
                            unit(j)
                        else:
                            unit(j, between=lambda: rotate(turn))
                            n_ += 1
                        n_ += 1

                for step, (first, second) in enumerate(ALONGSIDE[tag]):
                    if step < n:
                        maxima(step)
                    if step >= 2 and kind == "diff":
                        over_root(step - 2)
                    if step < n:
                        normalise_rows(step)
                    if step >= 2:
                        outputs(step - 2)
                    alongside(first + second)

            def statistics(t, h):
                return dve.bn_stats(stat[:, t, h, :], nrm[:, t, h * S:(h + 1) * S])

            def residual(j, i):
                cs = slice(j * S, (j + 1) * S)
                link(stt(nrm[:, :, cs], x_tok[:, :, cs], ALPHA, ps[:, j % 2, :].rearrange("p (t s) -> p t s", t=NT),
                         ALU.mult, ALU.add))
                statistics(0, j)
                statistics(1, j).then_inc(sem("bank_free"), 1)

            def residual_ffn(n):
                for t in range(NT):
                    if t == 0:
                        dve.wait_ge(sem("rows_done"), n + 1)
                    else:
                        dve.wait_ge(sem("w_used"), last_unit(f"ffn{n}"))
                    for h in range(2):
                        cs = slice(h * 512, (h + 1) * 512)
                        mm = stt(nrm[:, t, cs], x_tok[:, t, cs], ALPHA, ps[:, 4 + 2 * t + h, :], ALU.mult, ALU.add)
                    link(mm)
                    for h in range(4):
                        mm = statistics(t, h)
                mm.then_inc(sem("acc_read"), 1)

            def normalise(src, mean):
                for b in range(4):
                    cs = slice(b * S, (b + 1) * S)
                    for t in range(NT):
                        if mean:
                            mm = dve.tensor_scalar(nrm[:, t, cs], src[:, t, cs], mv[:, t, 0:1], rstd[:, t:t + 1], ALU.subtract, ALU.mult)
                        else:
                            mm = dve.tensor_scalar(nrm[:, t, cs], src[:, t, cs], rstd[:, t:t + 1], None, ALU.mult)
                        mm.then_inc(sem("src"), 1)

            def layer_norm(tag, needed):
                dve.wait_ge(*needed)
                for t in range(NT):
                    mm = dve.bn_aggr(mv[:, t, :], stat[:, t, :, :])
                mm.then_inc(sem("mv"), 1)
                dve.wait_ge(sem("rstd_" + tag), 1)
                normalise(nrm, True)

            def scaled(j, i):
                cs = slice(j * S, (j + 1) * S)
                dve.wait_ge(sem("ss"), ss_before[0] + 2 * j + 2)
                dve.tensor_tensor(nrm[:, :, cs], ps[:, j % 2, :].rearrange("p (t s) -> p t s", t=NT),
                                  gmap[:, None, cs].to_broadcast([P, NT, S]), ALU.mult).then_inc(sem("bank_free"), 1)

            def post_norm(tag, done, n_ss, needed):
                dve.tensor_reduce(ssq[:, :], ssum[:, :, 0:n_ss], AX, ALU.add).then_inc(sem("sq_" + tag), 1)
                dve.wait_ge(sem("rstd_" + tag), 1)
                dve.wait_ge(*needed)
                for t in range(NT):
                    stt(x_tok[:, t, :], nrm[:, t, :], rstd[:, t:t + 1], x_tok[:, t, :], ALU.mult, ALU.add).then_inc(sem(done), 1)

            def pre_norm(tag):
                dve.wait_ge(sem("rstd_" + tag), 1)
                normalise(x_tok, False)

            def ffn(phase, tag, second=False):
                g0 = FIRST[phase]
                w = col("conv" + tag[1])
                cols = 12 if second else 8

                def iteration(u, k, i=None, third=True):
                    q = k % 2
                    K = lambda n, more=0: per_iteration(k, i, n, more)
                    gb, ub = bank(phase, 2 * k), bank(phase, 2 * k + 1)

                    def side_taps(buf, b, at_, signal):
                        for back in (True, False):
                            for c in range(2):
                                tap = w[:, bass.ds(K(cols, 6 * c + at_ + (0 if back else 2)), 1)]
                                dst = buf[q][:, c, 1:S] if back else buf[q][:, c, 0:S - 1]
                                src = ps[:, b, c * S:c * S + S - 1] if back else ps[:, b, c * S + 1:c * S + S]
                                last = not back and c == 1
                                stt(dst, src, tap, dst, ALU.mult, ALU.add).then_inc(sem("bank_free" if last else "ffn_" + signal), 1)
                            if back:
                                dve.wait_ge(sem("ffn_" + signal), FFN0[tag][signal] + K(3, 2))

                    next_lo(dve, u)
                    dve.wait_ge(sem("ffn_fa"), FFN0[tag]["fa"] + K(2, 2))
                    if second:
                        side_taps(f_a, gb, 0, "fc")
                        c1 = math.sqrt(2 / math.pi)
                        dve.wait_ge(sem("ffn_fs"), FFN0[tag]["fs"] + K(1, 1))
                        dve.tensor_scalar(f_t[:, :, :], f_t[:, :, :], 0.044715 * c1, c1, ALU.mult, ALU.add)\
                           .then_inc(sem("ffn_fp"), 1)
                        dve.wait_ge(sem("ffn_fp"), FFN0[tag]["fp"] + K(1, 1))
                        dve.tensor_tensor(f_t[:, :, :], f_t[:, :, :], f_a[q][:, :, :], ALU.mult).then_inc(sem("ffn_fm"), 1)
                        next_lo(dve, u.plus(1))
                        dve.wait_ge(sem("ffn_fb"), FFN0[tag]["fb"] + K(2, 2))
                        side_taps(f_u, ub, 3, "fe")
                        dve.wait_ge(sem("ffn_ft"), FFN0[tag]["ft"] + K(1, 1))
                        stt(f_t[:, :, :], f_t[:, :, :], 1.0, f_a[q][:, :, :], ALU.add, ALU.mult).then_inc(sem("ffn_fd"), 1)
                        dve.wait_ge(sem("ffn_fd"), FFN0[tag]["fd"] + K(1, 1))
                        dve.wait_ge(sem("bank_free"), bank_value(phase, 2 * k + 2, i, body=4))
                        stt(f_v[:, :, :], f_t[:, :, :], 0.5, f_u[q][:, :, :], ALU.mult, ALU.mult).then_inc(sem("ffn_fv"), 1)
                    else:
                        for tap in (1, 0):
                            for c in range(2):
                                back = 2 - tap
                                dst = f_a[q][:, c, back:S]
                                stt(dst, ps[:, gb, c * S:c * S + S - back], w[:, bass.ds(K(cols, 4 * c + tap), 1)], dst,
                                    ALU.mult, ALU.add).then_inc(sem("bank_free" if tap == 0 and c == 1 else "ffn_fc"), 1)
                            if tap:
                                dve.wait_ge(sem("ffn_fc"), FFN0[tag]["fc"] + K(3, 2))
                        next_lo(dve, u.plus(1))
                        dve.wait_ge(sem("ffn_ft"), FFN0[tag]["ft"] + K(1, 1))
                        stt(f_t[:, :, :], f_t[:, :, :], 1.0, f_a[q][:, :, :], ALU.add, ALU.mult).then_inc(sem("ffn_fd"), 1)
                        dve.wait_ge(sem("ffn_fd"), FFN0[tag]["fd"] + K(1, 1))
                        dve.wait_ge(sem("w_used"), u.count(2))
                        stt(f_v[:, :, :], f_t[:, :, :], 0.5, ps[:, ub, :].rearrange("p (c s) -> p c s", c=2), ALU.mult, ALU.mult)\
                            .then_inc(sem("bank_free"), 1)
                    dve.wait_ge(sem("ffn_fh"), FFN0[tag]["fh"] + K(1, 1))
                    dve.tensor_tensor(hT_lo[q][:, :, :], f_v[:, :, :], hT_hi[q][:, :, :], ALU.subtract)\
                       .then_inc(sem("ffn_h"), 1)
                    if third:
                        next_lo(dve, u.plus(2))

                ffn_iterations(dve, g0, iteration, lambda u: None)

            MAGIC = 1.5 * 2.0 ** 23
            TWO_PI = [6.28125, 0.0019350051879882812, 3.0199159819e-07]
            assert abs(sum(TWO_PI) - 2 * math.pi) < 1e-15

            def reduce_angle(x, k, out):
                link(dve.tensor_scalar(k, x, 1 / (2 * math.pi), MAGIC, ALU.mult, ALU.add))
                link(dve.tensor_scalar(k, k, MAGIC, None, ALU.subtract))
                for part in TWO_PI:
                    link(stt(x, k, -part, x, ALU.mult, ALU.add))
                return dve.tensor_scalar(out, x, 3.1415925, -3.1415925, ALU.min, ALU.max)

            lows("t_x")
            convert_lo(dve, Unit(0))
            dve.wait_ge(sem("cst_loaded"), 16)
            dve.wait_ge(sem("pos_loaded"), 16)
            link(dve.tensor_scalar(ang[:, :], pos_i[:, :], col("invf"), None, ALU.mult))
            reduce_angle(ang[:, :], ang_k[:, :], ang[:, :]).then_inc(sem("ang_red"), 1)
            dve.wait_ge(sem("lam_loaded"), 16)
            for n in range(2):
                dve.tensor_tensor_reduce(out=lam_j[:, n, :], in0=lam_in[:, 2 * n, :], in1=lam_in[:, 2 * n + 1, :], scale=1.0,
                                         scalar=0.0, op0=ALU.mult, op1=ALU.add, accum_out=lam[:, n:n + 1])\
                   .then_inc(sem("lam_dot"), 1)
            convert_lo(dve, Unit(1))
            unit = unit_with("l0_qkv", qkv_out("l0_qkv"))
            dve.wait_ge(sem("lam_exp"), 1)
            dve.tensor_scalar(lam[:, 2:3], lam[:, 1:2], lam[:, 0:1], -LAMBDA_INIT, ALU.subtract, ALU.add)\
               .then_inc(sem("lam_ready"), 1)
            dve.tensor_scalar(sub_g[:, :], col("subg"), 1.0 - LAMBDA_INIT, None, ALU.mult).then_inc(sem("lam_ready"), 1)
            dve.wait_ge(sem("rope"), 3)
            unit(0, between=lambda: rotate(0))
            dve.wait_ge(sem("lam_ready"), 2)
            attention("att0", "diff", 8, unit)
            follow("l0_wo", residual)
            layer_norm("ln0", (sem("bank_free"), BANK0["ffn0"]))
            lows("t_ln0", g=col("ln1g")[:, 0:8], offset=col("ln1b")[:, 0:8])
            convert_after("l0_wo")
            dve.wait_ge(sem("fw_hi"), 1)
            dve.tensor_tensor(fw_lo[:, :, :], fw[:, :, :], fw_hi[:, :, :], ALU.subtract).then_inc(sem("fw_split"), 1)
            ffn("ffn0", "f0")
            dve.wait_ge(sem("x_new1"), 2)
            residual_ffn(0)
            layer_norm("ln1", (sem("acc_read"), 1))
            lows("t_ln1", g=col("ln2g")[:, 0:8], offset=col("ln2b")[:, 0:8])
            convert_after("ffn0")
            link(dve.memset(f_ones[:, :], 1.0))
            unit = unit_with("l1_qkv", qkv_out("l1_qkv"))
            dve.wait_ge(sem("f_done"), 1)
            dve.tensor_tensor(f_tok[:, :, :], ps[:, 4, 0:32].rearrange("p (t h) -> p t h", t=NT),
                              f_b[:, None, :].to_broadcast([P, NT, 16]), ALU.add).then_inc(sem("f_tok"), 1)
            unit(0)
            dve.wait_ge(sem("f_done"), 2)
            dve.tensor_copy(f_z[:, :], ps[0:16, 5, 0:S]).then_inc(sem("f_z"), 1)
            dve.tensor_scalar(f_min[:, :], ps[0:16, 5, 0:S], 0.0, None, ALU.min).then_inc(sem("f_min"), 1)
            dve.wait_ge(sem("f_min"), 1)
            dve.wait_ge(sem("f_act"), 3)
            link(dve.tensor_tensor(f_min[:, :], f_min[:, :], f_abs[:, :], ALU.subtract))
            dve.tensor_tensor_scan(f_cum[:, :], f_ones[:, :], f_min[:, :], 0.0, ALU.mult, ALU.add).then_inc(sem("f_cum"), 1)
            unit(1)
            attention("att1", "fox", 8, unit)
            dve.wait_ge(sem("x_new2"), 2)
            follow("l1_wo", residual)
            layer_norm("ln2", (sem("bank_free"), BANK0["ffn1"]))
            lows("t_ln2", g=col("ln1g")[:, 8:16], offset=col("ln1b")[:, 8:16])
            convert_after("l1_wo")
            ffn("ffn1", "f1")
            dve.wait_ge(sem("x_new3"), 2)
            residual_ffn(1)
            dve.wait_ge(sem("acc_read"), 2)
            for t in range(NT):
                mm = dve.bn_aggr(mv[:, t, :], stat[:, t, :, :])
            mm.then_inc(sem("mv"), 1)
            dve.wait_ge(sem("mv"), 4)
            dve.wait_ge(sem("maps_loaded"), 16 * 8)
            for t in range(NT):
                link(stt(nrm[:, t, :], nrm[:, t, :], mv[:, t, 0:1], gmap[:, :], ALU.subtract, ALU.mult))
                if t == 0:
                    dve.wait_ge(sem("rstd_ln3"), 1)
                stt(x_tok[:, t, :], nrm[:, t, :], rstd[:, t:t + 1], bmap[:, :], ALU.mult, ALU.add).then_inc(sem("x_new4"), 1)
            dve.wait_ge(sem("x_new4"), 2)
            pre_norm("r0")
            lows("t_r0", g=col("ng")[:, 0:8])
            convert_after("ffn1")
            dve.wait_ge(sem("hin_loaded"), 16 * 6)

            def filter_layer(layer):
                dve.wait_ge(sem("h_pe"), layer + 1)
                link(dve.tensor_scalar(h_a[:, :], ps[0:64, 4 + layer, 0:S], col("hb1" if layer == 0 else "hb2")[0:64, :],
                                       col("hf1" if layer == 0 else "hf2")[0:64, :], ALU.add, ALU.mult))
                if layer:
                    dve.wait_ge(sem("h_sin"), 1)
                reduce_angle(h_a[:, :], h_k[:, :], h_k[:, :]).then_inc(sem("h_red"), 1)

            def filter_taps(o, t):
                n = 2 * o + t
                dve.wait_ge(sem("h_pe"), 3 + n)
                if n == 2:
                    dve.wait_ge(sem("spec_pe"), 4)
                if n:
                    dve.wait_ge(sem("h_mix"), 2 * n)
                link(dve.tensor_tensor(h_t[:, :], ps[:, 4, :], decay[:, 0, t, :], ALU.mult))
                link(dve.tensor_tensor(h_u[:, :], ps[:, 5, :], decay[:, 1, t, :], ALU.mult))
                dve.tensor_tensor(h_s[:, 0, t, :], h_t[:, :], h_u[:, :], ALU.add).then_inc(sem("h_mix"), 1)
                dve.tensor_tensor(h_s[:, 1, t, :], h_t[:, :], h_u[:, :], ALU.subtract).then_inc(sem("h_mix"), 1)

            def hysc_out(j, i):
                dve.tensor_copy(hysc[:, 2 * j:2 * j + 2, :], ps[:, bank("hysc", j), :].rearrange("p (c s) -> p c s", c=2))\
                   .then_inc(sem("bank_free"), 1)

            unit = unit_with("hysc", hysc_out)
            for j in range(12):
                unit(j)
                for what, *args in FILTERS_ALONGSIDE.get(j, []):
                    if what != "spectrum":
                        {"layer": filter_layer, "taps": filter_taps}[what](*args)
            dve.wait_ge(sem("h_mix"), 8)

            def na_out(j, i):
                if j < 4:
                    kind, jj = j // 2, j % 2
                    dve.tensor_copy(qkv[:, 2 * jj:2 * jj + 2, kind * S:(kind + 1) * S],
                                    ps[:, bank("naqkv", j), :].rearrange("p (c s) -> p c s", c=2)).then_inc(sem("bank_free"), 1)
                else:
                    v_out("naqkv", j, j - 4)

            unit = unit_with("naqkv", na_out)
            dve.wait_ge(sem("spec_read"), 8)
            dve.wait_ge(sem("hy_conv"), 3)
            for o in range(2):
                src = z_s if o else hysc
                dve.wait_ge(sem("zf_pe"), o + 1)
                for f in range(2):
                    zr, zi = ps[:, 4 + f, :], ps[:, 6 + f, :]
                    kr, ki = spec[:, o, 0, f, :], spec[:, o, 1, f, :]
                    if f == 0 and o == 1:
                        dve.wait_ge(sem("yt_pe"), 1)
                    link(dve.tensor_tensor(y_f[:, 0, f, :], zr, kr, ALU.mult))
                    link(dve.tensor_tensor(y_t[:, :], zi, ki, ALU.mult))
                    link(dve.tensor_tensor(y_f[:, 0, f, :], y_f[:, 0, f, :], y_t[:, :], ALU.subtract))
                    link(dve.tensor_tensor(y_f[:, 1, f, :], zr, ki, ALU.mult))
                    link(dve.tensor_tensor(y_t[:, :], zi, kr, ALU.mult))
                    mm = dve.tensor_tensor(y_f[:, 1, f, :], y_f[:, 1, f, :], y_t[:, :], ALU.add)
                    if f == 0:
                        link(mm)
                mm.then_inc(sem("y_f"), 1)
                unit(3 * o)
                unit(3 * o + 1)
                dve.wait_ge(sem("yt_pe"), o + 1)
                for k in range(4):
                    mm = stt(cv[0][:, k, :], src[:, k, :], col("hyb")[:, 4 * o + k:4 * o + k + 1],
                             ps[:, 4 + k // 2, (k % 2) * S:(k % 2 + 1) * S], ALU.mult, ALU.add)
                link(mm)
                if o == 0:
                    dve.tensor_tensor(z_s[:, :, :], cv[0][:, :, :], hysc[:, 4:8, :], ALU.mult).then_inc(sem("z_ready"), 1)
                    dve.wait_ge(sem("z_ready"), 1)
                    unit(2)
                else:
                    dve.tensor_tensor(cv[1][:, :, :], cv[0][:, :, :], hysc[:, 8:12, :], ALU.mult).then_inc(sem("ya"), 1)
                    dve.wait_ge(sem("ya"), 1)
                    link(dve.tensor_copy(ya_hi[:, :, :], cv[1][:, :, :]))
                    link(dve.tensor_tensor(ya_lo[:, :, :], cv[1][:, :, :], ya_hi[:, :, :], ALU.subtract))

            unit(5)

            def gates_out(j, i):
                if j == 6:
                    dve.wait_ge(sem("yc_split"), 2)
                c = slice(2 * j, 2 * j + 2)
                dve.tensor_tensor(gates[:, c, :], ps[:, bank("gates", j), :].rearrange("p (c s) -> p c s", c=2),
                                  col("gateb")[:, c][:, :, None].to_broadcast([P, 2, S]), ALU.add)\
                   .then_inc(sem("bank_free"), 1)

            unit = unit_with("gates", gates_out)
            unit(0)
            attention("attn", "na", 4, unit)

            def merged_lo(half):
                for b in (2 * half, 2 * half + 1):
                    dve.wait_ge(sem("merged_hi"), b + 1)
                    stt(aT_lo[:, 2 * b:2 * b + 2, :], m_acc[:, 2 * b:2 * b + 2, :], 0.5, aT_hi[:, 2 * b:2 * b + 2, :],
                        ALU.mult, ALU.subtract).then_inc(sem("merged"), 1)

            dve.wait_ge(sem("gate_t"), 12)
            for j in range(6):
                u, half, br = Unit(FIRST["branch"] + j), j // 3, j % 3
                for b in range(2):
                    if b == 0:
                        dve.wait_ge(sem("branch_half"), j + 1)
                    else:
                        dve.wait_ge(sem("w_used"), u.count(1))
                    c = 4 * half + 2 * b
                    g = gates[:, 8 * br + c:8 * br + c + 2, :]
                    src = ps[:, branch_bank(j, b), :].rearrange("p (c s) -> p c s", c=2)
                    acc = m_acc[:, c:c + 2, :]
                    if br == 0:
                        stt(acc, g, 1.0, src, ALU.add, ALU.mult).then_inc(sem("bank_free"), 1)
                    else:
                        stt(m_t[:, :, :], g, 1.0, src, ALU.add, ALU.mult).then_inc(sem("bank_free"), 1)
                        dve.wait_ge(sem("bank_free"), BANK0["branch"] + 2 * j + b + 1)
                        mm = dve.tensor_tensor(acc, acc, m_t[:, :, :], ALU.add)
                        if br == 2 and b == 1:
                            mm.then_inc(sem("m_acc"), 1)
                            dve.wait_ge(sem("m_acc"), half + 1)
                        else:
                            link(mm)
                if j < 5:
                    next_lo(dve, u)
                if j == 3:
                    merged_lo(0)
                    dve.wait_ge(sem("rstd_mem"), 1)
                    for b in range(4):
                        cs = slice(b * S, (b + 1) * S)
                        for t in range(NT):
                            dve.tensor_scalar(mem_tok[:, t, cs], mem_tok[:, t, cs], mx[1][:, t:t + 1], None, ALU.mult)\
                               .then_inc(sem("src"), 1)
            merged_lo(1)
            convert_after("branch")
            lows("t_mem", memT_lo, memT_hi, g=col("memg"))
            dve.wait_ge(sem("maps_loaded"), 16 * 9)
            follow("wout", scaled)
            post_norm("p0", "x_post0", 4, (sem("bank_free"), BANK0["xkvq"]))
            convert_after("wout")

            def x_out(j, i):
                what, head = XKVQ[j]
                at_ = {"q": 0, "k": 512, "v": 1024}[what]
                dve.tensor_copy(xqkv[:, head, at_:at_ + 512], ps[:, bank("xkvq", j), :]).then_inc(sem("bank_free"), 1)

            unit = unit_with("xkvq", x_out)
            for j in range(3):
                unit(j)
            pre_norm("r1")
            unit(3)
            lows("t_r1", g=col("ng")[:, 16:24])
            unit(4)
            unit(5)
            attention("attx", "xa", 4, unit)
            dve.wait_ge(sem("maps_loaded"), 16 * 10)
            ss_before[0] = 8
            follow("xo", scaled)
            post_norm("p1", "x_post1", 4, (sem("bank_free"), BANK0["ffn2"]))
            pre_norm("r2")
            lows("t_r2", g=col("ng")[:, 32:40])
            convert_after("xo")
            ffn("ffn2", "f2", second=True)
            dve.wait_ge(sem("maps_loaded"), 16 * 11)
            for t in range(NT):
                for h in range(2):
                    dve.wait_ge(sem("ss"), 16 + 2 * t + h + 1)
                    cs = slice(h * 512, (h + 1) * 512)
                    dve.tensor_tensor(nrm[:, t, cs], ps[:, 4 + 2 * t + h, :], gmap[:, cs], ALU.mult).then_inc(sem("acc_read"), 1)
            post_norm("p2", "out_ready", 2, (sem("acc_read"), 2 + 4))

        @block.gpsimd
        def _(pool):
            chain = [0]

            def link(ins):
                chain[0] += 1
                ins.then_inc(sem("pool_chain"), 1)
                pool.wait_ge(sem("pool_chain"), chain[0])

            def load_map(dst, row):
                r = ROWS.index(row)
                pool.dma_start(dst[:, :], A["rows"][r:r + 1, :].to_broadcast([P, D])).then_inc(sem("maps_loaded"), 16)

            def inverse_root(tag, src, eps, scale=1.0, dst=None):
                dst = rstd if dst is None else dst
                link(pool.tensor_scalar(dst[:, 0:NT], src, scale, eps, ALU.mult, ALU.add))
                pool.tensor_tensor(dst[:, 0:NT], dst[:, 0:NT], mhalf[:, :], ALU.pow).then_inc(sem("rstd_" + tag), 1)

            def layer_norm(tag, n, maps, nxt):
                pool.wait_ge(sem("mv"), n)
                inverse_root(tag, mv[:, :, 1], 1e-5)
                pool.wait_ge(sem("maps_loaded"), 16 * maps)
                pool.wait_ge(sem("src"), 8 * n)
                for t in range(NT):
                    link(pool.tensor_tensor(x_tok[:, t, :], nrm[:, t, :], gmap[:, :], ALU.mult))
                    pool.tensor_tensor(x_tok[:, t, :], x_tok[:, t, :], bmap[:, :], ALU.add).then_inc(sem(f"x_new{n}"), 1)
                pool.wait_ge(sem(f"x_new{n}"), 2)
                for dst, row in zip((gmap, bmap), nxt):
                    load_map(dst, row)

            def fox_masks():
                base = ATT0["att1"]
                for u in range(8):
                    p = u % 2
                    if u > 1:
                        pool.wait_ge(sem("att_sc_read"), base["sc_read"] + 4 * (u - 1))
                    for m in range(2):
                        c = fox_c[:, 2 * u + m, :]
                        pool.tensor_tensor(mc[p][:, m, 0:P], col("cmask")[:, 0:P], c[:, 0:P], ALU.add)
                        mm = pool.tensor_tensor(mc[p][:, m, P:384], col("cmask")[:, P:384], c, ALU.add)
                    mm.then_inc(sem("mask_ready"), 1)

            def window_masks():
                base = ATT0["attn"]
                for u in range(4):
                    p = u % 2
                    if u > 1:
                        pool.wait_ge(sem("att_sc_read"), base["sc_read"] + 4 * (u - 1))
                    pool.dma_start(mc[p][:, :, :].rearrange("p m (t k) -> p (m t) k", t=NT),
                                   A["nabias"].rearrange("h (t q) k -> q (h t) k", q=P)[:, 4 * u:4 * u + 4, :])\
                        .then_inc(sem(f"bias_in{p}"), 16)
                    pool.wait_ge(sem(f"bias_in{p}"), 16 * (u // 2 + 1))
                    b4 = mc[p][:, :, :].rearrange("p m (t k) -> p (m t) k", t=NT)
                    link(pool.tensor_scalar(b4, b4, 8.0, 0.0, ALU.mult, ALU.add))
                    pool.tensor_tensor(b4, b4, col("namask")[:, None, :].to_broadcast([P, 4, S]), ALU.add)\
                        .then_inc(sem("mask_ready"), 1)

            link(pool.memset(mhalf[:, :], -0.5))
            pool.dma_start(pos_i[:, :], A["positions"].to_broadcast([P, S])).then_inc(sem("pos_loaded"), 16)
            pool.dma_start(lam_in[:, :, :].rearrange("p a b -> p (a b)"), A["lam"].to_broadcast([P, 256]))\
                .then_inc(sem("lam_loaded"), 16)
            pool.wait_ge(sem("rope"), 3)

            def cosines(h):
                pool.wait_ge(sem("rot_done"), h + 1)
                both = qkv[:, h, 0:512].rearrange("p (a s) -> p a s", a=2)
                pool.tensor_tensor(both, both, rope_c[:, None, :].to_broadcast([P, 2, S]), ALU.mult).then_inc(sem("rot_cos"), 1)

            cosines(0)
            pool.dma_start(fw[:, :, :], A["fw"]).then_inc(sem("fw_loaded"), 16)
            pool.dma_start(f_b[:, :], A["fb"].to_broadcast([P, 16])).then_inc(sem("fw_loaded"), 16)
            load_map(gmap, "ln1g0")
            load_map(bmap, "ln1b0")
            pool.dma_start(head_row[:, :, :], A["head_row"]).then_inc(sem("head_row"), 16)
            for h in range(1, 8):
                cosines(h)
            pool.dma_start(A["narep"], A["rpb"].to_broadcast([64, A["rpb"].shape[1]])).then_inc(sem("narep"), 16)
            layer_norm("ln0", 1, 2, ["ln2g0", "ln2b0"])
            layer_norm("ln1", 2, 4, ["ln1g1", "ln1b1"])
            pool.wait_ge(sem("narep"), 16)
            for h in range(8):
                for r in range(4):
                    src = bass.AP(tensor=A["narep"].tensor, offset=(h * 7 + 3 - r) * 127 + 63,
                                  ap=[[A["rpb"].shape[1] - 1, 64], [127, 4], [1, 64]])
                    pool.dma_start(A["nabias"][h, r * 64:(r + 1) * 64, :].rearrange("q (a b) -> q a b", a=4), src)\
                        .then_inc(sem("nabias"), 16)
            pool.wait_ge(sem("fox_c"), 8)
            fox_masks()
            pool.wait_ge(sem("att_o"), ATT0["att1"]["o"] + 8)
            for dst, src in ((hw1, "hw1"), (hw2, "hw2"), (hw3, "hw3")):
                pool.dma_start(dst[:, :], A[src]).then_inc(sem("hin_loaded"), 16)
            layer_norm("ln2", 3, 6, ["ln2g1", "ln2b1"])
            pool.wait_ge(sem("w_used"), FIRST["ffn1"])
            pool.dma_start(decay[:, :, :, :], A["decay"]).then_inc(sem("hin_loaded"), 16)
            pool.wait_ge(sem("mv"), 4)
            inverse_root("ln3", mv[:, :, 1], 1e-5)
            pool.wait_ge(sem("x_new4"), 2)
            pool.dma_start(dft[:, :, :, :], A["dft"]).then_inc(sem("hin_loaded"), 16)
            pool.wait_ge(sem("w_used"), FIRST["hysc"])
            pool.dma_start(zembT[:, :], A["zembT"]).then_inc(sem("hin_loaded"), 16)
            pool.wait_ge(sem("sq_r0"), 2)
            inverse_root("r0", ssq[:, :], 1e-6, 1 / D)

            def short(first, name, w0, src, buf):
                x = src[:, first:first + 4, :]
                t3 = col(name).rearrange("p (k j) -> p k j", j=3)

                def tap(j, n):
                    return t3[:, w0:w0 + 4, j][:, :, None].to_broadcast([P, 4, n])

                a, b = buf
                link(pool.tensor_tensor(a[:, :, :], x, tap(1, S), ALU.mult))
                link(pool.tensor_tensor(b[:, :, 1:S], x[:, :, 0:S - 1], tap(0, S - 1), ALU.mult))
                link(pool.tensor_tensor(a[:, :, 1:S], a[:, :, 1:S], b[:, :, 1:S], ALU.add))
                link(pool.tensor_tensor(b[:, :, 0:S - 1], x[:, :, 1:S], tap(2, S - 1), ALU.mult))
                link(pool.tensor_tensor(x[:, :, 0:S - 1], a[:, :, 0:S - 1], b[:, :, 0:S - 1], ALU.add))
                return pool.tensor_copy(x[:, :, S - 1:S], a[:, :, S - 1:S])

            for n in range(3):
                pool.wait_ge(sem("bank_free"), BANK0["hysc"] + 2 * (n + 1))
                short(4 * n, "hyw", 4 * n, hysc, cv).then_inc(sem("hy_conv"), 1)
                pool.wait_ge(sem("hy_conv"), n + 1)
            pool.wait_ge(sem("bank_free"), BANK0["naqkv"])
            pool.wait_ge(sem("spec_pe"), 8)
            link(pool.tensor_tensor(hysc[:, 16:20, :], hysc[:, 16:20, :], hysc[:, 20:24, :], ALU.mult))
            link(short(16, "scw", 0, hysc, cp))
            link(pool.tensor_tensor(hysc[:, 16:20, :], hysc[:, 16:20, :], hysc[:, 12:16, :], ALU.mult))
            pool.wait_ge(sem("ya"), 1)
            pool.tensor_copy(yc_hi[:, :, :], hysc[:, 16:20, :]).then_inc(sem("yc_split"), 1)
            pool.wait_ge(sem("yc_split"), 1)
            pool.tensor_tensor(yc_lo[:, :, :], hysc[:, 16:20, :], yc_hi[:, :, :], ALU.subtract).then_inc(sem("yc_split"), 1)
            pool.wait_ge(sem("nabias"), 16 * 32)
            load_map(gmap, "ng1")
            window_masks()
            pool.wait_ge(sem("att_o"), ATT0["attn"]["o"] + 4)
            pool.dma_start(mem_tok[:, :, :], A["mem"].rearrange("(t p) d -> p t d", p=P)).then_inc(sem("mem_loaded"), 16)
            pool.wait_ge(sem("sq_mem"), 2)
            inverse_root("mem", mx[0][:, 0:NT], 1e-6, 1 / D, dst=mx[1])
            pool.wait_ge(sem("sq_p0"), 1)
            inverse_root("p0", ssq[:, :], 1e-6, 1 / D)
            pool.wait_ge(sem("x_post0"), 2)
            load_map(gmap, "ng3")
            pool.wait_ge(sem("sq_r1"), 2)
            inverse_root("r1", ssq[:, :], 1e-6, 1 / D)
            pool.wait_ge(sem("sq_p1"), 1)
            inverse_root("p1", ssq[:, :], 1e-6, 1 / D)
            pool.wait_ge(sem("x_post1"), 2)
            load_map(gmap, "ng5")
            pool.wait_ge(sem("sq_r2"), 2)
            inverse_root("r2", ssq[:, :], 1e-6, 1 / D)
            pool.wait_ge(sem("sq_p2"), 1)
            inverse_root("p2", ssq[:, :], 1e-6, 1 / D)


def b_units(w):
    n = w.shape[1]
    return w.reshape(KC, P, n // 256, 256).transpose(2, 1, 0, 3).reshape(n // 256, P, UNIT)


def qkv_units(w):
    q, k, v = (w[:, j * D:(j + 1) * D].reshape(D, KC, P) for j in range(3))
    seq = []
    for j in range(0, KC, 2):
        seq += [q[:, j], k[:, j], q[:, j + 1], k[:, j + 1], v[:, j], v[:, j + 1]]
    return b_units(np.concatenate(seq, 1))


def xkvq_units(w_q, w_kv):
    q, k, v = b_units(w_q), b_units(w_kv[:, :D]), b_units(w_kv[:, D:])
    return np.stack([{"q": q, "k": k, "v": v}[what][head] for what, head in XKVQ])


def ffn_units(w_in, w_out):
    gate, up = b_units(w_in[:, :DFF]), b_units(w_in[:, DFF:])
    down = w_out.reshape(FI, 2, P, D).transpose(0, 2, 1, 3).reshape(FI, P, UNIT)
    seq = [gate[0], up[0], gate[1], up[1], down[0]]
    for k in range(2, FI):
        seq += [gate[k], up[k], down[k - 1]]
    return np.stack(seq + [down[FI - 1]])


def branch_units(w):
    return w.reshape(3, 4, P, 2, 512).transpose(3, 0, 2, 1, 4).reshape(6, P, UNIT)


def constants():
    f = np.float32
    out = {"ident": np.eye(P, dtype=f), "mean": np.full((P, P), 1 / P, f)}
    rot = np.zeros((P, P), f)
    for base in (0, 64):
        for j in range(8):
            rot[base + j, base + 8 + j] = -1
            rot[base + 8 + j, base + j] = 1
    out["rotT"] = rot.T
    tri = np.where(np.arange(P)[None, :] <= np.arange(P)[:, None], 0, NEG).astype(f)
    out["cmask"] = np.concatenate([tri, np.zeros((P, P), f), tri], 1)
    c = np.arange(64)
    start = np.clip(c - 8, 0, 48)
    win = np.where((c[None, :] >= start[:, None]) & (c[None, :] < start[:, None] + 16), 0, NEG).astype(f)
    out["namask"] = np.tile(win, (2, 4))
    inv = 500000.0 ** (-np.arange(0, 16, 2) / 16)
    invf = np.zeros((P, 1), f)
    for base in (0, 64):
        invf[base:base + 8, 0] = invf[base + 8:base + 16, 0] = inv
    out["invf"] = invf
    out["eps_rms"] = np.full((P, 1), 1e-6, f)
    out["halfpi"] = np.full((P, 1), np.pi / 2, f)
    return out


def fourier():
    j, q = np.arange(S)[:, None], np.arange(S)[None, :] + 0.5
    th = 2 * np.pi * j * q / (2 * S)
    m = [np.cos(th), -np.sin(th), np.cos(th).T / S, -np.sin(th).T / S]
    return np.stack([x.reshape(2, P, S).transpose(1, 0, 2) for x in m], 1).astype(np.float32)


def filter_inputs():
    L = S
    t = np.linspace(0.0, 1.0, L)[:, None]
    w = 2.0 * np.pi * np.arange(L)[:, None] / L
    f = np.linspace(1e-4, 15, 16)[None, :]
    z = np.concatenate([t, np.cos(f * w), -np.sin(f * w)], 1)
    deltas = np.abs(np.linspace(np.log(1e-2) / 1.5, np.log(1e-2) / 0.3, 512))
    dec = np.exp(-t * deltas)
    back = dec.copy()
    back[0] = 0
    d = np.stack([x.reshape(2, P, 512).transpose(1, 0, 2) for x in (dec, back)], 1)
    return np.ascontiguousarray(z.T).astype(np.float32), d.astype(np.float32)


def cols_of(v):
    return v.reshape(-1, P).T


def kernel(**a):
    import concourse.bacc as _bacc
    from concourse import mybir as _mybir
    from concourse.bass_utils import run_bass_kernel_spmd as _run

    a = {k: np.asarray(x) for k, x in a.items()}
    w_in = a["w_in_2"][0]
    hy, na, sc, ga = w_in[:, :1536], w_in[:, 1536:3072], w_in[:, 3072:4608], w_in[:, 4608:]
    fox = a["fox_w_in"][0]
    stream = np.concatenate([
        qkv_units(a["diff_w_qkv"][0]), b_units(a["diff_w_o"][0]), ffn_units(a["ffn_w_in"][0], a["ffn_w_out"][0]),
        qkv_units(fox[:, :3072]), b_units(a["fox_w_o"][0]), ffn_units(a["ffn_w_in"][1], a["ffn_w_out"][1]),
        b_units(hy), b_units(sc), b_units(na), b_units(ga), branch_units(a["w_branch_2"][0]), b_units(a["w_out_2"][0]),
        xkvq_units(a["xa_wq_2"][0], a["xa_wkv_2"][0]), b_units(a["xa_wo_2"][0]),
        ffn_units(a["ffn_up_2"][0], a["ffn_down_2"][0])])
    assert stream.shape == (NUNITS, P, UNIT)

    con = constants()
    con.update(ln1g=cols_of(a["ln1_g"]), ln1b=cols_of(a["ln1_b"]), ln2g=cols_of(a["ln2_g"]), ln2b=cols_of(a["ln2_b"]),
               ng=cols_of(a["norm_gains_2"][0]), memg=cols_of(a["mem_norm_2"][0]),
               hyw=a["hy_short_w_2"][0].reshape(3, 12, P).transpose(2, 1, 0).reshape(P, 36),
               hyb=cols_of(a["hy_bias_2"][0]), scw=a["sc_conv_w_2"][0].reshape(3, 4, P).transpose(2, 1, 0).reshape(P, 12),
               gateb=cols_of(a["gate_bias_2"][0]), subg=cols_of(a["diff_subln_g"][0]))
    for l in range(2):
        w = np.concatenate([a["ffn_conv_w"][l], a["ffn_conv_b"][l][None]])
        con[f"conv{l}"] = w.reshape(4, 2 * FI, P).transpose(2, 1, 0).reshape(P, 8 * FI)
    w = a["ffn_conv_2"][0].reshape(3, 2, 2 * FI, P)
    con["conv2"] = w.transpose(3, 2, 1, 0).reshape(P, 12 * FI)
    for name, src in (("hb1", a["hy_b1_2"][0]), ("hb2", a["hy_b2_2"][0]), ("hf1", a["hy_freq_2"][0, 0]),
                      ("hf2", a["hy_freq_2"][0, 1])):
        con[name] = np.concatenate([src, np.zeros(64, np.float32)])[:, None]
    cst = np.concatenate([con[n] for n in COLS], 1).astype(np.float32)
    assert cst.shape == (P, NCOLS)

    rows = np.stack([a["ln1_g"][0], a["ln1_b"][0], a["ln2_g"][0], a["ln2_b"][0], a["ln1_g"][1], a["ln1_b"][1],
                     a["ln2_g"][1], a["ln2_b"][1]] + [a["norm_gains_2"][0, n] for n in (1, 3, 5)])
    zembT, decay = filter_inputs()
    arrays = {
        "x": a["x"][0], "positions": a["positions"].reshape(1, S), "mem": a["mem_2"][0], "wstream": stream, "cst": cst,
        "rows": rows,
        "lam": np.concatenate([a["diff_lambda_q1"], a["diff_lambda_k1"], a["diff_lambda_q2"], a["diff_lambda_k2"]], 1),
        "fw": fox[:, 3072:].reshape(KC, P, 16).transpose(1, 0, 2), "fb": a["fox_b_f"],
        "rpb": np.pad(a["na_rpb_2"][0][:, 4:11], ((0, 0), (0, 0), (48, 48))).reshape(1, -1),
        "zembT": zembT, "hw1": a["hy_w1_2"][0], "hw2": a["hy_w2_2"][0], "hw3": a["hy_w3_2"][0], "decay": decay,
        "dft": fourier(), "head_row": np.repeat(-8 * np.eye(16, dtype=np.float32)[:, :, None], P, 2),
    }
    arrays = {k: np.ascontiguousarray(x) for k, x in arrays.items()}
    nc = _bacc.Bacc("TRN2", target_bir_lowering=False, num_devices=1)
    A = {k: nc.dram_tensor("in_" + k, x.shape, _mybir.dt.from_np(x.dtype), kind="ExternalInput").ap()
         for k, x in arrays.items()}
    A["narep"] = nc.dram_tensor("narep", (64, arrays["rpb"].shape[1]), F32, kind="Internal").ap()
    A["nabias"] = nc.dram_tensor("nabias", (8, S, S), F32, kind="Internal").ap()
    A["out"] = nc.dram_tensor("out_0", (S, D), F32, kind="ExternalOutput").ap()
    two_blocks_kernel(nc, A)
    r = _run(nc, [{"in_" + k: x for k, x in arrays.items()}], core_ids=[0])
    return r.results[0]["out_0"].reshape(1, S, D)
```
